# Optimizing a Trainium2 kernel written in Bass

```python
import jax, jax.numpy as jnp
from jax import lax
import numpy as np

D_MODEL = 1024
BATCH = 1
SEQ = 256
DEPTH = 2

GRID_W = 64
CTX_LEN = 256
N_HEADS = 16
N_KV_HEADS = 4
HEAD_DIM = 64
GROUP = N_HEADS // N_KV_HEADS
ROPE_THETA = 10000.0
ROPE_PAIRS_PER_AXIS = HEAD_DIM // 4
Q_BLOCK = 128
D_CONV = D_MODEL
CONV_K = 31
CONV_PAD = (CONV_K - 1) // 2
D_FF = 2816
N_EXPERTS = 8
TOP_K = 2
D_EXPERT = 3584
MOE_BLOCK = 128
N_BRANCHES = 2
N_MOD = 6
EPS = 1e-6

Q_W = N_HEADS * HEAD_DIM
KV_W = N_KV_HEADS * HEAD_DIM
OFF_K = Q_W
OFF_V = OFF_K + KV_W
OFF_CONV = OFF_V + KV_W
OFF_GATE = OFF_CONV + 2 * D_CONV
IN_W = OFF_GATE + N_BRANCHES * D_MODEL
N_DENSE = (DEPTH + 1) // 2
N_MOE = DEPTH // 2

kernel_name = "hybrid_gqa_conformer_moe_dit"

def rmsnorm(x, g):
    xf = x.astype(jnp.float32)
    y = xf * lax.rsqrt(jnp.mean(xf * xf, axis=-1, keepdims=True) + EPS)
    return (y * g.astype(jnp.float32)).astype(x.dtype)

def layernorm(x, g, b):
    xf = x.astype(jnp.float32)
    mu = jnp.mean(xf, axis=-1, keepdims=True)
    var = jnp.mean(jnp.square(xf - mu), axis=-1, keepdims=True)
    y = (xf - mu) * lax.rsqrt(var + EPS)
    return (y * g.astype(jnp.float32) + b.astype(jnp.float32)).astype(x.dtype)

def modulate(h, shift, scale):
    return h * (1.0 + scale) + shift

def axial_rope(seq_len):
    rows = seq_len // GRID_W
    row = jnp.repeat(jnp.arange(rows, dtype=jnp.float32), GRID_W)
    col = jnp.tile(jnp.arange(GRID_W, dtype=jnp.float32), rows)
    freqs = ROPE_THETA ** (-jnp.arange(ROPE_PAIRS_PER_AXIS, dtype=jnp.float32) / ROPE_PAIRS_PER_AXIS)
    ang = jnp.concatenate([row[:, None] * freqs, col[:, None] * freqs], axis=-1)
    return jnp.cos(ang)[:, None, :], jnp.sin(ang)[:, None, :]

def apply_rope(x, cos, sin):
    xf = x.astype(jnp.float32)
    half = HEAD_DIM // 2
    x1, x2 = xf[..., :half], xf[..., half:]
    return jnp.concatenate([x1 * cos - x2 * sin, x1 * sin + x2 * cos], axis=-1).astype(x.dtype)

def gqa_block(q, k, v):
    s = jnp.einsum('bqkgd,blkd->bkgql', q, k, preferred_element_type=jnp.float32) * (HEAD_DIM ** -0.5)
    p = jax.nn.softmax(s, axis=-1).astype(v.dtype)
    return jnp.einsum('bkgql,blkd->bqkgd', p, v)

def latent_attention(q, k, v):
    b, s = q.shape[:2]
    nb = s // Q_BLOCK
    qb = q.reshape(b, nb, Q_BLOCK, N_KV_HEADS, GROUP, HEAD_DIM).swapaxes(0, 1)
    o = lax.map(lambda qblk: gqa_block(qblk, k, v), qb)
    return o.swapaxes(0, 1).reshape(b, s, Q_W)

def conformer_conv(u, dw, db, lg, lb, wo):
    a, g = jnp.split(u, 2, axis=-1)
    z = a * jax.nn.sigmoid(g)
    z = lax.conv_general_dilated(z, dw[:, None, :].astype(z.dtype), window_strides=(1,),
                                 padding=[(CONV_PAD, CONV_PAD)],
                                 dimension_numbers=('NWC', 'WIO', 'NWC'),
                                 feature_group_count=D_CONV) + db
    z = jax.nn.silu(layernorm(z, lg, lb))
    return z @ wo

def merge_branches(p, attn_o, conv_o, w_attn_o, w_out):
    ga, gc = jnp.split(jax.nn.sigmoid(p[..., OFF_GATE:]), N_BRANCHES, axis=-1)
    return (ga * (attn_o @ w_attn_o) + gc * conv_o) @ w_out

def swiglu(h, wg, wu, wd):
    return (jax.nn.silu(h @ wg) * (h @ wu)) @ wd

def moe_swiglu(h, w_router, b_router, w_g, w_u, w_d):
    n, d = h.shape
    logits = jnp.einsum('nd,de->ne', h, w_router, preferred_element_type=jnp.float32) + b_router.astype(jnp.float32)
    top_logit, top_idx = lax.top_k(logits, TOP_K)
    gates = jax.nn.softmax(top_logit, axis=-1)
    flat_e = top_idx.reshape(-1)
    flat_tok = jnp.repeat(jnp.arange(n, dtype=jnp.int32), TOP_K)
    flat_gate = gates.reshape(-1)
    order = jnp.argsort(flat_e, stable=True)
    e_sorted = flat_e[order]
    counts = jnp.bincount(flat_e, length=N_EXPERTS)
    starts = jnp.cumsum(counts) - counts
    pcounts = (counts + MOE_BLOCK - 1) // MOE_BLOCK * MOE_BLOCK
    pends = jnp.cumsum(pcounts)
    pstarts = pends - pcounts
    dest = pstarts[e_sorted] + jnp.arange(n * TOP_K, dtype=jnp.int32) - starts[e_sorted]
    n_blocks = -(-(n * TOP_K) // MOE_BLOCK) + N_EXPERTS
    total = n_blocks * MOE_BLOCK
    tok_buf = jnp.zeros((total,), jnp.int32).at[dest].set(flat_tok[order])
    gate_buf = jnp.zeros((total,), h.dtype).at[dest].set(flat_gate[order].astype(h.dtype))
    block_start = jnp.arange(n_blocks, dtype=jnp.int32) * MOE_BLOCK
    block_e = jnp.minimum(jnp.sum(block_start[:, None] >= pends[None, :], axis=1), N_EXPERTS - 1)

    def run_block(args):
        tok, e = args
        xb = h[tok]
        return (jax.nn.silu(xb @ w_g[e]) * (xb @ w_u[e])) @ w_d[e]

    out = lax.map(run_block, (tok_buf.reshape(n_blocks, MOE_BLOCK), block_e))
    out = out.reshape(total, d) * gate_buf[:, None]
    return jnp.zeros_like(h).at[tok_buf].add(out)

def setup_inputs(seed: int = 0) -> dict:
    key = jax.random.key(seed)
    ks = iter(jax.random.split(key, 40))

    def nrm(shape, scale):
        return jax.random.normal(next(ks), shape, jnp.float32) * scale

    def gain(shape):
        return 1.0 + nrm(shape, 0.02)

    D = D_MODEL
    return {
        "x": nrm((BATCH, SEQ, D), 1.0),
        "c": nrm((BATCH, D), 1.0),
        "ctx": nrm((BATCH, CTX_LEN, D), 1.0),
        "c_ctx": nrm((D,), 1.0),
        "w_ada": nrm((DEPTH, D, N_MOD * D), D ** -0.5),
        "b_ada": nrm((DEPTH, N_MOD * D), 0.02),
        "g_mix": gain((DEPTH, D)),
        "g_ffn": gain((DEPTH, D)),
        "w_in": nrm((DEPTH, D, IN_W), D ** -0.5),
        "q_norm": gain((DEPTH, HEAD_DIM)),
        "k_norm": gain((DEPTH, HEAD_DIM)),
        "w_attn_o": nrm((DEPTH, Q_W, D), Q_W ** -0.5),
        "conv_dw": nrm((DEPTH, CONV_K, D_CONV), CONV_K ** -0.5),
        "conv_b": nrm((DEPTH, D_CONV), 0.02),
        "conv_ln_g": gain((DEPTH, D_CONV)),
        "conv_ln_b": nrm((DEPTH, D_CONV), 0.02),
        "w_conv_o": nrm((DEPTH, D_CONV, D), D_CONV ** -0.5),
        "w_out": nrm((DEPTH, D, D), D ** -0.5),
        "w_ff_gate": nrm((N_DENSE, D, D_FF), D ** -0.5),
        "w_ff_up": nrm((N_DENSE, D, D_FF), D ** -0.5),
        "w_ff_down": nrm((N_DENSE, D_FF, D), D_FF ** -0.5),
        "w_router": nrm((N_MOE, D, N_EXPERTS), D ** -0.5),
        "b_router": nrm((N_MOE, N_EXPERTS), 0.01),
        "w_moe_gate": nrm((N_MOE, N_EXPERTS, D, D_EXPERT), D ** -0.5),
        "w_moe_up": nrm((N_MOE, N_EXPERTS, D, D_EXPERT), D ** -0.5),
        "w_moe_down": nrm((N_MOE, N_EXPERTS, D_EXPERT, D), D_EXPERT ** -0.5),
        "g_final": gain((D,)),
    }

def reference(x, c, ctx, c_ctx, w_ada, b_ada, g_mix, g_ffn, w_in, q_norm, k_norm, w_attn_o,
              conv_dw, conv_b, conv_ln_g, conv_ln_b, w_conv_o, w_out, w_ff_gate, w_ff_up,
              w_ff_down, w_router, b_router, w_moe_gate, w_moe_up, w_moe_down, g_final):
    b, s, d = x.shape
    cos, sin = axial_rope(s)
    xc = ctx
    for l in range(DEPTH):
        last = l == DEPTH - 1
        mod_x = (jax.nn.silu(c) @ w_ada[l] + b_ada[l])[:, None, :]
        mod_c = jax.nn.silu(c_ctx) @ w_ada[l] + b_ada[l]
        sh1, sc1, gt1, sh2, sc2, gt2 = jnp.split(mod_x, N_MOD, axis=-1)
        csh1, csc1, cgt1, csh2, csc2, cgt2 = jnp.split(mod_c, N_MOD, axis=-1)

        hx = modulate(rmsnorm(x, g_mix[l]), sh1, sc1)
        hc = modulate(rmsnorm(xc, g_mix[l]), csh1, csc1)
        w_l = w_in[l]
        px = hx @ w_l
        pc = hc @ (w_l[:, OFF_K:OFF_CONV] if last else w_l)
        off = OFF_K if last else 0

        qx = apply_rope(rmsnorm(px[..., :OFF_K].reshape(b, s, N_HEADS, HEAD_DIM), q_norm[l]), cos, sin)
        kx = apply_rope(rmsnorm(px[..., OFF_K:OFF_V].reshape(b, s, N_KV_HEADS, HEAD_DIM), k_norm[l]), cos, sin)
        vx = px[..., OFF_V:OFF_CONV].reshape(b, s, N_KV_HEADS, HEAD_DIM)
        kc = rmsnorm(pc[..., OFF_K - off:OFF_V - off].reshape(b, -1, N_KV_HEADS, HEAD_DIM), k_norm[l])
        vc = pc[..., OFF_V - off:OFF_CONV - off].reshape(b, -1, N_KV_HEADS, HEAD_DIM)

        k_all = jnp.concatenate([kx, kc], axis=1)
        v_all = jnp.concatenate([vx, vc], axis=1)
        attn_x = latent_attention(qx, k_all, v_all)
        conv_x = conformer_conv(px[..., OFF_CONV:OFF_GATE], conv_dw[l], conv_b[l],
                                conv_ln_g[l], conv_ln_b[l], w_conv_o[l])
        x = x + gt1 * merge_branches(px, attn_x, conv_x, w_attn_o[l], w_out[l])

        if not last:
            qc = rmsnorm(pc[..., :OFF_K].reshape(b, -1, N_HEADS, HEAD_DIM), q_norm[l])
            qc = qc.reshape(b, -1, N_KV_HEADS, GROUP, HEAD_DIM)
            attn_c = gqa_block(qc, kc, vc).reshape(b, -1, Q_W)
            conv_c = conformer_conv(pc[..., OFF_CONV:OFF_GATE], conv_dw[l], conv_b[l],
                                    conv_ln_g[l], conv_ln_b[l], w_conv_o[l])
            xc = xc + cgt1 * merge_branches(pc, attn_c, conv_c, w_attn_o[l], w_out[l])

        tokens = modulate(rmsnorm(x, g_ffn[l]), sh2, sc2).reshape(-1, d)
        if not last:
            hc2 = modulate(rmsnorm(xc, g_ffn[l]), csh2, csc2).reshape(-1, d)
            tokens = jnp.concatenate([tokens, hc2], axis=0)
        i = l // 2
        if l % 2 == 0:
            y = swiglu(tokens, w_ff_gate[i], w_ff_up[i], w_ff_down[i])
        else:
            y = moe_swiglu(tokens, w_router[i], b_router[i], w_moe_gate[i], w_moe_up[i], w_moe_down[i])
        n_lat = b * s
        x = x + gt2 * y[:n_lat].reshape(b, s, d)
        if not last:
            xc = xc + cgt2 * y[n_lat:].reshape(b, -1, d)
    return rmsnorm(x, g_final)


_drawn_inputs = setup_inputs


def setup_inputs(seed=0):
    import zlib

    import numpy as np

    out = dict(_drawn_inputs(seed))
    spreads = {}
    factors = {'q_norm': 8.0,
     'k_norm': 8.0,
     'conv_b': 6.684,
     'conv_ln_g': 2.709,
     'conv_ln_b': 3.606,
     'g_final': 7.786,
     'b_router': 3.212}
    for name, (base, spread) in spreads.items():
        noise = np.random.default_rng([zlib.crc32(name.encode()), seed]).standard_normal(out[name].shape)
        drawn = base * np.exp(spread * noise) if base else spread * noise
        out[name] = __import__('jax').numpy.asarray(drawn.astype(out[name].dtype))
    for name, factor in factors.items():
        out[name] = (out[name] * factor).astype(out[name].dtype)
    return out
```

```python
import concourse.bass as bass
from concourse import mybir
from contextlib import ExitStack, contextmanager
import numpy as np

P = 128
D = 1024
SEQ = 256
CTX = 256
TOK = SEQ + CTX
DEPTH = 2
NH, NKV, HD = 16, 4, 64
HALF = HD // 2
GRID_W = 64
ROPE_THETA = 10000.0
TAPS, PAD = 31, 15
DFF = 2816
NE = 8
DE = 3584
NMOD = 6
EPS = 1e-6
KT = D // P
QW, KVW = NH * HD, NKV * HD
OFF_K, OFF_V, OFF_CONV = QW, QW + KVW, QW + 2 * KVW
OFF_GATE = OFF_CONV + 2 * D
FT = DFF // P
CC = 256
CHUNK = KT * CC
HP = NH // 2
ZW = SEQ + 2 * PAD
EC = 512
NC = DE // EC
TAPS_ATT = 12
MOE_RAW = 6
MOE_N = 6 * NC

PHASES = []
for _l in range(DEPTH):
    PHASES += [("ada", _l, NMOD * D // CC), ("q", _l, QW // CC), ("kv", _l, 2), ("ag", _l, 2 * D // CC),
               ("attn_o", _l, D // CC), ("ga", _l, D // CC), ("gc", _l, D // CC), ("conv_o", _l, D // CC),
               ("w_out", _l, D // CC)]
    if _l % 2 == 0:
        PHASES += [("ffn_up", _l, 2 * DFF // CC), ("ffn_down", _l, 2 * KT)]
BASE, COUNT, _n = {}, {}, 0
for _name, _l, _c in PHASES:
    BASE[_name, _l], COUNT[_name, _l] = _n, _c
    _n += _c
DENSE_CHUNKS = _n
LAST_PHASE = PHASES[-1][:2]


class Chain:

    def __init__(self, eng, sem):
        self.eng, self.sem, self.base, self.k = eng, sem, 0, 0

    def step(self, ins):
        self.k += 1
        ins.then_inc(self.sem, 1)

    def wait(self, back=0):
        self.eng.wait_ge(self.sem, self.base + (self.k - back))

    def link(self, ins):
        self.step(ins)
        self.wait()

    @contextmanager
    def loop(self, start, stop, count):
        at = self.base + self.k
        with self.eng.Fori(start, stop) as i:
            self.base, self.k = i * count + (at - start * count), 0
            yield i
            assert self.k == count, (self.k, count)
        self.base, self.k = at + (stop - start) * count, 0


def build(nc, A, out_t):
    f32, f32r, i32 = mybir.dt.float32, mybir.dt.float32r, mybir.dt.int32
    ALU, ACT, AX = mybir.AluOpType, mybir.ActivationFunctionType, mybir.AxisListType
    ds = bass.ds
    with ExitStack() as ctx:
        def sb(name, shape, dt=f32):
            return ctx.enter_context(nc.sbuf_tensor(name, shape, dt))

        def sem(name):
            return ctx.enter_context(nc.semaphore(name))

        x = sb("x", [P, KT, TOK])
        raw = sb("raw", [P, 2, CHUNK])
        w_hi = sb("w_hi", [P, 2, CHUNK], f32r)
        w_lo = sb("w_lo", [P, 2, CHUNK], f32r)
        ident = sb("ident", [P, P])
        mean_w = sb("mean_w", [P, P])
        rope = sb("rope", [P, 2, 2, HALF])
        dw = sb("dw", [P, DEPTH, KT, TAPS])
        vecs = sb("vecs", [P, 5, DEPTH, KT])
        g_final = sb("g_final", [P, KT])
        qk_gain = sb("qk_gain", [P, 2, DEPTH, HD])
        b_ada = sb("b_ada", [P, DEPTH, NMOD * KT])
        cvec = sb("cvec", [P, KT, 2])
        cs = sb("cs", [P, KT, 2])
        cs_split = sb("cs_split", [P, KT, 4], f32r)
        pair_sum = sb("pair_sum", [4, 2])
        ada_row = sb("ada_row", [4, 2, CC])
        mods = sb("mods", [P, NMOD * KT, 2])
        scale1 = sb("scale1", [P, KT, 2])
        eps_t = sb("eps_t", [P, 1])
        rstd = sb("rstd", [P, TOK])
        ss = sb("ss", [P, 4 * NH])
        nbias = sb("nbias", [P, 4])
        rowsum = sb("rowsum", [P, 4])
        rinv = sb("rinv", [P, 2])

        top = -(-nc.sbuf_base // 64) * 64
        end = nc.sbuf_usable_end

        def at(name, offset, shape, dt=f32):
            assert offset + 4 * int(np.prod(shape[1:])) <= end, (name, offset)
            return nc.alloc_sbuf_tensor_at(name, shape, dt, offset=offset)

        KB = 1024
        h_hi = at("h_hi", top, [P, KT, TOK], f32r)
        h_lo = at("h_lo", top + 16 * KB, [P, KT, TOK], f32r)
        r1 = top + 32 * KB
        r2 = r1 + 4 * KT * 2 * ZW
        r3, r4, r5, r6 = (r2 + n * 16 * KB for n in (1, 2, 3, 4))
        normed = at("normed", r1, [P, KT, TOK])
        zpad = at("zpad", r1, [P, KT, 2, ZW])
        conv_sq = at("conv_sq", r1, [P, KT, TOK])
        z_hi = at("z_hi", r1, [P, KT, TOK], f32r)
        conv = at("conv", r2, [P, KT, TOK])
        z_lo = at("z_lo", r2, [P, KT, TOK], f32r)
        q_tm = at("q_tm", r3, [P, 4, QW])
        o_lo = at("o_lo", r3, [P, KT, TOK], f32r)
        m_hi = at("m_hi", r3, [P, KT, TOK], f32r)
        qk_tmp = at("qk_tmp", r4, [P, 4 * QW])
        q_fm = at("q_fm", r4, [P, HP, TOK])
        o_hi = at("o_hi", r4, [P, KT, TOK], f32r)
        gate_c = at("gate_c", r4, [P, KT, TOK])
        kv_tm = at("kv_tm", r5, [P, 4, 2 * KVW])
        k_fm = at("k_fm", r5 + 8 * KB, [P, NKV, TOK])
        merged = at("merged", r5, [P, KT, TOK])
        m_lo = at("m_lo", r5, [P, KT, TOK], f32r)
        sig = at("sig", r6, [P, 2, TOK])
        prob = at("prob", r6 + 4 * KB, [P, 2, TOK])
        prob_t = at("prob_t", r6 + 8 * KB, [P, 2, 4, P])
        k_dup = at("k_dup", r6 + 4 * KB, [P, 4, NKV, 2, HD])
        ff_normed = at("ff_normed", r1, [P, KT, TOK])
        gu_hi = at("gu_hi", r1, [P, FT, TOK], f32r)
        gu_lo = at("gu_lo", r1 + FT * 2 * KB, [P, FT, TOK], f32r)
        ff_silu = at("ff_silu", r1 + FT * 4 * KB, [P, 2, TOK])
        ff_gu = at("ff_gu", r1 + FT * 4 * KB + 4 * KB, [P, 2, TOK])
        e0 = r1 + 16 * KB
        moe_raw = at("moe_raw", e0, [P, MOE_RAW - 2, CHUNK])
        e1 = e0 + 32 * KB
        t_hi = at("t_hi", e1, [P, 2, D], f32r)
        t_lo = at("t_lo", e1 + 8 * KB, [P, 2, D], f32r)
        xe_hi = at("xe_hi", e1 + 16 * KB, [P, KT, P], f32r)
        xe_lo = at("xe_lo", e1 + 20 * KB, [P, KT, P], f32r)
        hu_hi = at("hu_hi", e1 + 24 * KB, [P, 4, P], f32r)
        hu_lo = at("hu_lo", e1 + 26 * KB, [P, 4, P], f32r)
        e_silu = at("e_silu", e1 + 28 * KB, [P, EC])
        e_hid = at("e_hid", e1 + 30 * KB, [P, EC])
        y_rows = at("y_rows", e1 + 32 * KB, [P, D])
        e2 = e1 + 36 * KB
        pick = at("pick", e2, [P, 2, P], f32r)
        pick_g = at("pick_g", e2 + KB, [P, 2, P])
        put = at("put", e2 + 2 * KB, [P, 2, P])
        wr = at("wr", e2 + 3 * KB, [P, KT, NE])
        wr_hi = at("wr_hi", e2 + 3 * KB + 256, [P, KT, NE], f32r)
        wr_lo = at("wr_lo", e2 + 3 * KB + 512, [P, KT, NE], f32r)
        e3 = e2 + 4 * KB
        b_router = at("b_router", e3, [P, NE])
        iota = at("iota", e3 + 64, [P, 2 * P])
        before = at("before", e3 + 64 + KB, [P, P])
        ones = at("ones", e3 + 64 + KB + 512, [P, P])
        e4 = e3 + 64 + 2 * KB
        logit = at("logit", e4, [P, 2, NE])
        rank8 = at("rank8", e4 + 64, [P, NE])
        top1 = at("top1", e4 + 128, [P, 2, NE])
        top2 = at("top2", e4 + 192, [P, 2, NE])
        rest = at("rest", e4 + 256, [P, 2, NE])
        tie = at("tie", e4 + 320, [P, 2, NE])
        two = at("two", e4 + 384, [P, 2, 8])
        mask = at("mask", e4 + 448, [P, 2, NE])
        gate_e = at("gate_e", e4 + 512, [P, 2, NE])
        slot = at("slot", e4 + 640, [P, 2, 16])
        most = at("most", e4 + 768, [P, 1])
        most_i = at("most_i", e4 + 800, [P, 1], i32)
        zeros = at("zeros", e4 + 1024, [P, EC])
        zero_r = at("zero_r", e4 + 1024 + 2 * KB, [P, EC], f32r)

        ps = ctx.enter_context(nc.psum_tensor("ps", [P, 8, 512], f32))

        raw_loaded = [sem(f"raw_loaded{s}") for s in range(MOE_RAW)]
        hi_done = sem("hi_done")
        lo_done = sem("lo_done")
        mm_done = sem("mm_done")
        evac = [sem("evac0"), sem("evac1")]
        c_loaded, consts_loaded, x_loaded, fills = (sem(n) for n in ("c_loaded", "consts_loaded", "x_loaded", "fills"))
        cs_done, cs_hi_done, cs_ready = (sem(n) for n in ("cs_done", "cs_hi_done", "cs_ready"))
        ada_turned, scale_ready = sem("ada_turned"), sem("scale_ready")
        sq_done, ms_done, std_done = (sem(n) for n in ("sq_done", "ms_done", "std_done"))
        unit_done, h_hi_done, h_ready = (sem(n) for n in ("unit_done", "h_hi_done", "h_ready"))
        qk_sq, qk_ss, qk_std, qk_ready = (sem(n) for n in ("qk_sq", "qk_ss", "qk_std", "qk_ready"))
        turn_done, turn_copied = sem("turn_done"), sem("turn_copied")
        score_done, nbias_done, exp_done, prob_done = (sem(n) for n in ("score_done", "nbias_done", "exp_done", "prob_done"))
        pt_done, pt_copied, pv_done = (sem(n) for n in ("pt_done", "pt_copied", "pv_done"))
        o_hi_done, o_lo_done = sem("o_hi_done"), sem("o_lo_done")
        conv_done, mean_done, cent_done, csq_done, var_done = (sem(n) for n in ("conv_done", "mean_done", "cent_done", "csq_done", "var_done"))
        cstd_done, cunit_done, z_hi_done, z_ready = (sem(n) for n in ("cstd_done", "cunit_done", "z_hi_done", "z_ready"))
        sig_used, merged_done, m_hi_done, m_ready = (sem(n) for n in ("sig_used", "merged_done", "m_hi_done", "m_ready"))
        gu_hi_done, gu_ready = sem("gu_hi_done"), sem("gu_ready")
        moe_consts, moe_fills = sem("moe_consts"), sem("moe_fills")
        wr_hi_done, wr_ready, tok_turned, tok_copied, logit_done = (sem(n) for n in ("wr_hi_done", "wr_ready", "tok_turned", "tok_copied", "logit_done"))
        top_ready, top_exp, mask_ready, pos_done, route_ready = (sem(n) for n in ("top_ready", "top_exp", "mask_ready", "pos_done", "route_ready"))
        pick_ready, pick_g_ready, sent, xe_hi_done, xe_lo_done = (sem(n) for n in ("pick_ready", "pick_g_ready", "sent", "xe_hi_done", "xe_lo_done"))
        silu_done, hid_done, hid_turned, hu_hi_done, hu_lo_done = (sem(n) for n in ("silu_done", "hid_done", "hid_turned", "hu_hi_done", "hu_lo_done"))
        y_zeroed, y_copied, put_turned, put_copied, back_done, back_added = (sem(n) for n in ("y_zeroed", "y_copied", "put_turned", "put_copied", "back_done", "back_added"))
        x_final, out_ready, out_done = sem("x_final"), sem("out_ready"), sem("out_done")
        act_own, dve_own = sem("act_own"), sem("dve_own")

        def tokens(l):
            return SEQ if l == DEPTH - 1 else TOK

        def src(name, l, i, s):
            def cols(w, c):
                return w.rearrange("(t p) c -> p t c", p=P)[:, :, ds(c, CC)]
            if name == "ag":
                return cols(A["w_in"][l], i * CC + (OFF_CONV + D if s == 0 else OFF_CONV))
            first = {"q": 0, "kv": OFF_K, "ga": OFF_GATE, "gc": OFF_GATE + D}
            if name in first:
                return cols(A["w_in"][l], i * (2 * CC) + (first[name] + s * CC))
            square = {"ada": "w_ada", "attn_o": "w_attn_o", "conv_o": "w_conv_o", "w_out": "w_out"}
            if name in square:
                return cols(A[square[name]][l], i * (2 * CC) + s * CC)
            if name == "ffn_up":
                return cols(A["w_ff_up" if s else "w_ff_gate"][l // 2], i * CC)
            half = FT // 2
            w = A["w_ff_down"][l // 2].rearrange("(t p) c -> p t c", p=P)
            return w[:, s * half:(s + 1) * half, ds(i * P, P)]

        def as_chunk(name, buf):
            if name == "ffn_down":
                return buf[:, 0:FT // 2 * P].rearrange("p (t c) -> p t c", c=P)
            return buf.rearrange("p (t c) -> p t c", c=CC)

        def moe_slot(slot_):
            return raw[:, slot_, :] if slot_ < 2 else moe_raw[:, slot_ - 2, :]

        def moe_loads(h, slot_, j):
            return (h + (j // MOE_RAW + 1 + (DENSE_CHUNKS // 2 if slot_ < 2 else 0))) * 16

        def turn_groups(l):
            return [("q", t, a) for t in range(tokens(l) // P) for a in range(2)] + [("k", t, 0) for t in range(TOK // P)]

        def turn_base(l):
            return sum(len(turn_groups(m)) for m in range(l))

        def steps(l):
            return 2 * (tokens(l) // P)

        def step_base(l):
            return sum(HP * steps(m) for m in range(l))

        def step(l, u):
            nt = tokens(l) // P
            t = u % nt
            return u // nt, t, (range(4) if t < SEQ // P else range(2, 4))

        block = ctx.enter_context(nc.Block())

        @block.sync
        def _(sp):
            sp.dma_start(cvec[:, :, :], A["c_t"]).then_inc(c_loaded, 16)

            def load(name, l, i, wait=True):
                n = BASE[name, l] + 2 * i
                for s in range(2):
                    if wait:
                        sp.wait_ge(lo_done, n + (s - 1))
                    sp.dma_start(as_chunk(name, raw[:, s, :]), src(name, l, i, s)).then_inc(raw_loaded[s], 16)

            for name, l, chunks in PHASES:
                if BASE[name, l] == 0:
                    load(name, l, 0, wait=False)
                    for dst, nm in ((ident, "ident"), (rope, "rope"), (dw, "dw"), (vecs, "vecs"), (g_final, "g_final"),
                                    (qk_gain, "qk_gain"), (b_ada, "b_ada"), (pair_sum, "pair_sum")):
                        sp.dma_start(dst[:], A[nm]).then_inc(consts_loaded, 16)
                    sp.dma_start(x[:, :, 0:SEQ], A["x_t"].rearrange("(k p) t -> p k t", p=P)).then_inc(x_loaded, 16)
                    sp.dma_start(x[:, :, SEQ:TOK], A["ctx_t"].rearrange("(k p) t -> p k t", p=P)).then_inc(x_loaded, 16)
                with sp.Fori(1 if BASE[name, l] == 0 else 0, chunks // 2) as i:
                    load(name, l, i)

            sp.wait_ge(mm_done, DENSE_CHUNKS)
            for dst, nm in ((wr, "w_router"), (b_router, "b_router"), (iota, "iota"), (before, "before"), (rank8, "rank8")):
                sp.dma_start(dst[:], A[nm]).then_inc(moe_consts, 16)
            w_g, w_u, w_d = (A[n].rearrange("l e (t p) c -> (l e) p t c", p=P) for n in ("w_moe_gate", "w_moe_up", "w_moe_down"))

            def moe_load(e, q, j, slot_, w, row, rows, col, cols):
                sp.wait_ge(lo_done, q * MOE_N + (j + (DENSE_CHUNKS - MOE_RAW + 1)))
                sp.dma_start(moe_slot(slot_).rearrange("p (t c) -> p t c", t=rows),
                             w[ds(e, 1), :, ds(row, rows), ds(col, cols)].rearrange("o p t c -> p (o t) c")).then_inc(raw_loaded[slot_], 16)

            def load_up(e, q, c, j, slot0):
                for a in range(4):
                    moe_load(e, q, j + a, (slot0 + a) % MOE_RAW, w_g if a < 2 else w_u, a % 2 * (KT // 2), KT // 2, c * EC, EC)

            def load_down(e, q, c, j, slot0):
                for a in range(2):
                    moe_load(e, q, j + a, (slot0 + a) % MOE_RAW, w_d, c * 4 + 2 * a, 2, 0, D)

            def experts(rnd):
                with sp.Fori(0, NE) as e:
                    q = e + rnd * NE
                    load_up(e, q, 0, 0, 0)
                    with sp.Fori(1, NC) as c:
                        load_up(e, q, c, c * 6 - 2, 4)
                        load_down(e, q, c - 1, c * 6 + 2, 2)
                    load_down(e, q, NC - 1, MOE_N - 2, 4)

            experts(0)
            sp.wait_ge(route_ready, 1)
            full = sp.value_load(most_i[0:1, 0:1], min_val=0, max_val=SEQ)
            with sp.If(full > P):
                experts(1)
            with sp.Else():
                sp.nop()
            for k in range(KT):
                sp.wait_ge(out_ready, k + 1)
                sp.dma_start(out_t[k * P:(k + 1) * P, :], x[:, k, 0:SEQ]).then_inc(out_done, 16)
            sp.wait_ge(out_done, 16 * KT)

        @block.gpsimd
        def _(pool):
            nc.gpsimd.memset(mean_w[:], 1.0 / D).then_inc(fills, 1)
            nc.gpsimd.memset(eps_t[:], EPS).then_inc(fills, 1)

        @block.scalar
        def _(act):
            own = Chain(act, act_own)

            def split(n, s, pair, first=False):
                act.wait_ge(raw_loaded[s], pair * 16 + 16)
                if not first:
                    act.wait_ge(mm_done, n - 1)
                nc.scalar.activation(w_hi[:, s, :], raw[:, s, :], ACT.Copy).then_inc(hi_done, 1)

            def phase(name, l, evacuate, start=0, stop=None):
                n0, pairs = BASE[name, l], COUNT[name, l] // 2
                stop = pairs if stop is None else stop
                last = (name, l) == LAST_PHASE and stop == pairs

                def body(i, more=True):
                    n = n0 + 2 * i
                    split(n + 1, 1, n0 // 2 + i, first=isinstance(n, int) and n == 0)
                    evacuate(i, n, 0)
                    if more:
                        split(n + 2, 0, n0 // 2 + 1 + i)
                    evacuate(i, n + 1, 1)
                if n0 == 0:
                    body(start)
                    start += 1
                if stop - last > start:
                    with act.Fori(start, stop - last) as i:
                        body(i)
                if last:
                    body(stop - 1, more=False)

            def none(i, n, s):
                pass

            act.wait_ge(c_loaded, 16)
            nc.scalar.activation(cs[:], cvec[:], ACT.Silu).then_inc(cs_done, 1)
            act.wait_ge(cs_done, 1)
            nc.scalar.activation(cs_split[:, :, 0:2], cs[:], ACT.Copy).then_inc(cs_hi_done, 1)
            split(0, 0, 0, first=True)

            def norm(nrm, l, T, shift, buf):
                act.wait_ge(ms_done, nrm + 1)
                nc.scalar.activation(rstd[:, 0:T], ps[:, 5, 0:T], ACT.Sqrt, bias=eps_t[:, 0:1]).then_inc(std_done, 1)
                for k in range(KT):
                    act.wait_ge(unit_done, nrm * KT + k + 1)
                    for g in range(T // SEQ):
                        seg_ = slice(g * SEQ, (g + 1) * SEQ)
                        own.step(nc.scalar.activation(buf[:, k, seg_], buf[:, k, seg_], ACT.Identity,
                                                      bias=mods[:, shift * KT + k, g:g + 1], scale=scale1[:, k, g:g + 1]))
                    own.wait()
                    nc.scalar.activation(h_hi[:, k, 0:T], buf[:, k, 0:T], ACT.Copy).then_inc(h_hi_done, 1)

            def whole(name, l):
                for s in range(2):
                    act.wait_ge(evac[s], (BASE[name, l] + COUNT[name, l]) // 2)

            for l in range(DEPTH):
                T = tokens(l)
                nt = T // P

                def e_ada(i, n, s):
                    act.wait_ge(mm_done, n + 1)
                    a = i * 2 + (s - 1 + l * COUNT["ada", l])
                    if not (l == 0 and isinstance(i, int) and i == 0):
                        act.wait_ge(ada_turned, a)
                    nc.scalar.activation(ada_row[:, s, :], ps[0:4, 2 * s, 0:CC], ACT.Copy).then_inc(evac[s], 1)

                if l == 0:
                    act.wait_ge(x_loaded, 32)
                    act.wait_ge(fills, 2)
                else:
                    whole(*PHASES[[p[:2] for p in PHASES].index(("ada", l)) - 1][:2])
                nc.scalar.activation(normed[:], x[:], ACT.Square).then_inc(sq_done, 1)
                phase("ada", l, e_ada)
                norm(2 * l, l, TOK, 0, normed)

                def e_q(i, n, s):
                    act.wait_ge(mm_done, n + 1)
                    for b in range(nt // 2):
                        ins = nc.scalar.activation(q_tm[:, 2 * b:2 * b + 2, ds(i * (2 * CC) + s * CC, CC)],
                                                   ps[:, 2 * s + b, :].rearrange("p (t c) -> p t c", t=2), ACT.Copy)
                    ins.then_inc(evac[s], 1)

                def e_kv(i, n, s):
                    act.wait_ge(mm_done, n + 1)
                    for b in range(2):
                        ins = nc.scalar.activation(kv_tm[:, 2 * b:2 * b + 2, s * CC:(s + 1) * CC],
                                                   ps[:, 2 * s + b, :].rearrange("p (t c) -> p t c", t=2), ACT.Copy)
                    ins.then_inc(evac[s], 1)

                def e_ag(i, n, s):
                    if s == 0:
                        act.wait_ge(mm_done, n + 1)
                        act.wait_ge(evac[1], i + BASE["ag", l] // 2)
                        nc.scalar.activation(sig[:, :, 0:T], ps[:, 0:2, 0:T], ACT.Sigmoid).then_inc(evac[0], 1)

                phase("q", l, e_q)
                phase("kv", l, e_kv)
                phase("ag", l, e_ag, 0, 1)
                for s in range(2):
                    act.wait_ge(evac[s], BASE["ag", l] // 2)
                nc.scalar.activation(qk_tmp[:, 0:nt * QW], q_tm[:, 0:nt, :].rearrange("p t c -> p (t c)"), ACT.Square).then_inc(qk_sq, 1)
                act.wait_ge(qk_ss, 2 * l + 1)
                nc.scalar.activation(ss[:, 0:nt * NH], ss[:, 0:nt * NH], ACT.Sqrt, scale=1.0 / HD, bias=eps_t[:, 0:1]).then_inc(qk_std, 1)
                phase("ag", l, e_ag, 1, 2)
                act.wait_ge(qk_ready, 3 * l + 1)
                nc.scalar.activation(qk_tmp[:, 0:4 * KVW].rearrange("p (t c) -> p t c", t=4), kv_tm[:, :, 0:KVW], ACT.Square).then_inc(qk_sq, 1)
                act.wait_ge(qk_ss, 2 * l + 2)
                nc.scalar.activation(ss[:, 0:4 * NKV], ss[:, 0:4 * NKV], ACT.Sqrt, scale=1.0 / HD, bias=eps_t[:, 0:1]).then_inc(qk_std, 1)
                phase("ag", l, e_ag, 2, 4)

                for g, (kind, t, a) in enumerate(turn_groups(l)):
                    act.wait_ge(turn_done, turn_base(l) + g + 1)
                    dst = q_fm[:, 4 * a:4 * a + 4, t * P:(t + 1) * P] if kind == "q" else k_fm[:, :, t * P:(t + 1) * P]
                    nc.scalar.activation(dst, ps[:, 6 + g % 2, :].rearrange("p (b c) -> p b c", b=4), ACT.Copy).then_inc(turn_copied, 1)

                U = steps(l)
                with act.Fori(0, HP // 2) as r:
                    g0 = r * (2 * U) + step_base(l)
                    for w in range(2 * U + 1):
                        if w < 2 * U:
                            _, _, keys = step(l, w % U)
                            K = len(keys) * P
                            act.wait_ge(nbias_done, g0 + (w + 1))
                            act.wait_ge(pt_done, g0 + w if w == 0 else g0 + (w - 1))
                            nc.scalar.activation(prob[:, w % 2, 0:K], ps[:, 2 + w % 4, 0:K], ACT.Exp, bias=nbias[:, w % 4:w % 4 + 1],
                                                 accum_out=rowsum[:, w % 4:w % 4 + 1]).then_inc(exp_done, 1)
                        if w >= 1:
                            v = w - 1
                            nb = len(step(l, v % U)[2])
                            act.wait_ge(pt_done, g0 + (v + 1))
                            act.wait_ge(pv_done, g0 + v if v == 0 else g0 + (v - 1))
                            nc.scalar.activation(prob_t[:, v % 2, 0:nb, :], ps[:, 6 + v % 2, 0:nb * P].rearrange("p (b c) -> p b c", b=nb),
                                                 ACT.Copy).then_inc(pt_copied, 1)
                        if w == U + 2:
                            act.wait_ge(pv_done, g0 + U)
                            nc.scalar.activation(o_hi[:, ds(r * 2, 1), 0:T], ps[:, 0:1, 0:T], ACT.Copy).then_inc(o_hi_done, 1)
                    act.wait_ge(pv_done, g0 + 2 * U)
                    nc.scalar.activation(o_hi[:, ds(r * 2 + 1, 1), 0:T], ps[:, 1:2, 0:T], ACT.Copy).then_inc(o_hi_done, 1)

                def e_ga(i, n, s):
                    act.wait_ge(mm_done, n + 1)
                    act.wait_ge(sig_used, i * 2 + (4 * l + s))
                    nc.scalar.activation(sig[:, :, 0:T], ps[:, 2 * s:2 * s + 2, 0:T], ACT.Sigmoid).then_inc(evac[s], 1)

                def e_gc(i, n, s):
                    act.wait_ge(mm_done, n + 1)
                    nc.scalar.activation(gate_c[:, ds(i * 4 + 2 * s, 2), 0:T], ps[:, 2 * s:2 * s + 2, 0:T], ACT.Sigmoid).then_inc(evac[s], 1)

                phase("attn_o", l, none)
                phase("ga", l, e_ga)
                phase("gc", l, e_gc, 0, 1)
                act.wait_ge(cent_done, l + 1)
                nc.scalar.activation(conv_sq[:, :, 0:T], conv[:, :, 0:T], ACT.Square).then_inc(csq_done, 1)
                phase("gc", l, e_gc, 1, 2)
                act.wait_ge(var_done, l + 1)
                nc.scalar.activation(rstd[:, 0:T], ps[:, 7, 0:T], ACT.Sqrt, bias=eps_t[:, 0:1]).then_inc(cstd_done, 1)
                for k in range(KT):
                    act.wait_ge(cunit_done, l * KT + k + 1)
                    own.link(nc.scalar.activation(conv[:, k, 0:T], conv[:, k, 0:T], ACT.Silu,
                                                  bias=vecs[:, 4, l, k:k + 1], scale=vecs[:, 3, l, k:k + 1]))
                    nc.scalar.activation(z_hi[:, k, 0:T], conv[:, k, 0:T], ACT.Copy).then_inc(z_hi_done, 1)
                phase("conv_o", l, none)
                for k in range(KT):
                    act.wait_ge(merged_done, 4 * l + k // 2 + 1)
                    nc.scalar.activation(m_hi[:, k, 0:T], merged[:, k, 0:T], ACT.Copy).then_inc(m_hi_done, 1)
                phase("w_out", l, none)

                whole("w_out", l)
                nc.scalar.activation(ff_normed[:, :, 0:T], x[:, :, 0:T], ACT.Square).then_inc(sq_done, 1)
                norm(2 * l + 1, l, T, 3, ff_normed)

                if l % 2 == 0:
                    def e_up(i, n, s):
                        act.wait_ge(mm_done, n + 1)
                        if s == 0:
                            act.wait_ge(evac[1], i + BASE["ffn_up", l] // 2)
                            nc.scalar.activation(ff_silu[:], ps[:, 0:2, :], ACT.Silu).then_inc(evac[0], 1)
                        else:
                            act.wait_ge(evac[1], i + (BASE["ffn_up", l] // 2 + 1))
                            nc.scalar.activation(gu_hi[:, ds(i * 2, 2), :], ff_gu[:], ACT.Copy).then_inc(gu_hi_done, 1)
                    phase("ffn_up", l, e_up)
                    phase("ffn_down", l, none)

            act.wait_ge(moe_consts, 16 * 5)
            nc.scalar.activation(wr_hi[:], wr[:], ACT.Copy).then_inc(wr_hi_done, 1)
            for g in range(8):
                act.wait_ge(tok_turned, g + 1)
                nc.scalar.activation((t_hi if g < 4 else t_lo)[:, g // 2 % 2, g % 2 * 512:(g % 2 + 1) * 512], ps[:, 6 + g % 2, :],
                                     ACT.Copy).then_inc(tok_copied, 1)
            act.wait_ge(top_ready, 1)
            nc.scalar.activation(two[:, :, 2:3], two[:, :, 4:5], ACT.Exp).then_inc(top_exp, 1)

            def moe_split(n, h, j, slot_):
                act.wait_ge(raw_loaded[slot_], moe_loads(h, slot_, j if isinstance(j, int) else slot_))
                act.wait_ge(mm_done, n + (j - 1))
                nc.scalar.activation(w_hi[:, slot_ % 2, :], moe_slot(slot_), ACT.Copy).then_inc(hi_done, 1)

            def copy_sent(v):
                act.wait_ge(sent, v + 1)
                for a in range(2):
                    nc.scalar.activation(xe_hi[:, 4 * a:4 * a + 4, :], ps[:, 3 + a, :].rearrange("p (b c) -> p b c", b=4), ACT.Copy).then_inc(xe_hi_done, 1)

            def copy_rows(v, n):
                act.wait_ge(mm_done, n)
                act.wait_ge(y_zeroed, v + 1)
                act.wait_ge(back_done, v * 4)
                for a in range(2):
                    nc.scalar.activation(y_rows[:, a * 512:(a + 1) * 512], ps[:, 6 + a, :], ACT.Copy).then_inc(y_copied, 1)

            def silu(h, n):
                act.wait_ge(mm_done, n)
                act.wait_ge(hid_done, h)
                nc.scalar.activation(e_silu[:], ps[:, 0, :], ACT.Silu).then_inc(silu_done, 1)

            def turned(h):
                act.wait_ge(hid_turned, h + 1)
                nc.scalar.activation(hu_hi[:], ps[:, 2, :].rearrange("p (b c) -> p b c", b=4), ACT.Copy).then_inc(hu_hi_done, 1)

            def experts(rnd):
                copy_sent(rnd * (NE + 1))
                with act.Fori(0, NE) as e:
                    q = e + rnd * NE
                    v = e + rnd * (NE + 1)
                    n = q * MOE_N + DENSE_CHUNKS
                    h = q * NC
                    moe_split(n, h, 0, 0)
                    moe_split(n, h, 1, 1)
                    copy_rows(v, n)
                    moe_split(n, h, 2, 2)
                    silu(h, n + 2)
                    moe_split(n, h, 3, 3)
                    with act.Fori(1, NC) as c:
                        nn = n + c * 6 - 2
                        hc = h + c
                        for j, slot_ in ((0, 4), (1, 5)):
                            act.wait_ge(raw_loaded[slot_], hc * 16)
                            act.wait_ge(mm_done, nn + (j - 1))
                            nc.scalar.activation(w_hi[:, slot_ % 2, :], moe_slot(slot_), ACT.Copy).then_inc(hi_done, 1)
                        turned(hc - 1)
                        for j, slot_ in ((2, 0), (3, 1)):
                            act.wait_ge(raw_loaded[slot_], moe_loads(hc, slot_, 0))
                            act.wait_ge(mm_done, nn + (j - 1))
                            nc.scalar.activation(w_hi[:, slot_ % 2, :], moe_slot(slot_), ACT.Copy).then_inc(hi_done, 1)
                        silu(hc, nn + 2)
                        for j, slot_ in ((4, 2), (5, 3)):
                            act.wait_ge(raw_loaded[slot_], moe_loads(hc, slot_, 0))
                            act.wait_ge(mm_done, nn + (j - 1))
                            nc.scalar.activation(w_hi[:, slot_ % 2, :], moe_slot(slot_), ACT.Copy).then_inc(hi_done, 1)
                    moe_split(n, h, MOE_N - 2, 4)
                    moe_split(n, h, MOE_N - 1, 5)
                    turned(h + (NC - 1))
                    copy_sent(v + 1)
                    act.wait_ge(put_turned, q + 1)
                    nc.scalar.activation(put[:], ps[:, 1, 0:2 * P].rearrange("p (t c) -> p t c", t=2), ACT.Copy).then_inc(put_copied, 1)
                copy_rows(rnd * (NE + 1) + NE, (rnd + 1) * NE * MOE_N + DENSE_CHUNKS)

            experts(0)
            act.wait_ge(route_ready, 1)
            full = act.value_load(most_i[0:1, 0:1], min_val=0, max_val=SEQ)
            with act.If(full > P):
                experts(1)
            with act.Else():
                act.nop()

            act.wait_ge(x_final, 1)
            nc.scalar.activation(ff_normed[:, :, 0:SEQ], x[:, :, 0:SEQ], ACT.Square).then_inc(sq_done, 1)
            act.wait_ge(ms_done, 2 * DEPTH + 1)
            nc.scalar.activation(rstd[:, 0:SEQ], ps[:, 5, 0:SEQ], ACT.Sqrt, bias=eps_t[:, 0:1]).then_inc(std_done, 1)

        @block.vector
        def _(dve):
            own = Chain(dve, dve_own)
            V = nc.vector

            def split(n, s):
                dve.wait_ge(hi_done, n + 1)
                V.tensor_tensor(w_lo[:, s, :], raw[:, s, :], w_hi[:, s, :].bitcast(f32), ALU.subtract).then_inc(lo_done, 1)

            def phase(name, l, evacuate, start=0, stop=None, between=None, count=0):
                n0, pairs = BASE[name, l], COUNT[name, l] // 2
                stop = pairs if stop is None else stop
                last = (name, l) == LAST_PHASE and stop == pairs
                by = 2 if name == "ffn_down" else 1

                def body(i, more=True):
                    for b in range(by):
                        n = n0 + 2 * by * i + 2 * b
                        split(n + 1, 1)
                        evacuate(i * by + b, n, 0, b)
                        if between:
                            between(i, 0)
                        if more:
                            split(n + 2, 0)
                        evacuate(i * by + b, n + 1, 1, b)
                        if between:
                            between(i, 1)
                if stop // by - last > start:
                    with own.loop(start, stop // by - last, 2 * count) as i:
                        body(i)
                if last:
                    body(stop - 1, more=False)

            def none(i, n, s, b):
                pass

            dve.wait_ge(cs_hi_done, 1)
            V.tensor_tensor(cs_split[:, :, 2:4], cs[:], cs_split[:, :, 0:2].bitcast(f32), ALU.subtract).then_inc(cs_ready, 1)
            split(0, 0)
            dve.wait_ge(consts_loaded, 8 * 16)

            def norm(nrm, l, T, which, scale, buf):
                own.step(V.scalar_tensor_tensor(out=scale1[:], in0=mods[:, scale * KT:(scale + 1) * KT, :], scalar=1.0,
                                                in1=vecs[:, which, l, :].unsqueeze(2).to_broadcast([P, KT, 2]), op0=ALU.add, op1=ALU.mult))
                dve.wait_ge(std_done, nrm + 1)
                own.link(V.reciprocal(rstd[:, 0:T], rstd[:, 0:T]))
                for k in range(KT):
                    V.tensor_tensor(buf[:, k, 0:T], x[:, k, 0:T], rstd[:, 0:T], ALU.mult).then_inc(unit_done, 1)
                for k in range(KT):
                    dve.wait_ge(h_hi_done, nrm * KT + k + 1)
                    V.tensor_tensor(h_lo[:, k, 0:T], buf[:, k, 0:T], h_hi[:, k, 0:T].bitcast(f32), ALU.subtract).then_inc(h_ready, 1)

            for l in range(DEPTH):
                T = tokens(l)
                nt = T // P
                S = T // SEQ

                phase("ada", l, none)
                dve.wait_ge(ada_turned, (l + 1) * COUNT["ada", l])
                own.link(V.tensor_tensor(mods[:], ps[:, 4, 0:2 * NMOD * KT].rearrange("p (t c) -> p t c", c=2),
                                         b_ada[:, l, :].unsqueeze(2).to_broadcast([P, NMOD * KT, 2]), ALU.add))
                norm(2 * l, l, TOK, 0, 1, normed)
                dve.wait_ge(h_ready, (2 * l + 1) * KT)
                for g in range(S):
                    V.memset(zpad[:, :, g, 0:PAD], 0.0)
                    own.step(V.memset(zpad[:, :, g, PAD + SEQ:ZW], 0.0))
                phase("q", l, none)
                phase("kv", l, none)

                def e_ag(i, n, s, b):
                    if s == 1:
                        dve.wait_ge(mm_done, n + 1)
                        dve.wait_ge(evac[0], i + (BASE["ag", l] // 2 + 1))
                        for a in range(2):
                            ins = V.tensor_tensor(zpad[:, ds(i * 2 + a, 1), 0:S, PAD:PAD + SEQ].rearrange("p o g t -> p (o g) t"),
                                                  ps[:, 2 + a, 0:T].rearrange("p (g t) -> p g t", g=S),
                                                  sig[:, a, 0:T].rearrange("p (g t) -> p g t", g=S), ALU.mult)
                        ins.then_inc(evac[1], 1)

                def head_norm(t_all, t_lat, nh, v, gain, more):
                    r = ss[:, 0:t_all * nh]
                    dve.wait_ge(qk_sq, 2 * l + more + 1)
                    V.tensor_reduce(r, qk_tmp[:, 0:t_all * nh * HD].rearrange("p (h d) -> p h d", d=HD), AX.X, ALU.add).then_inc(qk_ss, 1)
                    dve.wait_ge(qk_std, 2 * l + more + 1)
                    own.link(V.reciprocal(r, r))
                    for t in range(t_all):
                        own.step(V.tensor_tensor(v(t), v(t), ss[:, t * nh:(t + 1) * nh].unsqueeze(2).to_broadcast([P, nh, HD]), ALU.mult))
                    for t in range(t_all):
                        own.wait(back=t_all - 1)
                        own.step(V.scalar_tensor_tensor(out=v(t), in0=v(t), scalar=1.0 if more else HD ** -0.5,
                                                        in1=gain.unsqueeze(1).to_broadcast([P, nh, HD]), op0=ALU.mult, op1=ALU.mult))
                    size = t_lat * nh * HALF
                    tmp = [qk_tmp[:, a * size:(a + 1) * size].rearrange("p (t h d) -> p t h d", t=t_lat, h=nh) for a in range(4)]
                    own.wait()
                    for t in range(t_lat):
                        x1, x2 = v(t)[:, :, 0:HALF], v(t)[:, :, HALF:HD]
                        cos_, sin_ = (rope[:, a, t, :].unsqueeze(1).to_broadcast([P, nh, HALF]) for a in range(2))
                        own.step(V.tensor_tensor(tmp[0][:, t], x1, cos_, ALU.mult))
                        own.step(V.tensor_tensor(tmp[1][:, t], x2, sin_, ALU.mult))
                        own.step(V.tensor_tensor(tmp[2][:, t], x1, sin_, ALU.mult))
                        own.step(V.tensor_tensor(tmp[3][:, t], x2, cos_, ALU.mult))
                    own.wait()
                    for t in range(t_lat):
                        V.tensor_tensor(v(t)[:, :, 0:HALF], tmp[0][:, t], tmp[1][:, t], ALU.subtract)
                        ins = V.tensor_tensor(v(t)[:, :, HALF:HD], tmp[2][:, t], tmp[3][:, t], ALU.add)
                    ins.then_inc(qk_ready, 1)

                def q_view(t):
                    return q_tm[:, t, :].rearrange("p (h d) -> p h d", d=HD)

                def k_view(t):
                    return kv_tm[:, t, 0:KVW].rearrange("p (h d) -> p h d", d=HD)

                phase("ag", l, e_ag, 0, 1)
                head_norm(nt, SEQ // P, NH, q_view, qk_gain[:, 0, l, :], 0)
                phase("ag", l, e_ag, 1, 2)
                head_norm(TOK // P, SEQ // P, NKV, k_view, qk_gain[:, 1, l, :], 1)
                dve.wait_ge(qk_ready, 3 * l + 2)
                for t in range(TOK // P):
                    for a in range(2):
                        ins = V.tensor_copy(k_dup[:, t, :, a, :], k_view(t))
                ins.then_inc(qk_ready, 1)
                phase("ag", l, e_ag, 2, 4)

                def taps(k, a, b):
                    for tap in range(a, b):
                        for g in range(S):
                            out = conv[:, ds(k, 1), g * SEQ:(g + 1) * SEQ]
                            z = zpad[:, ds(k, 1), g, tap:tap + SEQ]
                            wt = dw[:, l, ds(k, 1), tap]
                            if tap == 0:
                                own.step(V.tensor_scalar(out, z, wt, vecs[:, 2, l, ds(k, 1)], ALU.mult, ALU.add))
                            else:
                                own.wait(back=0 if S == 1 or (tap == a and g == 0) else 1)
                                own.step(V.scalar_tensor_tensor(out=out, in0=z, scalar=wt, in1=out, op0=ALU.mult, op1=ALU.add))

                U = steps(l)
                dve.wait_ge(evac[1], (BASE["ag", l] + COUNT["ag", l]) // 2)
                with own.loop(0, HP // 2, 2 * U + 2 * TAPS_ATT * S) as r:
                    g0 = r * (2 * U) + step_base(l)

                    def top(w):
                        K = len(step(l, w % U)[2]) * P
                        dve.wait_ge(score_done, g0 + (w + 1))
                        V.tensor_reduce(nbias[:, w % 4:w % 4 + 1], ps[:, 2 + w % 4, 0:K], AX.X, ALU.max, negate=True).then_inc(nbias_done, 1)

                    def lower(a):
                        dve.wait_ge(o_hi_done, r * 2 + (HP * l + a + 1))
                        V.tensor_tensor(o_lo[:, ds(r * 2 + a, 1), 0:T], ps[:, a:a + 1, 0:T], o_hi[:, ds(r * 2 + a, 1), 0:T].bitcast(f32),
                                        ALU.subtract).then_inc(o_lo_done, 1)

                    top(0)
                    done = 0
                    for w in range(2 * U):
                        if w + 1 < 2 * U:
                            top(w + 1)
                        K = len(step(l, w % U)[2]) * P
                        dve.wait_ge(exp_done, g0 + (w + 1))
                        own.link(V.reciprocal(rinv[:, w % 2:w % 2 + 1], rowsum[:, w % 4:w % 4 + 1]))
                        V.tensor_scalar(prob[:, w % 2, 0:K], prob[:, w % 2, 0:K], rinv[:, w % 2:w % 2 + 1], None, ALU.mult).then_inc(prob_done, 1)
                        upto = 2 * TAPS_ATT * (w + 1) // (2 * U)
                        for a in range(done, upto):
                            taps(r * 2 + a // TAPS_ATT, a % TAPS_ATT, a % TAPS_ATT + 1)
                        done = upto
                        if w == U + 3:
                            lower(0)
                    lower(1)

                def e_ao(i, n, s, b):
                    dve.wait_ge(mm_done, n + 1)
                    V.tensor_copy(merged[:, ds(i * 4 + 2 * s, 2), 0:T], ps[:, 2 * s:2 * s + 2, 0:T]).then_inc(evac[s], 1)

                def e_ga(i, n, s, b):
                    dve.wait_ge(evac[s], i + (BASE["ga", l] // 2 + 1))
                    m = merged[:, ds(i * 4 + 2 * s, 2), 0:T]
                    V.tensor_tensor(m, m, sig[:, :, 0:T], ALU.mult).then_inc(sig_used, 1)

                def e_co(i, n, s, b):
                    dve.wait_ge(mm_done, n + 1)
                    m = merged[:, ds(i * 4 + 2 * s, 2), 0:T]
                    dve.wait_ge(merged_done, i * 2 + (4 * l + s))
                    V.tensor_tensor(sig[:, :, 0:T], ps[:, 2 * s:2 * s + 2, 0:T], gate_c[:, ds(i * 4 + 2 * s, 2), 0:T], ALU.mult).then_inc(evac[s], 1)
                    dve.wait_ge(evac[s], i + (BASE["conv_o", l] // 2 + 1))
                    V.tensor_tensor(m, m, sig[:, :, 0:T], ALU.add).then_inc(merged_done, 1)

                def add_to_x(which, k, bank):
                    for g in range(S):
                        xs = x[:, ds(k, 1), g * SEQ:(g + 1) * SEQ]
                        ins = V.scalar_tensor_tensor(out=xs, in0=ps[:, bank:bank + 1, g * SEQ:(g + 1) * SEQ],
                                                     scalar=mods[:, ds(k + which * KT, 1), g], in1=xs, op0=ALU.mult, op1=ALU.add)
                    return ins

                def e_out(i, n, s, b):
                    dve.wait_ge(mm_done, n + 1)
                    for a in range(2):
                        ins = add_to_x(2, i * 4 + (2 * s + a), 2 * s + a)
                    ins.then_inc(evac[s], 1)

                phase("attn_o", l, e_ao, between=lambda i, s: taps(i * 2 + s, TAPS_ATT, TAPS), count=(TAPS - TAPS_ATT) * S)
                phase("ga", l, e_ga, between=lambda i, s: taps(i * 2 + (4 + s), TAPS_ATT, TAPS), count=(TAPS - TAPS_ATT) * S)
                own.wait()
                V.memset(rinv[:], 0.0).then_inc(conv_done, 1)
                phase("gc", l, none, 0, 1)
                dve.wait_ge(mean_done, l + 1)
                V.tensor_tensor(conv[:, :, 0:T], conv[:, :, 0:T], ps[:, 6, 0:T].unsqueeze(1).to_broadcast([P, KT, T]), ALU.subtract).then_inc(cent_done, 1)
                phase("gc", l, none, 1, 2)
                dve.wait_ge(cstd_done, l + 1)
                own.link(V.reciprocal(rstd[:, 0:T], rstd[:, 0:T]))
                for k in range(KT):
                    V.tensor_tensor(conv[:, k, 0:T], conv[:, k, 0:T], rstd[:, 0:T], ALU.mult).then_inc(cunit_done, 1)
                for k in range(KT):
                    dve.wait_ge(z_hi_done, l * KT + k + 1)
                    V.tensor_tensor(z_lo[:, k, 0:T], conv[:, k, 0:T], z_hi[:, k, 0:T].bitcast(f32), ALU.subtract).then_inc(z_ready, 1)
                phase("conv_o", l, e_co)
                for k in range(KT):
                    dve.wait_ge(m_hi_done, l * KT + k + 1)
                    V.tensor_tensor(m_lo[:, k, 0:T], merged[:, k, 0:T], m_hi[:, k, 0:T].bitcast(f32), ALU.subtract).then_inc(m_ready, 1)
                phase("w_out", l, e_out)
                norm(2 * l + 1, l, T, 1, 4, ff_normed)

                if l % 2 == 0:
                    def e_up(i, n, s, b):
                        if s == 1:
                            dve.wait_ge(mm_done, n + 1)
                            dve.wait_ge(evac[0], i + (BASE["ffn_up", l] // 2 + 1))
                            dve.wait_ge(gu_hi_done, i)
                            V.tensor_tensor(ff_gu[:], ps[:, 2:4, :], ff_silu[:], ALU.mult).then_inc(evac[1], 1)
                            dve.wait_ge(gu_hi_done, i + 1)
                            V.tensor_tensor(gu_lo[:, ds(i * 2, 2), :], ff_gu[:], gu_hi[:, ds(i * 2, 2), :].bitcast(f32), ALU.subtract).then_inc(gu_ready, 1)

                    def e_down(i, n, s, b):
                        if s == 1:
                            dve.wait_ge(mm_done, n + 1)
                            add_to_x(5, i, 2 * b).then_inc(evac[b], 2)

                    phase("ffn_up", l, e_up)
                    phase("ffn_down", l, e_down)

            V.memset(ones[:], 1.0)
            V.memset(zeros[:], 0.0)
            V.memset(slot[:], -1.0)
            V.memset(put[:], 0.0).then_inc(moe_fills, 1)
            dve.wait_ge(moe_fills, 1)
            V.tensor_copy(zero_r[:], zeros[:]).then_inc(moe_fills, 1)
            dve.wait_ge(wr_hi_done, 1)
            V.tensor_tensor(wr_lo[:], wr[:], wr_hi[:].bitcast(f32), ALU.subtract).then_inc(wr_ready, 1)
            dve.wait_ge(logit_done, 1)
            own.link(V.tensor_tensor(logit[:], ps[:, 5, 0:2 * NE].rearrange("p (t e) -> p t e", t=2),
                                     b_router[:].unsqueeze(1).to_broadcast([P, 2, NE]), ALU.add))

            def col(a):
                return two[:, :, a:a + 1]

            def wide(a):
                return two[:, :, a:a + 1].to_broadcast([P, 2, NE])

            def best(of, value, index, hot):
                own.link(V.tensor_reduce(col(value), of, AX.X, ALU.max))
                own.link(V.tensor_tensor(tie[:], of, wide(value), ALU.is_equal))
                own.link(V.tensor_tensor(tie[:], tie[:], rank8[:].unsqueeze(1).to_broadcast([P, 2, NE]), ALU.mult))
                own.link(V.tensor_reduce(col(index), tie[:], AX.X, ALU.max))
                own.link(V.tensor_tensor(hot, tie[:], wide(index), ALU.is_equal))

            best(logit[:], 0, 1, top1[:])
            own.link(V.scalar_tensor_tensor(out=rest[:], in0=top1[:], scalar=-3.0e38, in1=logit[:], op0=ALU.mult, op1=ALU.add))
            best(rest[:], 3, 1, top2[:])
            V.tensor_tensor(col(4), col(3), col(0), ALU.subtract).then_inc(top_ready, 1)
            V.tensor_tensor(mask[:], top1[:], top2[:], ALU.add).then_inc(mask_ready, 1)
            dve.wait_ge(top_exp, 1)
            own.link(V.tensor_scalar(col(5), col(2), 1.0, None, ALU.add))
            own.link(V.reciprocal(col(5), col(5)))
            own.link(V.tensor_tensor(col(6), col(5), col(2), ALU.mult))
            own.link(V.tensor_tensor(tie[:], top1[:], wide(5), ALU.mult))
            own.link(V.tensor_tensor(rest[:], top2[:], wide(6), ALU.mult))
            own.link(V.tensor_tensor(gate_e[:], tie[:], rest[:], ALU.add))
            dve.wait_ge(pos_done, 1)
            own.link(V.scalar_tensor_tensor(out=tie[:], in0=ps[:, 4, 0:2 * NE].rearrange("p (t e) -> p t e", t=2), scalar=1.0,
                                            in1=mask[:], op0=ALU.add, op1=ALU.mult))
            own.step(V.tensor_scalar(slot[:, :, 0:NE], tie[:], -1.0, None, ALU.add))
            own.link(V.tensor_reduce(most[:], ps[:, 4, 2 * NE:3 * NE], AX.X, ALU.max))
            V.tensor_copy(most_i[:], most[:]).then_inc(route_ready, 1)

            def moe_split(n, jn, slot_):
                dve.wait_ge(hi_done, n + (jn + 1))
                V.tensor_tensor(w_lo[:, slot_ % 2, :], moe_slot(slot_), w_hi[:, slot_ % 2, :].bitcast(f32), ALU.subtract).then_inc(lo_done, 1)

            def build_pick(e, v, rnd):
                dve.wait_ge(sent, v)
                for t in range(2):
                    ins = V.tensor_scalar(pick[:, t, :], iota[:, rnd * P:(rnd + 1) * P], slot[:, t, ds(e, 1)], None, ALU.is_equal)
                ins.then_inc(pick_ready, 1)

            def copy_sent(v):
                dve.wait_ge(sent, v + 1)
                for a, bank in ((0, 5), (1, 0)):
                    V.tensor_copy(xe_lo[:, 4 * a:4 * a + 4, :], ps[:, bank, :].rearrange("p (b c) -> p b c", b=4)).then_inc(xe_lo_done, 1)

            def hidden(h, n):
                dve.wait_ge(mm_done, n)
                dve.wait_ge(silu_done, h + 1)
                dve.wait_ge(hid_turned, h)
                V.tensor_tensor(e_hid[:], ps[:, 1, :], e_silu[:], ALU.mult).then_inc(hid_done, 1)

            def turned(h):
                dve.wait_ge(hu_hi_done, h + 1)
                V.tensor_tensor(hu_lo[:], ps[:, 2, :].rearrange("p (b c) -> p b c", b=4), hu_hi[:].bitcast(f32), ALU.subtract).then_inc(hu_lo_done, 1)

            def add_back(v):
                dve.wait_ge(back_added, v * 4)
                for a in range(4):
                    dve.wait_ge(back_done, v * 4 + (a + 1))
                    for b in range(2):
                        k = 2 * a + b
                        ins = V.scalar_tensor_tensor(out=x[:, k, 0:SEQ], in0=ps[:, 2 + a, b * SEQ:(b + 1) * SEQ],
                                                     scalar=mods[:, 5 * KT + k, 0:1], in1=x[:, k, 0:SEQ], op0=ALU.mult, op1=ALU.add)
                    ins.then_inc(back_added, 1)

            def experts(rnd):
                build_pick(0, rnd * (NE + 1), rnd)
                copy_sent(rnd * (NE + 1))
                with dve.Fori(0, NE) as e:
                    q = e + rnd * NE
                    v = e + rnd * (NE + 1)
                    n = q * MOE_N + DENSE_CHUNKS
                    h = q * NC
                    moe_split(n, 0, 0)
                    moe_split(n, 1, 1)
                    dve.wait_ge(put_turned, q)
                    for t in range(2):
                        ins = V.tensor_scalar(pick_g[:, t, :], iota[:, rnd * P:(rnd + 1) * P], slot[:, t, ds(e, 1)], gate_e[:, t, ds(e, 1)],
                                              ALU.is_equal, ALU.mult)
                    ins.then_inc(pick_g_ready, 1)
                    build_pick(e + 1, v + 1, rnd)
                    moe_split(n, 2, 2)
                    moe_split(n, 3, 3)
                    hidden(h, n + 4)
                    add_back(v)
                    with dve.Fori(1, NC) as c:
                        nn = n + c * 6 - 2
                        hc = h + c
                        moe_split(nn, 0, 4)
                        moe_split(nn, 1, 5)
                        turned(hc - 1)
                        for j in range(2, 6):
                            moe_split(nn, j, j - 2)
                        hidden(hc, nn + 4)
                    moe_split(n, MOE_N - 2, 4)
                    moe_split(n, MOE_N - 1, 5)
                    turned(h + (NC - 1))
                    copy_sent(v + 1)
                add_back(rnd * (NE + 1) + NE)

            experts(0)
            full = dve.value_load(most_i[0:1, 0:1], min_val=0, max_val=SEQ)
            with dve.If(full > P):
                experts(1)
            with dve.Else():
                dve.nop()
            V.memset(most[:], 0.0).then_inc(x_final, 1)

            dve.wait_ge(std_done, 2 * DEPTH + 1)
            own.link(V.reciprocal(rstd[:, 0:SEQ], rstd[:, 0:SEQ]))
            for k in range(KT):
                V.scalar_tensor_tensor(out=x[:, k, 0:SEQ], in0=x[:, k, 0:SEQ], scalar=g_final[:, k:k + 1], in1=rstd[:, 0:SEQ],
                                       op0=ALU.mult, op1=ALU.mult).then_inc(out_ready, 1)

        @block.tensor
        def _(pe):
            mm = nc.tensor.matmul

            def three(out, parts, first, last):
                for a, (lhs, rhs) in enumerate(parts):
                    ins = mm(out, lhs, rhs, start=first and a == 0, stop=last and a == len(parts) - 1)
                return ins

            def start(n, s, pair):
                pe.wait_ge(lo_done, n + 1)
                pe.wait_ge(evac[s], pair)

            def by_feature(xh, xl, T):
                def run(i, n, s, hi, lo):
                    for a in range(2):
                        c = slice(a * P, (a + 1) * P)
                        for k in range(KT):
                            ins = three(ps[:, 2 * s + a, 0:T], [(hi[:, k, c], xh[:, k, 0:T]), (hi[:, k, c], xl[:, k, 0:T]),
                                                                (lo[:, k, c], xh[:, k, 0:T])], k == 0, k == KT - 1)
                    return ins
                return run

            def by_token(tiles):
                def run(i, n, s, hi, lo):
                    for t in range(tiles):
                        r = slice(t * P, (t + 1) * P)
                        out = ps[:, 2 * s + t // 2, t % 2 * CC:(t % 2 + 1) * CC]
                        for k in range(KT):
                            ins = three(out, [(h_hi[:, k, r], hi[:, k, :]), (h_hi[:, k, r], lo[:, k, :]), (h_lo[:, k, r], hi[:, k, :])],
                                        k == 0, k == KT - 1)
                    return ins
                return run

            def phase(name, l, run, start_=0, stop=None, after=None):
                n0, pairs = BASE[name, l], COUNT[name, l] // 2
                stop = pairs if stop is None else stop

                def body(i):
                    n = n0 + 2 * i
                    for s in range(2):
                        start(n + s, s, i + n0 // 2)
                        run(i, n + s, s, as_chunk(name, w_hi[:, s, :]), as_chunk(name, w_lo[:, s, :])).then_inc(mm_done, 1)
                    if after:
                        after(i, n)
                with pe.Fori(start_, stop) as i:
                    body(i)

            def mean(buf, T, bank, done):
                for k in range(KT):
                    ins = mm(ps[:, bank, 0:T], mean_w[:], buf[:, k, 0:T], start=k == 0, stop=k == KT - 1)
                ins.then_inc(done, 1)

            pe.wait_ge(cs_ready, 1)
            pe.wait_ge(consts_loaded, 8 * 16)
            pe.wait_ge(fills, 2)
            for l in range(DEPTH):
                T = tokens(l)
                nt = T // P
                pe.wait_ge(sq_done, 2 * l + 1)
                mean(normed, TOK, 5, ms_done)

                def ada(i, n, s, hi, lo):
                    out = ps[0:4, 2 * s, 0:CC]
                    for k in range(KT):
                        mm(out, cs_split[:, k, :], hi[:, k, :], start=k == 0, stop=k == KT - 1)
                    for k in range(KT):
                        ins = mm(ps[0:2, 2 * s, 0:CC], cs_split[:, k, 0:2], lo[:, k, :], start=False, stop=k == KT - 1, skip_group_check=True)
                    return ins

                def ada_turn(i, n):
                    for s in range(2):
                        pe.wait_ge(evac[s], i + (BASE["ada", l] // 2 + 1))
                        for a in range(2):
                            ins = mm(ps[:, 4, ds(i * 8 + (4 * s + 2 * a), 2)], ada_row[:, s, a * P:(a + 1) * P], pair_sum[:], start=True, stop=True)
                        ins.then_inc(ada_turned, 1)

                phase("ada", l, ada, after=ada_turn)
                pe.wait_ge(h_ready, (2 * l + 1) * KT if l == 0 else 2 * l * KT + KT)
                phase("q", l, by_token(nt))
                phase("kv", l, by_token(TOK // P))
                phase("ag", l, by_feature(h_hi, h_lo, T))

                pe.wait_ge(qk_ready, 3 * l + 3)
                for g, (kind, t, a) in enumerate(turn_groups(l)):
                    tg = turn_base(l) + g
                    if tg >= 2:
                        pe.wait_ge(turn_copied, tg - 1)
                    for b in range(4):
                        if kind == "q":
                            block_ = q_tm[:, t, (4 * a + b) * P:(4 * a + b + 1) * P]
                        else:
                            block_ = k_dup[:, t, b, :, :].rearrange("p a d -> p (a d)")
                        ins = nc.tensor.transpose(ps[:, 6 + g % 2, b * P:(b + 1) * P], block_, ident[:])
                    ins.then_inc(turn_done, 1)
                pe.wait_ge(turn_copied, turn_base(l + 1))
                for s in range(2):
                    pe.wait_ge(evac[s], BASE["attn_o", l] // 2)

                U, G0 = steps(l), step_base(l)
                N = HP * U

                def score(g):
                    hp, u = divmod(g, U)
                    h2, t, keys = step(l, u)
                    if G0 + g >= 4:
                        pe.wait_ge(exp_done, G0 + g - 3)
                    r = slice(h2 * HD, (h2 + 1) * HD)
                    mm(ps[:, 2 + g % 4, 0:len(keys) * P], q_fm[r, hp, t * P:(t + 1) * P],
                       k_fm[r, (2 * hp + h2) * NKV // NH, keys[0] * P:TOK], start=True, stop=True).then_inc(score_done, 1)

                def turn(g):
                    _, _, keys = step(l, g % U)
                    pe.wait_ge(prob_done, G0 + g + 1)
                    if G0 + g >= 2:
                        pe.wait_ge(pt_copied, G0 + g - 1)
                    for b in range(len(keys)):
                        ins = nc.tensor.transpose(ps[:, 6 + g % 2, b * P:(b + 1) * P], prob[:, g % 2, b * P:(b + 1) * P], ident[:])
                    ins.then_inc(pt_done, 1)

                def weigh(g):
                    hp, u = divmod(g, U)
                    h2, t, keys = step(l, u)
                    kv = (2 * hp + h2) * NKV // NH
                    pe.wait_ge(pt_copied, G0 + g + 1)
                    if u == 0 and hp >= 2:
                        pe.wait_ge(o_lo_done, l * HP + hp - 1)
                    for b, kb in enumerate(keys):
                        ins = mm(ps[h2 * HD:(h2 + 1) * HD, hp % 2, t * P:(t + 1) * P], kv_tm[:, kb, KVW + kv * HD:KVW + (kv + 1) * HD],
                                 prob_t[:, g % 2, b, :], start=b == 0, stop=b == len(keys) - 1)
                    ins.then_inc(pv_done, 1)

                score(0)
                score(1)
                for g in range(N):
                    if g + 2 < N:
                        score(g + 2)
                    turn(g)
                    if g % (2 * U):
                        weigh(g - 1)
                    if g % (2 * U) == 2 * U - 1:
                        weigh(g)

                pe.wait_ge(o_lo_done, (l + 1) * HP)
                phase("attn_o", l, by_feature(o_hi, o_lo, T))
                phase("ga", l, by_feature(h_hi, h_lo, T))
                pe.wait_ge(conv_done, l + 1)
                mean(conv, T, 6, mean_done)
                phase("gc", l, by_feature(h_hi, h_lo, T), 0, 1)
                pe.wait_ge(csq_done, l + 1)
                mean(conv_sq, T, 7, var_done)
                phase("gc", l, by_feature(h_hi, h_lo, T), 1, 2)
                pe.wait_ge(z_ready, (l + 1) * KT)
                phase("conv_o", l, by_feature(z_hi, z_lo, T))
                pe.wait_ge(m_ready, (l + 1) * KT)
                phase("w_out", l, by_feature(m_hi, m_lo, T))

                pe.wait_ge(sq_done, 2 * l + 2)
                mean(ff_normed, T, 5, ms_done)
                pe.wait_ge(h_ready, (2 * l + 2) * KT)
                if l % 2 == 0:
                    phase("ffn_up", l, by_feature(h_hi, h_lo, T))
                    pe.wait_ge(gu_ready, COUNT["ffn_up", l] // 2)
                    n0 = BASE["ffn_down", l]
                    with pe.Fori(0, KT // 2) as ii:
                        for b in range(2):
                            pe.wait_ge(evac[b], ii * 2 + n0 // 2)
                            for s in range(2):
                                pe.wait_ge(lo_done, ii * 4 + (n0 + 2 * b + s + 1))
                                hi, lo = as_chunk("ffn_down", w_hi[:, s, :]), as_chunk("ffn_down", w_lo[:, s, :])
                                for k in range(FT // 2):
                                    kk = s * (FT // 2) + k
                                    ins = three(ps[:, 2 * b, 0:T], [(hi[:, k, :], gu_hi[:, kk, :]), (hi[:, k, :], gu_lo[:, kk, :]),
                                                                    (lo[:, k, :], gu_hi[:, kk, :])], kk == 0, kk == FT - 1)
                                ins.then_inc(mm_done, 1)

            for g in range(8):
                if g >= 2:
                    pe.wait_ge(tok_copied, g - 1)
                part, t, half = (h_hi if g < 4 else h_lo), g // 2 % 2, g % 2
                for b in range(4):
                    ins = nc.tensor.transpose(ps[:, 6 + g % 2, b * P:(b + 1) * P], part[:, half * 4 + b, t * P:(t + 1) * P].bitcast(f32), ident[:])
                ins.then_inc(tok_turned, 1)
            pe.wait_ge(wr_ready, 1)
            for t in range(2):
                r = slice(t * P, (t + 1) * P)
                for k in range(KT):
                    ins = three(ps[:, 5, t * NE:(t + 1) * NE], [(h_hi[:, k, r], wr_hi[:, k, :]), (h_hi[:, k, r], wr_lo[:, k, :]),
                                                                (h_lo[:, k, r], wr_hi[:, k, :])], k == 0, k == KT - 1)
            ins.then_inc(logit_done, 1)
            pe.wait_ge(mask_ready, 1)
            pos = ps[:, 4, :]
            mm(pos[:, 0:NE], before[:], mask[:, 0, :], start=True, stop=True)
            mm(pos[:, NE:2 * NE], before[:], mask[:, 1, :], start=True, stop=False)
            mm(pos[:, NE:2 * NE], ones[:], mask[:, 0, :], start=False, stop=True)
            mm(pos[:, 2 * NE:3 * NE], ones[:], mask[:, 0, :], start=True, stop=False)
            mm(pos[:, 2 * NE:3 * NE], ones[:], mask[:, 1, :], start=False, stop=True).then_inc(pos_done, 1)
            pe.wait_ge(tok_copied, 8)
            pe.wait_ge(route_ready, 1)
            pe.wait_ge(moe_fills, 2)

            def send(v):
                pe.wait_ge(pick_ready, v + 1)
                for part, banks in ((t_hi, (3, 4)), (t_lo, (5, 0))):
                    for k in range(KT):
                        for t in range(2):
                            ins = mm(ps[:, banks[k // 4], k % 4 * P:(k % 4 + 1) * P], part[:, t, k * P:(k + 1) * P], pick[:, t, :],
                                     start=t == 0, stop=t == 1)
                ins.then_inc(sent, 1)

            def zero_y():
                for a in range(2):
                    ins = mm(ps[:, 6 + a, :], zero_r[:, 0:P], zero_r[:], start=True, stop=True)
                ins.then_inc(y_zeroed, 1)

            def up(n, j0):
                for a in range(4):
                    pe.wait_ge(lo_done, n + (a + 1))
                    s = (j0 + a) % 2
                    hi, lo = (w[:, s, :].rearrange("p (t c) -> p t c", c=EC) for w in (w_hi, w_lo))
                    for k in range(4):
                        kk = a % 2 * 4 + k
                        ins = three(ps[:, a // 2, :], [(xe_hi[:, kk, :], hi[:, k, :]), (xe_hi[:, kk, :], lo[:, k, :]),
                                                       (xe_lo[:, kk, :], hi[:, k, :])], kk == 0, kk == KT - 1)
                    ins.then_inc(mm_done, 1)

            def turn_hidden(h):
                pe.wait_ge(hid_done, h + 1)
                for b in range(4):
                    ins = nc.tensor.transpose(ps[:, 2, b * P:(b + 1) * P], e_hid[:, b * P:(b + 1) * P], ident[:])
                ins.then_inc(hid_turned, 1)

            def down(n, h):
                pe.wait_ge(hu_hi_done, h + 1)
                pe.wait_ge(hu_lo_done, h + 1)
                for a in range(2):
                    pe.wait_ge(lo_done, n + (a + 1))
                    hi, lo = (w[:, a, :].rearrange("p (t c) -> p t c", c=D) for w in (w_hi, w_lo))
                    for k in range(2):
                        for half in range(2):
                            c = slice(half * 512, (half + 1) * 512)
                            for lhs, rhs in ((hu_hi, hi), (hu_hi, lo), (hu_lo, hi)):
                                ins = mm(ps[:, 6 + half, :], lhs[:, 2 * a + k, :], rhs[:, k, c], start=False, stop=True, skip_group_check=True)
                    ins.then_inc(mm_done, 1)

            def give_back(v):
                pe.wait_ge(y_copied, v * 2 + 2)
                zero_y()
                for a in range(4):
                    for b in range(2):
                        k = 2 * a + b
                        ins = mm(ps[:, 2 + a, b * SEQ:(b + 1) * SEQ], y_rows[:, k * P:(k + 1) * P], put[:].rearrange("p t c -> p (t c)"),
                                 start=True, stop=True)
                    ins.then_inc(back_done, 1)

            def experts(rnd):
                send(rnd * (NE + 1))
                with pe.Fori(0, NE) as e:
                    q = e + rnd * NE
                    v = e + rnd * (NE + 1)
                    n = q * MOE_N + DENSE_CHUNKS
                    h = q * NC
                    pe.wait_ge(xe_hi_done, v * 2 + 2)
                    pe.wait_ge(xe_lo_done, v * 2 + 2)
                    pe.wait_ge(put_copied, q)
                    up(n, 0)
                    give_back(v)
                    with pe.Fori(1, NC) as c:
                        nn = n + c * 6 - 2
                        hc = h + c
                        pe.wait_ge(back_added, v * 4 + 4)
                        turn_hidden(hc - 1)
                        pe.wait_ge(silu_done, hc)
                        up(nn, 4)
                        down(nn + 4, hc - 1)
                    pe.wait_ge(silu_done, h + NC)
                    send(v + 1)
                    turn_hidden(h + (NC - 1))
                    pe.wait_ge(pick_g_ready, q + 1)
                    for t in range(2):
                        ins = nc.tensor.transpose(ps[:, 1, t * P:(t + 1) * P], pick_g[:, t, :], ident[:])
                    ins.then_inc(put_turned, 1)
                    down(n + (MOE_N - 2), h + (NC - 1))
                v = rnd * (NE + 1) + NE
                pe.wait_ge(put_copied, (rnd + 1) * NE)
                pe.wait_ge(xe_hi_done, v * 2 + 2)
                pe.wait_ge(xe_lo_done, v * 2 + 2)
                give_back(v)
                pe.wait_ge(back_added, v * 4 + 4)

            zero_y()
            experts(0)
            full = pe.value_load(most_i[0:1, 0:1], min_val=0, max_val=SEQ)
            with pe.If(full > P):
                experts(1)
            with pe.Else():
                pe.nop()
            pe.wait_ge(sq_done, 2 * DEPTH + 1)
            mean(ff_normed, SEQ, 5, ms_done)


def kernel(**inputs):
    import concourse.bacc as bacc
    from concourse.bass_utils import run_bass_kernel_spmd as run

    a = {k: np.asarray(v) for k, v in inputs.items()}

    def c(v):
        return np.ascontiguousarray(v)

    def blocks(v):
        return c(np.moveaxis(v.reshape(*v.shape[:-1], -1, P), -1, 0))

    pos = np.arange(SEQ)
    freqs = np.float32(ROPE_THETA) ** (-np.arange(HD // 4, dtype=np.float32) / (HD // 4))
    ang = np.concatenate([(pos // GRID_W)[:, None].astype(np.float32) * freqs, (pos % GRID_W)[:, None].astype(np.float32) * freqs], -1)
    rope = np.stack([np.cos(ang), np.sin(ang)]).astype(np.float32).reshape(2, SEQ // P, P, HALF).transpose(2, 0, 1, 3)
    arrays = {
        "x_t": c(a["x"][0].T), "ctx_t": c(a["ctx"][0].T),
        "c_t": c(np.stack([a["c"][0], a["c_ctx"]], -1).reshape(KT, P, 2).transpose(1, 0, 2)),
        "ident": np.eye(P, dtype=np.float32), "rope": c(rope),
        "dw": c(a["conv_dw"].transpose(0, 2, 1).reshape(DEPTH, KT, P, TAPS).transpose(2, 0, 1, 3)),
        "vecs": blocks(np.stack([a[n] for n in ("g_mix", "g_ffn", "conv_b", "conv_ln_g", "conv_ln_b")])),
        "g_final": blocks(a["g_final"]),
        "qk_gain": c(np.broadcast_to(np.stack([a["q_norm"], a["k_norm"]])[None], (P, 2, DEPTH, HD))),
        "b_ada": blocks(a["b_ada"]),
        "pair_sum": np.concatenate([np.eye(2, dtype=np.float32)] * 2),
        "w_router": c(a["w_router"][0].reshape(KT, P, NE).transpose(1, 0, 2)),
        "b_router": c(np.broadcast_to(a["b_router"], (P, NE))),
        "iota": c(np.broadcast_to(np.arange(2 * P, dtype=np.float32), (P, 2 * P))),
        "before": np.triu(np.ones((P, P), np.float32), 1),
        "rank8": c(np.broadcast_to(np.arange(NE, 0, -1, dtype=np.float32), (P, NE))),
    }
    for name in ("w_ada", "w_in", "w_attn_o", "w_conv_o", "w_out", "w_ff_gate", "w_ff_up", "w_ff_down", "w_moe_gate", "w_moe_up", "w_moe_down"):
        arrays[name] = c(a[name])
    nc = bacc.Bacc("TRN2", target_bir_lowering=False, num_devices=1)
    A = {k: nc.dram_tensor("in_" + k, v.shape, mybir.dt.from_np(v.dtype), kind="ExternalInput").ap() for k, v in arrays.items()}
    out = nc.dram_tensor("out_t", (D, SEQ), mybir.dt.float32, kind="ExternalOutput").ap()
    build(nc, A, out)
    r = run(nc, [{"in_" + k: v for k, v in arrays.items()}], core_ids=[0])
    return np.ascontiguousarray(r.results[0]["out_t"].T)[None]
```

```python
import concourse.bass as bass
from concourse import mybir
from contextlib import ExitStack, contextmanager
import numpy as np

P = 128
D = 1024
SEQ = 256
CTX = 256
TOK = SEQ + CTX
DEPTH = 2
NH, NKV, HD = 16, 4, 64
HALF = HD // 2
GRID_W = 64
ROPE_THETA = 10000.0
TAPS, PAD = 31, 15
DFF = 2816
NE = 8
DE = 3584
NMOD = 6
EPS = 1e-6
KT = D // P
QW, KVW = NH * HD, NKV * HD
OFF_K, OFF_V, OFF_CONV = QW, QW + KVW, QW + 2 * KVW
OFF_GATE = OFF_CONV + 2 * D
FT = DFF // P
CC = 256
CHUNK = KT * CC
HP = NH // 2
ZW = SEQ + 2 * PAD
EC = 512
NC = DE // EC
TAPS_Q, TAPS_KV, TAPS_ATT = 8, 12, 24
TAPS_AO = (TAPS_KV + TAPS) // 2
TAPS_AO2 = (TAPS_ATT + TAPS) // 2
ADA = NMOD * D // CC
ADA_PHASES = {"ag_a": 0, "q": 2, "kv": 4, "ag_b": 5, "attn_o": 7, "ga": 9, "gc": 11}
ADA_FIRST = ADA - 13
MOE_RAW = 6
MOE_N = 6 * NC
MOE_PARTS = 3
FULL = 2 * SEQ // (P + 1)

PHASES = []
for _l in range(DEPTH):
    PHASES += [("ag_a", _l, D // CC), ("q", _l, QW // CC), ("kv", _l, 2), ("ag_b", _l, D // CC),
               ("attn_o", _l, D // CC), ("ga", _l, D // CC), ("gc", _l, D // CC), ("conv_o", _l, D // CC),
               ("w_out", _l, D // CC)]
    if _l % 2 == 0:
        PHASES += [("ffn_up", _l, 2 * DFF // CC), ("ffn_down", _l, 2 * KT)]
BASE, COUNT, _n = {}, {}, 0
for _name, _l, _c in PHASES:
    BASE[_name, _l], COUNT[_name, _l] = _n, _c
    _n += _c
DENSE_CHUNKS = _n
LAST_PHASE = PHASES[-1][:2]


class Chain:

    def __init__(self, eng, sem):
        self.eng, self.sem, self.base, self.k = eng, sem, 0, 0

    def step(self, ins):
        self.k += 1
        ins.then_inc(self.sem, 1)

    def wait(self, back=0):
        self.eng.wait_ge(self.sem, self.base + (self.k - back))

    def link(self, ins):
        self.step(ins)
        self.wait()

    @contextmanager
    def loop(self, start, stop, count):
        at = self.base + self.k
        with self.eng.Fori(start, stop) as i:
            self.base, self.k = i * count + (at - start * count), 0
            yield i
            assert self.k == count, (self.k, count)
        self.base, self.k = at + (stop - start) * count, 0


def build(nc, A, out_t):
    f32, f32r, i32 = mybir.dt.float32, mybir.dt.float32r, mybir.dt.int32
    ALU, ACT, AX = mybir.AluOpType, mybir.ActivationFunctionType, mybir.AxisListType
    ds = bass.ds
    with ExitStack() as ctx:
        def sb(name, shape, dt=f32):
            return ctx.enter_context(nc.sbuf_tensor(name, shape, dt))

        def sem(name):
            return ctx.enter_context(nc.semaphore(name))

        x = sb("x", [P, KT, TOK])
        raw = sb("raw", [P, 2, CHUNK])
        w_hi = sb("w_hi", [P, 2, CHUNK], f32r)
        w_lo = sb("w_lo", [P, 2, CHUNK], f32r)
        ident = sb("ident", [P, P])
        mean_w = sb("mean_w", [P, 1])
        ones = sb("ones", [P, P])
        rope = sb("rope", [P, 2, 2, HALF])
        dw = sb("dw", [P, DEPTH, KT, TAPS])
        vecs = sb("vecs", [P, 5, DEPTH, KT])
        g_final = sb("g_final", [P, KT])
        qk_gain = sb("qk_gain", [P, 2, DEPTH, HD])
        b_ada = sb("b_ada", [P, DEPTH * NMOD * KT])
        cvec = sb("cvec", [P, KT, 2])
        cs = sb("cs", [P, KT, 2])
        ada_row_0 = sb("ada_row_0", [2, CC])
        mods = sb("mods", [P, DEPTH * NMOD * KT, 2])
        scale1 = sb("scale1", [P, KT, 2])
        eps_t = sb("eps_t", [P, 1])
        col = sb("col", [P, TOK // P])
        diag = sb("diag", [P, TOK // P, P])
        ss = sb("ss", [P, 4 * NH])
        nbias = sb("nbias", [P, 4])
        rowsum = sb("rowsum", [P, 4])
        rinv = sb("rinv", [P, 2])

        top = -(-nc.sbuf_base // 64) * 64
        end = nc.sbuf_usable_end

        def at(name, offset, shape, dt=f32):
            assert offset + 4 * int(np.prod(shape[1:])) <= end, (name, offset)
            return nc.alloc_sbuf_tensor_at(name, shape, dt, offset=offset)

        KB = 1024
        h_hi = at("h_hi", top, [P, KT, TOK], f32r)
        h_lo = at("h_lo", top + 16 * KB, [P, KT, TOK], f32r)
        r1 = top + 32 * KB
        r2 = r1 + 4 * KT * 2 * ZW
        r3, r4, r5, r6 = (r2 + n * 16 * KB for n in (1, 2, 3, 4))
        normed = at("normed", r1, [P, KT, TOK])
        zpad = at("zpad", r1, [P, KT, 2, ZW])
        conv_sq = at("conv_sq", r1, [P, KT, TOK])
        z_hi = at("z_hi", r1, [P, KT, TOK], f32r)
        conv = at("conv", r2, [P, KT, TOK])
        z_lo = at("z_lo", r2, [P, KT, TOK], f32r)
        q_tm = at("q_tm", r3, [P, 4, QW])
        o_lo = at("o_lo", r3, [P, KT, TOK], f32r)
        m_hi = at("m_hi", r3, [P, KT, TOK], f32r)
        qk_tmp = at("qk_tmp", r4, [P, 4 * QW])
        q_fm = at("q_fm", r4, [P, HP, TOK])
        o_hi = at("o_hi", r4, [P, KT, TOK], f32r)
        gate_c = at("gate_c", r4, [P, KT, TOK])
        kv_tm = at("kv_tm", r5, [P, 4, 2 * KVW])
        k_fm = at("k_fm", r5 + 8 * KB, [P, NKV, TOK])
        merged = at("merged", r5, [P, KT, TOK])
        m_lo = at("m_lo", r5, [P, KT, TOK], f32r)
        sig = at("sig", r6, [P, 2, TOK])
        prob = at("prob", r6 + 4 * KB, [P, 2, TOK])
        prob_t = at("prob_t", r6 + 8 * KB, [P, 2, 4, P])
        k_dup = at("k_dup", r6 + 4 * KB, [P, 4, NKV, 2, HD])
        ff_normed = at("ff_normed", r1, [P, KT, TOK])
        gu_hi = at("gu_hi", r1, [P, FT, TOK], f32r)
        gu_lo = at("gu_lo", r1 + FT * 2 * KB, [P, FT, TOK], f32r)
        ff_silu = at("ff_silu", r1 + FT * 4 * KB, [P, 2, TOK])
        ada_raw = at("ada_raw", r1 + 94 * KB, [P, CHUNK])
        ada_row_1 = at("ada_row_1", r4, [2, CC])
        ada_row = (ada_row_0, ada_row_1)
        ada_first = at("ada_first", r3, [P, 2, CHUNK])
        w_hi_3 = at("w_hi_3", top, [P, CHUNK], f32r)
        w_lo_3 = at("w_lo_3", top + 16 * KB, [P, CHUNK], f32r)
        e0 = r1 + 16 * KB
        moe_raw = at("moe_raw", e0, [P, MOE_RAW - 2, CHUNK])
        e1 = e0 + 32 * KB
        t_hi = at("t_hi", e1, [P, 2, D], f32r)
        t_lo = at("t_lo", e1 + 8 * KB, [P, 2, D], f32r)
        xe_hi = at("xe_hi", e1 + 16 * KB, [P, KT, P], f32r)
        xe_lo = at("xe_lo", e1 + 20 * KB, [P, KT, P], f32r)
        hu_hi = at("hu_hi", e1 + 24 * KB, [P, 4, P], f32r)
        hu_lo = at("hu_lo", e1 + 26 * KB, [P, 4, P], f32r)
        e_silu = at("e_silu", e1 + 28 * KB, [P, EC])
        e_hid = at("e_hid", e1 + 30 * KB, [P, EC])
        y_rows = at("y_rows", e1 + 32 * KB, [P, D])
        e2 = e1 + 36 * KB
        pick = at("pick", e2, [P, 2, P], f32r)
        pick_g = at("pick_g", e2 + KB, [P, 2, P])
        put = at("put", e2 + 2 * KB, [P, 2, P])
        wr = at("wr", e2 + 3 * KB, [P, KT, NE])
        wr_hi = at("wr_hi", e2 + 3 * KB + 256, [P, KT, NE], f32r)
        wr_lo = at("wr_lo", e2 + 3 * KB + 512, [P, KT, NE], f32r)
        e3 = e2 + 4 * KB
        b_router = at("b_router", e3, [P, NE])
        iota = at("iota", e3 + 64, [P, 2 * P])
        before = at("before", e3 + 64 + KB, [P, P])
        e4 = e3 + 64 + 2 * KB
        logit = at("logit", e4, [P, 2, NE])
        rank8 = at("rank8", e4 + 64, [P, NE])
        top1 = at("top1", e4 + 128, [P, 2, NE])
        top2 = at("top2", e4 + 192, [P, 2, NE])
        rest = at("rest", e4 + 256, [P, 2, NE])
        tie = at("tie", e4 + 320, [P, 2, NE])
        two = at("two", e4 + 384, [P, 2, 8])
        mask = at("mask", e4 + 448, [P, 2, NE])
        gate_e = at("gate_e", e4 + 512, [P, 2, NE])
        slot = at("slot", e4 + 640, [P, 2, 16])
        over = at("over", e4 + 768, [P, 2, NE])
        full_sel = at("full_sel", e4 + 832, [P, FULL, NE])
        full_e = at("full_e", e4 + 928, [P, 4])
        full_i = at("full_i", e4 + 960, [P, 2, 4], i32)
        zeros = at("zeros", e4 + 1024, [P, EC])
        zero_r = at("zero_r", e4 + 1024 + 2 * KB, [P, EC], f32r)

        ps = ctx.enter_context(nc.psum_tensor("ps", [P, 8, 512], f32))

        raw_loaded = [sem(f"raw_loaded{s}") for s in range(MOE_RAW)]
        hi_done = sem("hi_done")
        lo_done = sem("lo_done")
        mm_done = sem("mm_done")
        evac = [sem("evac0"), sem("evac1")]
        c_loaded, consts_loaded, x_loaded, fills = (sem(n) for n in ("c_loaded", "consts_loaded", "x_loaded", "fills"))
        cs_done = sem("cs_done")
        ada_first_loaded = [sem("ada_first_loaded0"), sem("ada_first_loaded1")]
        ada_loaded, ada_done, ada_copied, ada_turned, mods_done = (sem(n) for n in ("ada_loaded", "ada_done", "ada_copied", "ada_turned", "mods_done"))
        sq_done, sum_done, ms_done, std_done = (sem(n) for n in ("sq_done", "sum_done", "ms_done", "std_done"))
        diag_done, spread_done = sem("diag_done"), sem("spread_done")
        unit_done, h_hi_done, h_ready = (sem(n) for n in ("unit_done", "h_hi_done", "h_ready"))
        qk_sq, qk_ss, qk_std, qk_ready = (sem(n) for n in ("qk_sq", "qk_ss", "qk_std", "qk_ready"))
        turn_done, turn_copied = sem("turn_done"), sem("turn_copied")
        score_done, nbias_done, exp_done, prob_done = (sem(n) for n in ("score_done", "nbias_done", "exp_done", "prob_done"))
        pt_done, pt_copied, pv_done = (sem(n) for n in ("pt_done", "pt_copied", "pv_done"))
        o_hi_done, o_lo_done = sem("o_hi_done"), sem("o_lo_done")
        csum_done, csum_spread, cent_done, csq_done, csq_sum, var_done = (
            sem(n) for n in ("csum_done", "csum_spread", "cent_done", "csq_done", "csq_sum", "var_done"))
        cstd_done, var_diag, var_spread = (sem(n) for n in ("cstd_done", "var_diag", "var_spread"))
        cunit_done, z_hi_done, z_ready = (sem(n) for n in ("cunit_done", "z_hi_done", "z_ready"))
        sig_used, merged_done, m_hi_done, m_ready = (sem(n) for n in ("sig_used", "merged_done", "m_hi_done", "m_ready"))
        gu_hi_done, gu_ready = sem("gu_hi_done"), sem("gu_ready")
        moe_consts, moe_fills = sem("moe_consts"), sem("moe_fills")
        wr_hi_done, wr_ready, tok_turned, tok_copied, logit_done = (sem(n) for n in ("wr_hi_done", "wr_ready", "tok_turned", "tok_copied", "logit_done"))
        top_ready, top_exp, mask_ready, pos_done, route_ready = (sem(n) for n in ("top_ready", "top_exp", "mask_ready", "pos_done", "route_ready"))
        pick_ready, pick_g_ready, sent, xe_hi_done, xe_lo_done = (sem(n) for n in ("pick_ready", "pick_g_ready", "sent", "xe_hi_done", "xe_lo_done"))
        silu_done, hid_done, hid_turned, hu_hi_done, hu_lo_done = (sem(n) for n in ("silu_done", "hid_done", "hid_turned", "hu_hi_done", "hu_lo_done"))
        y_zeroed, y_copied, put_turned, put_copied, back_done, back_added = (sem(n) for n in ("y_zeroed", "y_copied", "put_turned", "put_copied", "back_done", "back_added"))
        x_final, out_ready, out_done = sem("x_final"), sem("out_ready"), sem("out_done")
        act_own, dve_own = sem("act_own"), sem("dve_own")

        def tokens(l):
            return SEQ if l == DEPTH - 1 else TOK

        def src(name, l, i, s):
            def cols(w, c):
                return w.rearrange("(t p) c -> p t c", p=P)[:, :, ds(c, CC)]
            if name in ("ag_a", "ag_b"):
                first = OFF_CONV + (D // 2 if name == "ag_b" else 0)
                return cols(A["w_in"][l], i * CC + (first + D if s == 0 else first))
            first = {"q": 0, "kv": OFF_K, "ga": OFF_GATE, "gc": OFF_GATE + D}
            if name in first:
                return cols(A["w_in"][l], i * (2 * CC) + (first[name] + s * CC))
            square = {"attn_o": "w_attn_o", "conv_o": "w_conv_o", "w_out": "w_out"}
            if name in square:
                return cols(A[square[name]][l], i * (2 * CC) + s * CC)
            if name == "ffn_up":
                return cols(A["w_ff_up" if s else "w_ff_gate"][l // 2], i * CC)
            half = FT // 2
            w = A["w_ff_down"][l // 2].rearrange("(t p) c -> p t c", p=P)
            return w[:, s * half:(s + 1) * half, ds(i * P, P)]

        def as_chunk(name, buf):
            if name == "ffn_down":
                return buf[:, 0:FT // 2 * P].rearrange("p (t c) -> p t c", c=P)
            return buf.rearrange("p (t c) -> p t c", c=CC)

        def ada_number(name, l, i):
            if name in ADA_PHASES:
                return i + (l * ADA + ADA_FIRST + ADA_PHASES[name])
            return i + (l + 1) * ADA if name == "ffn_up" else None

        def moe_slot(slot_):
            return raw[:, slot_, :] if slot_ < 2 else moe_raw[:, slot_ - 2, :]

        def moe_parts(slot_):
            a = slot_ % MOE_PARTS
            return (w_hi[:, a, :], w_lo[:, a, :]) if a < 2 else (w_hi_3[:], w_lo_3[:])

        def moe_loads(h, slot_, j):
            return (h + (j // MOE_RAW + 1 + (DENSE_CHUNKS // 2 if slot_ < 2 else 0))) * 16

        def turn_groups(l):
            return [("q", t, a) for t in range(tokens(l) // P) for a in range(2)] + [("k", t, 0) for t in range(TOK // P)]

        def turn_base(l):
            return sum(len(turn_groups(m)) for m in range(l))

        def steps(l):
            return 2 * (tokens(l) // P)

        def step_base(l):
            return sum(HP * steps(m) for m in range(l))

        def step(l, u):
            nt = tokens(l) // P
            t = u % nt
            return u // nt, t, (range(4) if t < SEQ // P else range(2, 4))

        block = ctx.enter_context(nc.Block())

        @block.sync
        def _(sp):
            sp.dma_start(cvec[:, :, :], A["c_t"]).then_inc(c_loaded, 16)

            def load(name, l, i, wait=True):
                n = BASE[name, l] + 2 * i
                for s in range(2):
                    if wait:
                        sp.wait_ge(lo_done, n + (s - 1))
                    sp.dma_start(as_chunk(name, raw[:, s, :]), src(name, l, i, s)).then_inc(raw_loaded[s], 16)

            def ada_load(l, jl, dst, loaded):
                w = A["w_ada"][l].rearrange("(t p) c -> p t c", p=P)
                sp.dma_start(dst.rearrange("p (t c) -> p t c", c=CC), w[:, :, ds(jl * CC, CC)]).then_inc(loaded, 16)

            def load_beside(name, l, i):
                j = ada_number(name, l, i)
                if j is not None:
                    sp.wait_ge(ada_done, j)
                    if name == "ffn_up":
                        ada_load(l + 1, i, ada_raw[:], ada_loaded)
                    else:
                        ada_load(l, i + (ADA_FIRST + ADA_PHASES[name]), ada_raw[:], ada_loaded)

            for name, l, chunks in PHASES:
                if BASE[name, l] == 0:
                    for j in range(ADA_FIRST):
                        if j >= 2:
                            sp.wait_ge(ada_done, j - 1)
                        ada_load(0, j, ada_first[:, j % 2, :], ada_first_loaded[j % 2])
                        if j == ADA_FIRST - 3:
                            load(name, l, 0, wait=False)
                        if j != 1:
                            continue
                        for dst, nm in ((ident, "ident"), (rope, "rope"), (dw, "dw"), (vecs, "vecs"), (g_final, "g_final"),
                                        (qk_gain, "qk_gain"), (b_ada, "b_ada")):
                            sp.dma_start(dst[:], A[nm]).then_inc(consts_loaded, 16)
                        sp.dma_start(x[:, :, 0:SEQ], A["x_t"].rearrange("(k p) t -> p k t", p=P)).then_inc(x_loaded, 16)
                        sp.dma_start(x[:, :, SEQ:TOK], A["ctx_t"].rearrange("(k p) t -> p k t", p=P)).then_inc(x_loaded, 16)
                    load_beside(name, l, 0)
                with sp.Fori(1 if BASE[name, l] == 0 else 0, chunks // 2) as i:
                    load(name, l, i)
                    load_beside(name, l, i)

            sp.wait_ge(mm_done, DENSE_CHUNKS)
            for dst, nm in ((wr, "w_router"), (b_router, "b_router"), (iota, "iota"), (before, "before"), (rank8, "rank8")):
                sp.dma_start(dst[:], A[nm]).then_inc(moe_consts, 16)
            w_g, w_u, w_d = (A[n].rearrange("l e (t p) c -> (l e) p t c", p=P) for n in ("w_moe_gate", "w_moe_up", "w_moe_down"))

            def moe_load(e, q, j, slot_, w, row, rows, col, cols):
                sp.wait_ge(lo_done, q * MOE_N + (j + (DENSE_CHUNKS - MOE_RAW + 1)))
                sp.dma_start(moe_slot(slot_).rearrange("p (t c) -> p t c", t=rows),
                             w[ds(e, 1), :, ds(row, rows), ds(col, cols)].rearrange("o p t c -> p (o t) c")).then_inc(raw_loaded[slot_], 16)

            def load_up(e, q, c, j, slot0):
                for a in range(4):
                    moe_load(e, q, j + a, (slot0 + a) % MOE_RAW, w_g if a < 2 else w_u, a % 2 * (KT // 2), KT // 2, c * EC, EC)

            def load_down(e, q, c, j, slot0):
                for a in range(2):
                    moe_load(e, q, j + a, (slot0 + a) % MOE_RAW, w_d, c * 4 + 2 * a, 2, 0, D)

            def expert(e, q):
                load_up(e, q, 0, 0, 0)
                with sp.Fori(1, NC) as c:
                    load_up(e, q, c, c * 6 - 2, 4)
                    load_down(e, q, c - 1, c * 6 + 2, 2)
                load_down(e, q, NC - 1, MOE_N - 2, 4)

            with sp.Fori(0, NE) as e:
                expert(e, e)
            sp.wait_ge(route_ready, 1)
            with sp.Fori(0, FULL) as f:
                e = sp.value_load(full_i[0:1, 0, ds(f, 1)], min_val=0, max_val=NE - 1)
                used = sp.value_load(full_i[0:1, 1, ds(f, 1)], min_val=0, max_val=1)
                with sp.If(used > 0):
                    expert(e, f + NE)
                with sp.Else():
                    sp.nop()
            for k in range(KT):
                sp.wait_ge(out_ready, k + 1)
                sp.dma_start(out_t[k * P:(k + 1) * P, :], x[:, k, 0:SEQ]).then_inc(out_done, 16)
            sp.wait_ge(out_done, 16 * KT)

        @block.gpsimd
        def _(pool):
            nc.gpsimd.memset(mean_w[:], 1.0 / D).then_inc(fills, 1)
            nc.gpsimd.memset(eps_t[:], EPS).then_inc(fills, 1)
            nc.gpsimd.memset(ones[:], 1.0).then_inc(fills, 1)

        @block.scalar
        def _(act):
            own = Chain(act, act_own)

            act.nop().then_inc(put_copied, 1)

            def split(n, s, pair, first=False):
                act.wait_ge(raw_loaded[s], pair * 16 + 16)
                if not first:
                    act.wait_ge(mm_done, n - 1)
                nc.scalar.activation(w_hi[:, s, :], raw[:, s, :], ACT.Copy).then_inc(hi_done, 1)

            def phase(name, l, evacuate, start=0, stop=None):
                n0, pairs = BASE[name, l], COUNT[name, l] // 2
                stop = pairs if stop is None else stop
                last = (name, l) == LAST_PHASE and stop == pairs

                def body(i, more=True):
                    n = n0 + 2 * i
                    split(n + 1, 1, n0 // 2 + i, first=isinstance(n, int) and n == 0)
                    evacuate(i, n, 0)
                    if more:
                        split(n + 2, 0, n0 // 2 + 1 + i)
                    j = ada_number(name, l, i)
                    if j is not None:
                        ada_copy(j)
                    evacuate(i, n + 1, 1)
                if n0 == 0:
                    body(start)
                    start += 1
                if stop - last > start:
                    with act.Fori(start, stop - last) as i:
                        body(i)
                if last:
                    body(stop - 1, more=False)

            def none(i, n, s):
                pass

            act.wait_ge(c_loaded, 16)
            nc.scalar.activation(cs[:], cvec[:], ACT.Silu).then_inc(cs_done, 1)

            def ada_copy(j, b=0):
                act.wait_ge(ada_done, j + 1)
                nc.scalar.activation(ada_row[b][:], ps[0:2, 4 + b, 0:CC], ACT.Copy).then_inc(ada_copied, 1)

            def squares(dst, src_, T, done):
                for k in range(KT):
                    nc.scalar.activation(dst[:, k, 0:T], src_[:, k, 0:T], ACT.Square).then_inc(done, 1)

            def norm(nrm, l, T, shift, buf):
                act.wait_ge(ms_done, nrm + 1)
                nc.scalar.activation(col[:, 0:T // P], ps[:, 5, 0:T // P], ACT.Sqrt, bias=eps_t[:, 0:1]).then_inc(std_done, 1)
                for k in range(KT):
                    act.wait_ge(unit_done, nrm * KT + k + 1)
                    for g in range(T // SEQ):
                        seg_ = slice(g * SEQ, (g + 1) * SEQ)
                        own.step(nc.scalar.activation(buf[:, k, seg_], buf[:, k, seg_], ACT.Identity,
                                                      bias=mods[:, (l * NMOD + shift) * KT + k, g:g + 1], scale=scale1[:, k, g:g + 1]))
                    own.wait()
                    nc.scalar.activation(h_hi[:, k, 0:T], buf[:, k, 0:T], ACT.Copy).then_inc(h_hi_done, 1)

            def whole(name, l):
                for s in range(2):
                    act.wait_ge(evac[s], (BASE[name, l] + COUNT[name, l]) // 2)

            for l in range(DEPTH):
                T = tokens(l)
                nt = T // P

                if l == 0:
                    for j in range(ADA_FIRST // 2):
                        ada_copy(j, j % 2)
                    act.wait_ge(x_loaded, 32)
                    act.wait_ge(fills, 3)
                else:
                    whole(*PHASES[[p[:2] for p in PHASES].index(("ag_a", l)) - 1][:2])
                squares(normed, x, TOK, sq_done)
                if l == 0:
                    for j in range(ADA_FIRST // 2, ADA_FIRST):
                        ada_copy(j, j % 2)
                    split(0, 0, 0, first=True)
                norm(2 * l, l, TOK, 0, normed)

                def e_q(i, n, s):
                    act.wait_ge(mm_done, n + 1)
                    for b in range(nt // 2):
                        ins = nc.scalar.activation(q_tm[:, 2 * b:2 * b + 2, ds(i * (2 * CC) + s * CC, CC)],
                                                   ps[:, 2 * s + b, :].rearrange("p (t c) -> p t c", t=2), ACT.Copy)
                    ins.then_inc(evac[s], 1)

                def e_kv(i, n, s):
                    act.wait_ge(mm_done, n + 1)
                    for b in range(2):
                        ins = nc.scalar.activation(kv_tm[:, 2 * b:2 * b + 2, s * CC:(s + 1) * CC],
                                                   ps[:, 2 * s + b, :].rearrange("p (t c) -> p t c", t=2), ACT.Copy)
                    ins.then_inc(evac[s], 1)

                def e_ag(name):
                    def run(i, n, s):
                        if s == 0:
                            act.wait_ge(mm_done, n + 1)
                            act.wait_ge(evac[1], i + BASE[name, l] // 2)
                            nc.scalar.activation(sig[:, :, 0:T], ps[:, 0:2, 0:T], ACT.Sigmoid).then_inc(evac[0], 1)
                    return run

                phase("ag_a", l, e_ag("ag_a"))
                phase("q", l, e_q)
                phase("kv", l, e_kv)
                half = nt // 2
                for g in range(2):
                    if g == 0:
                        for s in range(2):
                            act.wait_ge(evac[s], BASE["ag_b", l] // 2)
                    else:
                        act.wait_ge(qk_ready, 4 * l + 1)
                    nc.scalar.activation(qk_tmp[:, 0:half * QW], q_tm[:, g * half:(g + 1) * half, :].rearrange("p t c -> p (t c)"), ACT.Square).then_inc(qk_sq, 1)
                    act.wait_ge(qk_ss, 3 * l + g + 1)
                    nc.scalar.activation(ss[:, 0:half * NH], ss[:, 0:half * NH], ACT.Sqrt, scale=1.0 / HD, bias=eps_t[:, 0:1]).then_inc(qk_std, 1)
                    phase("ag_b", l, e_ag("ag_b"), g, g + 1)
                act.wait_ge(qk_ready, 4 * l + 2)
                nc.scalar.activation(qk_tmp[:, 0:4 * KVW].rearrange("p (t c) -> p t c", t=4), kv_tm[:, :, 0:KVW], ACT.Square).then_inc(qk_sq, 1)
                act.wait_ge(qk_ss, 3 * l + 3)
                nc.scalar.activation(ss[:, 0:4 * NKV], ss[:, 0:4 * NKV], ACT.Sqrt, scale=1.0 / HD, bias=eps_t[:, 0:1]).then_inc(qk_std, 1)

                for g, (kind, t, a) in enumerate(turn_groups(l)):
                    act.wait_ge(turn_done, turn_base(l) + g + 1)
                    dst = q_fm[:, 4 * a:4 * a + 4, t * P:(t + 1) * P] if kind == "q" else k_fm[:, :, t * P:(t + 1) * P]
                    nc.scalar.activation(dst, ps[:, 6 + g % 2, :].rearrange("p (b c) -> p b c", b=4), ACT.Copy).then_inc(turn_copied, 1)

                U = steps(l)
                with act.Fori(0, HP // 2) as r:
                    g0 = r * (2 * U) + step_base(l)
                    for w in range(2 * U + 1):
                        if w < 2 * U:
                            _, _, keys = step(l, w % U)
                            K = len(keys) * P
                            act.wait_ge(nbias_done, g0 + (w + 1))
                            act.wait_ge(pt_done, (g0 + w if w == 0 else g0 + (w - 1)) + 1)
                            nc.scalar.activation(prob[:, w % 2, 0:K], ps[:, 2 + w % 4, 0:K], ACT.Exp, bias=nbias[:, w % 4:w % 4 + 1],
                                                 accum_out=rowsum[:, w % 4:w % 4 + 1]).then_inc(exp_done, 1)
                        if w >= 1:
                            v = w - 1
                            nb = len(step(l, v % U)[2])
                            act.wait_ge(pt_done, g0 + (v + 1) + 1)
                            act.wait_ge(pv_done, (g0 + v if v == 0 else g0 + (v - 1)) + 1)
                            nc.scalar.activation(prob_t[:, v % 2, 0:nb, :], ps[:, 6 + v % 2, 0:nb * P].rearrange("p (b c) -> p b c", b=nb),
                                                 ACT.Copy).then_inc(pt_copied, 1)
                        if w == U + 2:
                            act.wait_ge(pv_done, g0 + U + 1)
                            nc.scalar.activation(o_hi[:, ds(r * 2, 1), 0:T], ps[:, 0:1, 0:T], ACT.Copy).then_inc(o_hi_done, 1)
                    act.wait_ge(pv_done, g0 + 2 * U + 1)
                    nc.scalar.activation(o_hi[:, ds(r * 2 + 1, 1), 0:T], ps[:, 1:2, 0:T], ACT.Copy).then_inc(o_hi_done, 1)

                def e_ga(i, n, s):
                    act.wait_ge(mm_done, n + 1)
                    act.wait_ge(sig_used, i * 2 + (4 * l + s) + 1)
                    nc.scalar.activation(sig[:, :, 0:T], ps[:, 2 * s:2 * s + 2, 0:T], ACT.Sigmoid).then_inc(evac[s], 1)

                def e_gc(i, n, s):
                    act.wait_ge(mm_done, n + 1)
                    nc.scalar.activation(gate_c[:, ds(i * 4 + 2 * s, 2), 0:T], ps[:, 2 * s:2 * s + 2, 0:T], ACT.Sigmoid).then_inc(evac[s], 1)

                phase("attn_o", l, none)
                phase("ga", l, e_ga)
                phase("gc", l, e_gc, 0, 1)
                for k in range(KT):
                    act.wait_ge(cent_done, l * KT + k + 1)
                    nc.scalar.activation(conv_sq[:, k, 0:T], conv[:, k, 0:T], ACT.Square).then_inc(csq_done, 1)
                phase("gc", l, e_gc, 1, 2)
                act.wait_ge(var_done, l + 1)
                nc.scalar.activation(col[:, 0:nt], ps[:, 7, 0:nt], ACT.Sqrt, bias=eps_t[:, 0:1]).then_inc(cstd_done, 1)
                for k in range(KT):
                    act.wait_ge(cunit_done, l * KT + k + 1)
                    own.link(nc.scalar.activation(conv[:, k, 0:T], conv[:, k, 0:T], ACT.Silu,
                                                  bias=vecs[:, 4, l, k:k + 1], scale=vecs[:, 3, l, k:k + 1]))
                    nc.scalar.activation(z_hi[:, k, 0:T], conv[:, k, 0:T], ACT.Copy).then_inc(z_hi_done, 1)
                def e_co(i, n, s):
                    act.wait_ge(merged_done, i * 2 + (4 * l + s + 1) + 1)
                    nc.scalar.activation(m_hi[:, ds(i * 4 + 2 * s, 2), 0:T], merged[:, ds(i * 4 + 2 * s, 2), 0:T], ACT.Copy).then_inc(m_hi_done, 1)

                phase("conv_o", l, e_co)
                phase("w_out", l, none)

                whole("w_out", l)
                squares(ff_normed, x, T, sq_done)
                norm(2 * l + 1, l, T, 3, ff_normed)

                if l % 2 == 0:
                    def e_up(i, n, s):
                        act.wait_ge(mm_done, n + 1)
                        if s == 0:
                            act.wait_ge(gu_ready, i + 1)
                            nc.scalar.activation(ff_silu[:], ps[:, 0:2, :], ACT.Silu).then_inc(evac[0], 1)
                        else:
                            act.wait_ge(evac[1], i + (BASE["ffn_up", l] // 2 + 1))
                            nc.scalar.activation(gu_hi[:, ds(i * 2, 2), :], ff_silu[:], ACT.Copy).then_inc(gu_hi_done, 1)
                    phase("ffn_up", l, e_up)
                    phase("ffn_down", l, none)

            act.wait_ge(moe_consts, 16 * 5)
            nc.scalar.activation(wr_hi[:], wr[:], ACT.Copy).then_inc(wr_hi_done, 1)
            for g in range(8):
                act.wait_ge(tok_turned, g + 1)
                nc.scalar.activation((t_hi if g < 4 else t_lo)[:, g // 2 % 2, g % 2 * 512:(g % 2 + 1) * 512], ps[:, 6 + g % 2, :],
                                     ACT.Copy).then_inc(tok_copied, 1)
            act.wait_ge(top_ready, 1)
            nc.scalar.activation(two[:, :, 2:3], two[:, :, 4:5], ACT.Exp).then_inc(top_exp, 1)

            def moe_split(n, h, j, slot_):
                act.wait_ge(raw_loaded[slot_], moe_loads(h, slot_, j if isinstance(j, int) else slot_))
                act.wait_ge(mm_done, n + (j - (MOE_PARTS - 1)))
                nc.scalar.activation(moe_parts(slot_)[0], moe_slot(slot_), ACT.Copy).then_inc(hi_done, 1)

            def copy_sent(v):
                act.wait_ge(sent, v + 1)
                for a in range(2):
                    nc.scalar.activation(xe_hi[:, 4 * a:4 * a + 4, :], ps[:, 3 + a, :].rearrange("p (b c) -> p b c", b=4), ACT.Copy).then_inc(xe_hi_done, 1)

            def later_split(nn, hc, j):
                slot_ = (j + 4) % MOE_RAW
                act.wait_ge(raw_loaded[slot_], hc * 16 if j < 2 else moe_loads(hc, slot_, 0))
                act.wait_ge(mm_done, nn + (j - (MOE_PARTS - 1)))
                nc.scalar.activation(moe_parts(slot_)[0], moe_slot(slot_), ACT.Copy).then_inc(hi_done, 1)

            def copy_rows(v, n):
                act.wait_ge(mm_done, n)
                act.wait_ge(y_zeroed, v + 1)
                act.wait_ge(back_done, v * 4 + 1)
                for a in range(2):
                    nc.scalar.activation(y_rows[:, a * 512:(a + 1) * 512], ps[:, 6 + a, :], ACT.Copy).then_inc(y_copied, 1)

            def silu(h, n):
                act.wait_ge(mm_done, n)
                act.wait_ge(hid_done, h + 1)
                nc.scalar.activation(e_silu[:], ps[:, 0, :], ACT.Silu).then_inc(silu_done, 1)

            def turned(h):
                act.wait_ge(hid_turned, h + 1 + 1)
                nc.scalar.activation(hu_hi[:], ps[:, 2, :].rearrange("p (b c) -> p b c", b=4), ACT.Copy).then_inc(hu_hi_done, 1)

            def expert(q, v):
                n = q * MOE_N + DENSE_CHUNKS
                h = q * NC
                for j in range(3):
                    moe_split(n, h, j, j)
                copy_rows(v, n)
                moe_split(n, h, 3, 3)
                silu(h, n + 2)
                with act.Fori(1, NC) as c:
                    nn = n + c * 6 - 2
                    hc = h + c
                    later_split(nn, hc, 0)
                    later_split(nn, hc, 1)
                    turned(hc - 1)
                    later_split(nn, hc, 2)
                    later_split(nn, hc, 3)
                    silu(hc, nn + 2)
                    later_split(nn, hc, 4)
                    later_split(nn, hc, 5)
                moe_split(n, h, MOE_N - 2, 4)
                moe_split(n, h, MOE_N - 1, 5)
                turned(h + (NC - 1))
                copy_sent(v + 1)
                act.wait_ge(put_turned, q + 1 + 1)
                nc.scalar.activation(put[:], ps[:, 1, 0:2 * P].rearrange("p (t c) -> p t c", t=2), ACT.Copy).then_inc(put_copied, 1)

            copy_sent(0)
            with act.Fori(0, NE) as e:
                expert(e, e)
            copy_rows(NE, NE * MOE_N + DENSE_CHUNKS)
            act.wait_ge(route_ready, 1)
            with act.Fori(0, FULL) as f:
                used = act.value_load(full_i[0:1, 1, ds(f, 1)], min_val=0, max_val=1)
                with act.If(used > 0):
                    v = f * 2 + (NE + 1)
                    copy_sent(v)
                    expert(f + NE, v)
                    copy_rows(v + 1, f * MOE_N + ((NE + 1) * MOE_N + DENSE_CHUNKS))
                with act.Else():
                    act.nop()

            act.wait_ge(x_final, 1)
            squares(ff_normed, x, SEQ, sq_done)
            act.wait_ge(ms_done, 2 * DEPTH + 1)
            nc.scalar.activation(col[:, 0:SEQ // P], ps[:, 5, 0:SEQ // P], ACT.Sqrt, bias=eps_t[:, 0:1]).then_inc(std_done, 1)

        @block.vector
        def _(dve):
            own = Chain(dve, dve_own)
            V = nc.vector
            for s_ in (sig_used, merged_done, gu_ready, hid_done, back_added):
                dve.nop().then_inc(s_, 1)

            def split(n, s):
                dve.wait_ge(hi_done, n + 1)
                V.tensor_tensor(w_lo[:, s, :], raw[:, s, :], w_hi[:, s, :].bitcast(f32), ALU.subtract).then_inc(lo_done, 1)

            def phase(name, l, evacuate, start=0, stop=None, between=None, count=0):
                n0, pairs = BASE[name, l], COUNT[name, l] // 2
                stop = pairs if stop is None else stop
                last = (name, l) == LAST_PHASE and stop == pairs
                by = 2 if name == "ffn_down" else 1

                def body(i, more=True):
                    for b in range(by):
                        n = n0 + 2 * by * i + 2 * b
                        split(n + 1, 1)
                        evacuate(i * by + b, n, 0, b)
                        if between:
                            between(i, 0)
                        if more:
                            split(n + 2, 0)
                        evacuate(i * by + b, n + 1, 1, b)
                        j = ada_number(name, l, i)
                        if j is not None:
                            ada_add(j)
                        if between:
                            between(i, 1)
                if stop // by - last > start:
                    with own.loop(start, stop // by - last, count) as i:
                        body(i)
                if last:
                    body(stop - 1, more=False)

            def none(i, n, s, b):
                pass

            dve.wait_ge(consts_loaded, 7 * 16)

            def ada_add(j):
                dve.wait_ge(ada_turned, j + 1)
                V.tensor_tensor(mods[:, ds(j * 2, 2), :], ps[:, 6, 0:4].rearrange("p (t c) -> p t c", c=2),
                                b_ada[:, ds(j * 2, 2)].unsqueeze(2).to_broadcast([P, 2, 2]), ALU.add).then_inc(mods_done, 1)

            acc = diag.rearrange("p t c -> p (t c)")

            def sum_blocks(buf, T, ready, base, done):
                for k in range(1, KT):
                    if ready:
                        dve.wait_ge(ready, base + k + 1)
                    if k > 1:
                        own.wait()
                    own.step(V.tensor_tensor(acc[:, 0:T], buf[:, 0, 0:T] if k == 1 else acc[:, 0:T], buf[:, k, 0:T], ALU.add))
                own.wait()
                V.memset(rinv[:], 0.0).then_inc(done, 1)

            def make_diag(done, value, T):
                dve.wait_ge(done, value)
                own.link(V.reciprocal(col[:, 0:T // P], col[:, 0:T // P]))
                return V.tensor_tensor(diag[:, 0:T // P, :], ident[:].unsqueeze(1).to_broadcast([P, T // P, P]),
                                       col[:, 0:T // P].unsqueeze(2).to_broadcast([P, T // P, P]), ALU.mult)

            def norm(nrm, l, T, which, scale, buf):
                sum_blocks(buf, T, sq_done, nrm * KT, sum_done)
                if nrm == 0:
                    for j in range(ADA_FIRST // 2, ADA_FIRST):
                        ada_add(j)
                    split(0, 0)
                row = (l * NMOD + scale) * KT
                dve.wait_ge(mods_done, l * ADA + (ADA_FIRST if scale == 1 else ADA))
                own.step(V.scalar_tensor_tensor(out=scale1[:], in0=mods[:, row:row + KT, :], scalar=1.0,
                                                in1=vecs[:, which, l, :].unsqueeze(2).to_broadcast([P, KT, 2]), op0=ALU.add, op1=ALU.mult))
                make_diag(std_done, nrm + 1, T).then_inc(diag_done, 1)
                dve.wait_ge(spread_done, nrm + 1)
                for k in range(KT + 2):
                    if k < KT:
                        V.tensor_tensor(buf[:, k, 0:T], x[:, k, 0:T], ps[:, 5, 0:T], ALU.mult).then_inc(unit_done, 1)
                    if k >= 2:
                        b = k - 2
                        dve.wait_ge(h_hi_done, nrm * KT + b + 1)
                        V.tensor_tensor(h_lo[:, b, 0:T], buf[:, b, 0:T], h_hi[:, b, 0:T].bitcast(f32), ALU.subtract).then_inc(h_ready, 1)

            for l in range(DEPTH):
                T = tokens(l)
                nt = T // P
                S = T // SEQ

                if l == 0:
                    for j in range(ADA_FIRST // 2):
                        ada_add(j)
                norm(2 * l, l, TOK, 0, 1, normed)
                dve.wait_ge(h_ready, (2 * l + 1) * KT)
                for g in range(S):
                    V.memset(zpad[:, :, g, 0:PAD], 0.0)
                    own.step(V.memset(zpad[:, :, g, PAD + SEQ:ZW], 0.0))
                def e_ag(name):
                    def run(i, n, s, b):
                        if s == 1:
                            dve.wait_ge(mm_done, n + 1)
                            dve.wait_ge(evac[0], i + (BASE[name, l] // 2 + 1))
                            for a in range(2):
                                k = i * 2 + (a + (KT // 2 if name == "ag_b" else 0))
                                ins = V.tensor_tensor(zpad[:, ds(k, 1), 0:S, PAD:PAD + SEQ].rearrange("p o g t -> p (o g) t"),
                                                      ps[:, 2 + a, 0:T].rearrange("p (g t) -> p g t", g=S),
                                                      sig[:, a, 0:T].rearrange("p (g t) -> p g t", g=S), ALU.mult)
                            ins.then_inc(evac[1], 1)
                    return run

                def head_norm(tiles, nh, v, gain, which):
                    nt_ = len(tiles)
                    r = ss[:, 0:nt_ * nh]
                    dve.wait_ge(qk_sq, 3 * l + which + 1)
                    V.tensor_reduce(r, qk_tmp[:, 0:nt_ * nh * HD].rearrange("p (h d) -> p h d", d=HD), AX.X, ALU.add).then_inc(qk_ss, 1)
                    dve.wait_ge(qk_std, 3 * l + which + 1)
                    own.link(V.reciprocal(r, r))
                    for a, t in enumerate(tiles):
                        own.step(V.tensor_tensor(v(t), v(t), ss[:, a * nh:(a + 1) * nh].unsqueeze(2).to_broadcast([P, nh, HD]), ALU.mult))
                    for t in tiles:
                        own.wait(back=nt_ - 1)
                        ins = V.scalar_tensor_tensor(out=v(t), in0=v(t), scalar=1.0 if which == 2 else HD ** -0.5,
                                                     in1=gain.unsqueeze(1).to_broadcast([P, nh, HD]), op0=ALU.mult, op1=ALU.mult)
                        own.step(ins)
                    own.wait()
                    latent = [t for t in tiles if t < SEQ // P]
                    size = nh * HALF
                    for t in latent:
                        tmp = [qk_tmp[:, (4 * (t - latent[0]) + a) * size:(4 * (t - latent[0]) + a + 1) * size].rearrange("p (h d) -> p h d", h=nh) for a in range(4)]
                        x1, x2 = v(t)[:, :, 0:HALF], v(t)[:, :, HALF:HD]
                        cos_, sin_ = (rope[:, a, t, :].unsqueeze(1).to_broadcast([P, nh, HALF]) for a in range(2))
                        own.step(V.tensor_tensor(tmp[0], x1, cos_, ALU.mult))
                        own.step(V.tensor_tensor(tmp[1], x2, sin_, ALU.mult))
                        own.step(V.tensor_tensor(tmp[2], x1, sin_, ALU.mult))
                        own.step(V.tensor_tensor(tmp[3], x2, cos_, ALU.mult))
                        own.wait()
                        own.step(V.tensor_tensor(x1, tmp[0], tmp[1], ALU.subtract))
                        own.step(V.tensor_tensor(x2, tmp[2], tmp[3], ALU.add))
                    own.wait()
                    V.memset(rinv[:], 0.0).then_inc(qk_ready, 1)

                def q_view(t):
                    return q_tm[:, t, :].rearrange("p (h d) -> p h d", d=HD)

                def k_view(t):
                    return kv_tm[:, t, 0:KVW].rearrange("p (h d) -> p h d", d=HD)

                def taps(k, a, b):
                    for tap in range(a, b):
                        for g in range(S):
                            out = conv[:, ds(k, 1), g * SEQ:(g + 1) * SEQ]
                            z = zpad[:, ds(k, 1), g, tap:tap + SEQ]
                            wt = dw[:, l, ds(k, 1), tap]
                            if tap == 0:
                                own.step(V.tensor_scalar(out, z, wt, vecs[:, 2, l, ds(k, 1)], ALU.mult, ALU.add))
                            else:
                                own.wait(back=0 if S == 1 or (tap == a and g == 0) else 1)
                                own.step(V.scalar_tensor_tensor(out=out, in0=z, scalar=wt, in1=out, op0=ALU.mult, op1=ALU.add))

                def taps_kv(i, s):
                    for k in (2 * s, 2 * s + 1):
                        taps(k, TAPS_Q, TAPS_KV)

                phase("ag_a", l, e_ag("ag_a"))
                dve.wait_ge(evac[1], BASE["q", l] // 2)
                phase("q", l, none, between=lambda i, s: taps(i * 2 + s, 0, TAPS_Q), count=2 * TAPS_Q * S)
                phase("kv", l, none, between=taps_kv, count=4 * (TAPS_KV - TAPS_Q) * S)
                half = nt // 2
                head_norm(range(0, half), NH, q_view, qk_gain[:, 0, l, :], 0)
                phase("ag_b", l, e_ag("ag_b"), 0, 1)
                head_norm(range(half, nt), NH, q_view, qk_gain[:, 0, l, :], 1)
                phase("ag_b", l, e_ag("ag_b"), 1, 2)
                head_norm(range(0, TOK // P), NKV, k_view, qk_gain[:, 1, l, :], 2)
                for t in range(TOK // P):
                    for a in range(2):
                        ins = V.tensor_copy(k_dup[:, t, :, a, :], k_view(t))
                ins.then_inc(qk_ready, 1)

                U = steps(l)
                dve.wait_ge(evac[1], (BASE["ag_b", l] + COUNT["ag_b", l]) // 2)
                with own.loop(0, HP // 2, 2 * U + TAPS_ATT * S) as r:
                    g0 = r * (2 * U) + step_base(l)

                    def top(w):
                        K = len(step(l, w % U)[2]) * P
                        dve.wait_ge(score_done, g0 + (w + 1))
                        V.tensor_reduce(nbias[:, w % 4:w % 4 + 1], ps[:, 2 + w % 4, 0:K], AX.X, ALU.max, negate=True).then_inc(nbias_done, 1)

                    def lower(a):
                        dve.wait_ge(o_hi_done, r * 2 + (HP * l + a + 1))
                        V.tensor_tensor(o_lo[:, ds(r * 2 + a, 1), 0:T], ps[:, a:a + 1, 0:T], o_hi[:, ds(r * 2 + a, 1), 0:T].bitcast(f32),
                                        ALU.subtract).then_inc(o_lo_done, 1)

                    top(0)
                    done = 0
                    for w in range(2 * U):
                        if w + 1 < 2 * U:
                            top(w + 1)
                        K = len(step(l, w % U)[2]) * P
                        dve.wait_ge(exp_done, g0 + (w + 1))
                        own.link(V.reciprocal(rinv[:, w % 2:w % 2 + 1], rowsum[:, w % 4:w % 4 + 1]))
                        V.tensor_scalar(prob[:, w % 2, 0:K], prob[:, w % 2, 0:K], rinv[:, w % 2:w % 2 + 1], None, ALU.mult).then_inc(prob_done, 1)
                        upto = TAPS_ATT * (w + 1) // (2 * U)
                        if upto > done:
                            taps(r + KT // 2, done, upto)
                        done = upto
                        if w == U + 3:
                            lower(0)
                    lower(1)

                def e_ao(i, n, s, b):
                    dve.wait_ge(mm_done, n + 1)
                    V.tensor_copy(merged[:, ds(i * 4 + 2 * s, 2), 0:T], ps[:, 2 * s:2 * s + 2, 0:T]).then_inc(evac[s], 1)

                def e_ga(i, n, s, b):
                    dve.wait_ge(evac[s], i + (BASE["ga", l] // 2 + 1))
                    m = merged[:, ds(i * 4 + 2 * s, 2), 0:T]
                    V.tensor_tensor(m, m, sig[:, :, 0:T], ALU.mult).then_inc(sig_used, 1)

                def e_co(i, n, s, b):
                    dve.wait_ge(mm_done, n + 1)
                    m = merged[:, ds(i * 4 + 2 * s, 2), 0:T]
                    dve.wait_ge(merged_done, i * 2 + (4 * l + s) + 1)
                    V.tensor_tensor(sig[:, :, 0:T], ps[:, 2 * s:2 * s + 2, 0:T], gate_c[:, ds(i * 4 + 2 * s, 2), 0:T], ALU.mult).then_inc(evac[s], 1)
                    dve.wait_ge(evac[s], i + (BASE["conv_o", l] // 2 + 1))
                    V.tensor_tensor(m, m, sig[:, :, 0:T], ALU.add).then_inc(merged_done, 1)
                    dve.wait_ge(m_hi_done, i * 2 + (4 * l + s + 1))
                    V.tensor_tensor(m_lo[:, ds(i * 4 + 2 * s, 2), 0:T], m, m_hi[:, ds(i * 4 + 2 * s, 2), 0:T].bitcast(f32), ALU.subtract).then_inc(m_ready, 1)

                def add_to_x(which, k, bank):
                    for g in range(S):
                        xs = x[:, ds(k, 1), g * SEQ:(g + 1) * SEQ]
                        ins = V.scalar_tensor_tensor(out=xs, in0=ps[:, bank:bank + 1, g * SEQ:(g + 1) * SEQ],
                                                     scalar=mods[:, ds(k + (l * NMOD + which) * KT, 1), g], in1=xs, op0=ALU.mult, op1=ALU.add)
                    return ins

                def e_out(i, n, s, b):
                    dve.wait_ge(mm_done, n + 1)
                    for a in range(2):
                        ins = add_to_x(2, i * 4 + (2 * s + a), 2 * s + a)
                    ins.then_inc(evac[s], 1)

                def taps_ao(i, s):
                    taps(i * 2 + s, TAPS_KV, TAPS_AO)
                    taps(i * 2 + (s + KT // 2), TAPS_ATT, TAPS_AO2)

                def taps_ga(i, s):
                    taps(i * 2 + s, TAPS_AO, TAPS)
                    taps(i * 2 + (s + KT // 2), TAPS_AO2, TAPS)

                phase("attn_o", l, e_ao, between=taps_ao, count=2 * (TAPS_AO - TAPS_KV + TAPS_AO2 - TAPS_ATT) * S)
                phase("ga", l, e_ga, between=taps_ga, count=2 * (TAPS - TAPS_AO + TAPS - TAPS_AO2) * S)
                own.wait()
                sum_blocks(conv, T, None, 0, csum_done)
                phase("gc", l, none, 0, 1)
                dve.wait_ge(csum_spread, l + 1)
                for k in range(KT):
                    V.scalar_tensor_tensor(out=conv[:, k, 0:T], in0=ps[:, 5, 0:T], scalar=-1.0 / D, in1=conv[:, k, 0:T],
                                           op0=ALU.mult, op1=ALU.add).then_inc(cent_done, 1)
                sum_blocks(conv_sq, T, csq_done, l * KT, csq_sum)
                phase("gc", l, none, 1, 2)
                make_diag(cstd_done, l + 1, T).then_inc(var_diag, 1)
                dve.wait_ge(var_spread, l + 1)
                for k in range(KT + 2):
                    if k < KT:
                        V.tensor_tensor(conv[:, k, 0:T], conv[:, k, 0:T], ps[:, 7, 0:T], ALU.mult).then_inc(cunit_done, 1)
                    if k >= 2:
                        b = k - 2
                        dve.wait_ge(z_hi_done, l * KT + b + 1)
                        V.tensor_tensor(z_lo[:, b, 0:T], conv[:, b, 0:T], z_hi[:, b, 0:T].bitcast(f32), ALU.subtract).then_inc(z_ready, 1)
                phase("conv_o", l, e_co)
                phase("w_out", l, e_out)
                norm(2 * l + 1, l, T, 1, 4, ff_normed)

                if l % 2 == 0:
                    def e_up(i, n, s, b):
                        if s == 1:
                            dve.wait_ge(mm_done, n + 1)
                            dve.wait_ge(evac[0], i + (BASE["ffn_up", l] // 2 + 1))
                            V.tensor_tensor(ff_silu[:], ps[:, 2:4, :], ff_silu[:], ALU.mult).then_inc(evac[1], 1)
                            dve.wait_ge(gu_hi_done, i + 1)
                            V.tensor_tensor(gu_lo[:, ds(i * 2, 2), :], ff_silu[:], gu_hi[:, ds(i * 2, 2), :].bitcast(f32), ALU.subtract).then_inc(gu_ready, 1)

                    def e_down(i, n, s, b):
                        if s == 1:
                            dve.wait_ge(mm_done, n + 1)
                            add_to_x(5, i, 2 * b).then_inc(evac[b], 2)

                    phase("ffn_up", l, e_up)
                    phase("ffn_down", l, e_down)

            V.memset(zeros[:], 0.0)
            V.memset(slot[:], -1.0)
            V.memset(put[:], 0.0).then_inc(moe_fills, 1)
            dve.wait_ge(moe_fills, 1)
            V.tensor_copy(zero_r[:], zeros[:]).then_inc(moe_fills, 1)
            dve.wait_ge(wr_hi_done, 1)
            V.tensor_tensor(wr_lo[:], wr[:], wr_hi[:].bitcast(f32), ALU.subtract).then_inc(wr_ready, 1)
            dve.wait_ge(logit_done, 1)
            own.link(V.tensor_tensor(logit[:], ps[:, 5, 0:2 * NE].rearrange("p (t e) -> p t e", t=2),
                                     b_router[:].unsqueeze(1).to_broadcast([P, 2, NE]), ALU.add))

            def field(a):
                return two[:, :, a:a + 1]

            def wide(a):
                return two[:, :, a:a + 1].to_broadcast([P, 2, NE])

            def best(of, value, index, hot):
                own.link(V.tensor_reduce(field(value), of, AX.X, ALU.max))
                own.link(V.tensor_tensor(tie[:], of, wide(value), ALU.is_equal))
                own.link(V.tensor_tensor(tie[:], tie[:], rank8[:].unsqueeze(1).to_broadcast([P, 2, NE]), ALU.mult))
                own.link(V.tensor_reduce(field(index), tie[:], AX.X, ALU.max))
                own.link(V.tensor_tensor(hot, tie[:], wide(index), ALU.is_equal))

            best(logit[:], 0, 1, top1[:])
            own.link(V.scalar_tensor_tensor(out=rest[:], in0=top1[:], scalar=-3.0e38, in1=logit[:], op0=ALU.mult, op1=ALU.add))
            best(rest[:], 3, 1, top2[:])
            V.tensor_tensor(field(4), field(3), field(0), ALU.subtract).then_inc(top_ready, 1)
            V.tensor_tensor(mask[:], top1[:], top2[:], ALU.add).then_inc(mask_ready, 1)
            dve.wait_ge(top_exp, 1)
            own.link(V.tensor_scalar(field(5), field(2), 1.0, None, ALU.add))
            own.link(V.reciprocal(field(5), field(5)))
            own.link(V.tensor_tensor(field(6), field(5), field(2), ALU.mult))
            own.link(V.tensor_tensor(tie[:], top1[:], wide(5), ALU.mult))
            own.link(V.tensor_tensor(rest[:], top2[:], wide(6), ALU.mult))
            own.link(V.tensor_tensor(gate_e[:], tie[:], rest[:], ALU.add))
            dve.wait_ge(pos_done, 1)
            own.link(V.scalar_tensor_tensor(out=tie[:], in0=ps[:, 4, 0:2 * NE].rearrange("p (t e) -> p t e", t=2), scalar=1.0,
                                            in1=mask[:], op0=ALU.add, op1=ALU.mult))
            own.step(V.tensor_scalar(slot[:, :, 0:NE], tie[:], -1.0, None, ALU.add))
            V.memset(over[:, 1, 0:1], 0.0)
            own.link(V.tensor_scalar(over[:, 0, :], ps[:, 4, 2 * NE:3 * NE], float(P), None, ALU.is_gt))
            for e in range(1, NE):
                own.link(V.tensor_tensor(over[:, 1, e:e + 1], over[:, 1, e - 1:e], over[:, 0, e - 1:e], ALU.add))
            own.link(V.tensor_tensor(full_sel[:], over[:, 1:2, :].to_broadcast([P, FULL, NE]), iota[:, 0:FULL].unsqueeze(2).to_broadcast([P, FULL, NE]), ALU.is_equal))
            own.link(V.tensor_tensor(full_sel[:], full_sel[:], over[:, 0:1, :].to_broadcast([P, FULL, NE]), ALU.mult))
            own.link(V.tensor_tensor(full_sel[:], full_sel[:], rank8[:].unsqueeze(1).to_broadcast([P, FULL, NE]), ALU.mult))
            own.link(V.tensor_reduce(full_e[:, 0:FULL], full_sel[:], AX.X, ALU.max))
            own.link(V.tensor_scalar(full_i[:, 1, 0:FULL], full_e[:, 0:FULL], 1.0, None, ALU.min))
            own.link(V.tensor_scalar(full_e[:, 0:FULL], full_e[:, 0:FULL], -1.0, float(NE), ALU.mult, ALU.add))
            V.tensor_scalar(full_i[:, 0, 0:FULL], full_e[:, 0:FULL], float(NE - 1), None, ALU.min).then_inc(route_ready, 1)

            def moe_split(n, jn, slot_):
                dve.wait_ge(hi_done, n + (jn + 1))
                hi, lo = moe_parts(slot_)
                V.tensor_tensor(lo, moe_slot(slot_), hi.bitcast(f32), ALU.subtract).then_inc(lo_done, 1)

            def build_pick(e, v, row0):
                dve.wait_ge(sent, v)
                for t in range(2):
                    ins = V.tensor_scalar(pick[:, t, :], iota[:, row0:row0 + P], slot[:, t, ds(e, 1)], None, ALU.is_equal)
                ins.then_inc(pick_ready, 1)

            def copy_sent(v):
                dve.wait_ge(sent, v + 1)
                for a, bank in ((0, 5), (1, 0)):
                    V.tensor_copy(xe_lo[:, 4 * a:4 * a + 4, :], ps[:, bank, :].rearrange("p (b c) -> p b c", b=4)).then_inc(xe_lo_done, 1)

            def hidden(h, n):
                dve.wait_ge(mm_done, n)
                dve.wait_ge(silu_done, h + 1)
                dve.wait_ge(hid_turned, h + 1)
                V.tensor_tensor(e_hid[:], ps[:, 1, :], e_silu[:], ALU.mult).then_inc(hid_done, 1)

            def turned(h):
                dve.wait_ge(hu_hi_done, h + 1)
                V.tensor_tensor(hu_lo[:], ps[:, 2, :].rearrange("p (b c) -> p b c", b=4), hu_hi[:].bitcast(f32), ALU.subtract).then_inc(hu_lo_done, 1)

            def add_back(v):
                dve.wait_ge(back_added, v * 4 + 1)
                for a in range(4):
                    dve.wait_ge(back_done, v * 4 + (a + 1) + 1)
                    for b in range(2):
                        k = 2 * a + b
                        ins = V.scalar_tensor_tensor(out=x[:, k, 0:SEQ], in0=ps[:, 2 + a, b * SEQ:(b + 1) * SEQ],
                                                     scalar=mods[:, ((DEPTH - 1) * NMOD + 5) * KT + k, 0:1], in1=x[:, k, 0:SEQ], op0=ALU.mult, op1=ALU.add)
                    ins.then_inc(back_added, 1)

            def expert(e, e_next, q, v, row0):
                n = q * MOE_N + DENSE_CHUNKS
                h = q * NC
                moe_split(n, 0, 0)
                moe_split(n, 1, 1)
                dve.wait_ge(put_turned, q + 1)
                for t in range(2):
                    ins = V.tensor_scalar(pick_g[:, t, :], iota[:, row0:row0 + P], slot[:, t, ds(e, 1)], gate_e[:, t, ds(e, 1)],
                                          ALU.is_equal, ALU.mult)
                ins.then_inc(pick_g_ready, 1)
                build_pick(e_next, v + 1, row0)
                moe_split(n, 2, 2)
                moe_split(n, 3, 3)
                hidden(h, n + 4)
                add_back(v)
                with dve.Fori(1, NC) as c:
                    nn = n + c * 6 - 2
                    hc = h + c
                    moe_split(nn, 0, 4)
                    moe_split(nn, 1, 5)
                    turned(hc - 1)
                    for j in range(2, 6):
                        moe_split(nn, j, j - 2)
                        if j == 4:
                            hidden(hc, nn + 4)
                moe_split(n, MOE_N - 2, 4)
                moe_split(n, MOE_N - 1, 5)
                turned(h + (NC - 1))
                copy_sent(v + 1)

            build_pick(0, 0, 0)
            copy_sent(0)
            with dve.Fori(0, NE) as e:
                expert(e, e + 1, e, e, 0)
            add_back(NE)
            with dve.Fori(0, FULL) as f:
                e = dve.value_load(full_i[0:1, 0, ds(f, 1)], min_val=0, max_val=NE - 1)
                used = dve.value_load(full_i[0:1, 1, ds(f, 1)], min_val=0, max_val=1)
                with dve.If(used > 0):
                    v = f * 2 + (NE + 1)
                    build_pick(e, v, P)
                    copy_sent(v)
                    expert(e, NE, f + NE, v, P)
                    add_back(v + 1)
                with dve.Else():
                    dve.nop()
            V.memset(full_e[:], 0.0).then_inc(x_final, 1)

            sum_blocks(ff_normed, SEQ, sq_done, 2 * DEPTH * KT, sum_done)
            make_diag(std_done, 2 * DEPTH + 1, SEQ).then_inc(diag_done, 1)
            dve.wait_ge(spread_done, 2 * DEPTH + 1)
            for k in range(KT):
                V.scalar_tensor_tensor(out=x[:, k, 0:SEQ], in0=x[:, k, 0:SEQ], scalar=g_final[:, k:k + 1], in1=ps[:, 5, 0:SEQ],
                                       op0=ALU.mult, op1=ALU.mult).then_inc(out_ready, 1)

        @block.tensor
        def _(pe):
            mm = nc.tensor.matmul
            for s_ in (pt_done, pv_done, back_done, put_turned, hid_turned):
                pe.nop().then_inc(s_, 1)

            def three(out, parts, first, last):
                for a, (lhs, rhs) in enumerate(parts):
                    ins = mm(out, lhs, rhs, start=first and a == 0, stop=last and a == len(parts) - 1)
                return ins

            def start(n, s, pair):
                pe.wait_ge(lo_done, n + 1)
                pe.wait_ge(evac[s], pair)

            def by_feature(xh, xl, T):
                def run(i, n, s, hi, lo, block_ready=None):
                    for a in range(2):
                        c = slice(a * P, (a + 1) * P)
                        for k in range(KT):
                            if block_ready and s == 0 and a == 0:
                                block_ready(k)
                            ins = three(ps[:, 2 * s + a, 0:T], [(hi[:, k, c], xh[:, k, 0:T]), (hi[:, k, c], xl[:, k, 0:T]),
                                                                (lo[:, k, c], xh[:, k, 0:T])], k == 0, k == KT - 1)
                    return ins
                return run

            def by_token(tiles):
                def run(i, n, s, hi, lo, block_ready=None):
                    for t in range(tiles):
                        r = slice(t * P, (t + 1) * P)
                        out = ps[:, 2 * s + t // 2, t % 2 * CC:(t % 2 + 1) * CC]
                        for k in range(KT):
                            ins = three(out, [(h_hi[:, k, r], hi[:, k, :]), (h_hi[:, k, r], lo[:, k, :]), (h_lo[:, k, r], hi[:, k, :])],
                                        k == 0, k == KT - 1)
                    return ins
                return run

            def phase(name, l, run, start_=0, stop=None, block_ready=None):
                n0, pairs = BASE[name, l], COUNT[name, l] // 2
                stop = pairs if stop is None else stop

                def body(i, **first):
                    n = n0 + 2 * i
                    for s in range(2):
                        start(n + s, s, i + n0 // 2)
                        run(i, n + s, s, as_chunk(name, w_hi[:, s, :]), as_chunk(name, w_lo[:, s, :]), **first).then_inc(mm_done, 1)
                        j = ada_number(name, l, i)
                        if j is not None:
                            (ada_turn if s else ada)(j)
                if block_ready:
                    body(start_, block_ready=block_ready)
                    start_ += 1
                if stop > start_:
                    with pe.Fori(start_, stop) as i:
                        body(i)

            def mean(summed, value, T, bank, done):
                pe.wait_ge(summed, value)
                for t in range(T // P):
                    ins = mm(ps[:, bank, t:t + 1], diag[:, t, :], mean_w[:], start=True, stop=True)
                ins.then_inc(done, 1)

            def spread(made, value, T, bank, done):
                pe.wait_ge(made, value)
                mm(ps[:, bank, 0:T], ones[:], diag[:, 0:T // P, :].rearrange("p t c -> p (t c)"), start=True, stop=True).then_inc(done, 1)

            def waits(sem_, base, blocks=1):
                def block_ready(k):
                    pe.wait_ge(sem_, base + k // blocks + 1)
                return block_ready

            def ada(j, first=False):
                raw_ = (ada_first[:, j % 2, :] if first else ada_raw[:]).rearrange("p (t c) -> p t c", c=CC)
                if first:
                    pe.wait_ge(ada_first_loaded[j % 2], j // 2 * 16 + 16)
                else:
                    pe.wait_ge(ada_loaded, (j - ADA_FIRST) * 16 + 16)
                for k in range(KT):
                    ins = mm(ps[0:2, 4 + (j % 2 if first else 0), 0:CC], cs[:, k, :], raw_[:, k, :], start=k == 0, stop=k == KT - 1)
                ins.then_inc(ada_done, 1)

            def ada_turn(j, b=0):
                pe.wait_ge(ada_copied, j + 1)
                pe.wait_ge(mods_done, j)
                for a in range(2):
                    ins = mm(ps[:, 6, 2 * a:2 * a + 2], ada_row[b][:, a * P:(a + 1) * P], ident[0:2, 0:2], start=True, stop=True)
                ins.then_inc(ada_turned, 1)

            pe.wait_ge(cs_done, 1)
            for j in range(ADA_FIRST):
                ada(j, first=True)
                if j == 1:
                    pe.wait_ge(consts_loaded, 7 * 16)
                if j:
                    ada_turn(j - 1, (j - 1) % 2)
            ada_turn(ADA_FIRST - 1, (ADA_FIRST - 1) % 2)
            pe.wait_ge(fills, 3)
            for l in range(DEPTH):
                T = tokens(l)
                nt = T // P
                mean(sum_done, 2 * l + 1, TOK, 5, ms_done)

                spread(diag_done, 2 * l + 1, TOK, 5, spread_done)
                phase("ag_a", l, by_feature(h_hi, h_lo, T), block_ready=waits(h_ready, 2 * l * KT))
                phase("q", l, by_token(nt))
                phase("kv", l, by_token(TOK // P))
                phase("ag_b", l, by_feature(h_hi, h_lo, T))

                pe.wait_ge(qk_ready, 4 * l + 4)
                pe.wait_ge(mods_done, ada_number("ag_b", l, 1) + 1)
                for g, (kind, t, a) in enumerate(turn_groups(l)):
                    tg = turn_base(l) + g
                    if tg >= 2:
                        pe.wait_ge(turn_copied, tg - 1)
                    for b in range(4):
                        if kind == "q":
                            block_ = q_tm[:, t, (4 * a + b) * P:(4 * a + b + 1) * P]
                        else:
                            block_ = k_dup[:, t, b, :, :].rearrange("p a d -> p (a d)")
                        ins = nc.tensor.transpose(ps[:, 6 + g % 2, b * P:(b + 1) * P], block_, ident[:])
                    ins.then_inc(turn_done, 1)
                pe.wait_ge(turn_copied, turn_base(l + 1))
                for s in range(2):
                    pe.wait_ge(evac[s], BASE["attn_o", l] // 2)

                U, G0 = steps(l), step_base(l)
                N = HP * U

                def score(g):
                    hp, u = divmod(g, U)
                    h2, t, keys = step(l, u)
                    if G0 + g >= 4:
                        pe.wait_ge(exp_done, G0 + g - 3)
                    r = slice(h2 * HD, (h2 + 1) * HD)
                    mm(ps[:, 2 + g % 4, 0:len(keys) * P], q_fm[r, hp, t * P:(t + 1) * P],
                       k_fm[r, (2 * hp + h2) * NKV // NH, keys[0] * P:TOK], start=True, stop=True).then_inc(score_done, 1)

                def turn(g):
                    _, _, keys = step(l, g % U)
                    pe.wait_ge(prob_done, G0 + g + 1)
                    if G0 + g >= 2:
                        pe.wait_ge(pt_copied, G0 + g - 1)
                    for b in range(len(keys)):
                        ins = nc.tensor.transpose(ps[:, 6 + g % 2, b * P:(b + 1) * P], prob[:, g % 2, b * P:(b + 1) * P], ident[:])
                    ins.then_inc(pt_done, 1)

                def weigh(g):
                    hp, u = divmod(g, U)
                    h2, t, keys = step(l, u)
                    kv = (2 * hp + h2) * NKV // NH
                    pe.wait_ge(pt_copied, G0 + g + 1)
                    if u == 0 and hp >= 2:
                        pe.wait_ge(o_lo_done, l * HP + hp - 1)
                    for b, kb in enumerate(keys):
                        ins = mm(ps[h2 * HD:(h2 + 1) * HD, hp % 2, t * P:(t + 1) * P], kv_tm[:, kb, KVW + kv * HD:KVW + (kv + 1) * HD],
                                 prob_t[:, g % 2, b, :], start=b == 0, stop=b == len(keys) - 1)
                    ins.then_inc(pv_done, 1)

                score(0)
                score(1)
                for g in range(N):
                    if g + 2 < N:
                        score(g + 2)
                    turn(g)
                    if g % (2 * U):
                        weigh(g - 1)
                    if g % (2 * U) == 2 * U - 1:
                        weigh(g)

                pe.wait_ge(o_lo_done, (l + 1) * HP)
                phase("attn_o", l, by_feature(o_hi, o_lo, T))
                phase("ga", l, by_feature(h_hi, h_lo, T))
                spread(csum_done, l + 1, T, 5, csum_spread)
                phase("gc", l, by_feature(h_hi, h_lo, T), 0, 1)
                phase("gc", l, by_feature(h_hi, h_lo, T), 1, 2)
                mean(csq_sum, l + 1, T, 7, var_done)
                spread(var_diag, l + 1, T, 7, var_spread)
                phase("conv_o", l, by_feature(z_hi, z_lo, T), block_ready=waits(z_ready, l * KT))
                phase("w_out", l, by_feature(m_hi, m_lo, T), block_ready=waits(m_ready, l * KT // 2, 2))

                mean(sum_done, 2 * l + 2, T, 5, ms_done)
                spread(diag_done, 2 * l + 2, T, 5, spread_done)
                if l % 2 == 0:
                    phase("ffn_up", l, by_feature(h_hi, h_lo, T), block_ready=waits(h_ready, (2 * l + 1) * KT))
                    pe.wait_ge(gu_ready, COUNT["ffn_up", l] // 2 + 1)
                    n0 = BASE["ffn_down", l]
                    with pe.Fori(0, KT // 2) as ii:
                        for b in range(2):
                            pe.wait_ge(evac[b], ii * 2 + n0 // 2)
                            for s in range(2):
                                pe.wait_ge(lo_done, ii * 4 + (n0 + 2 * b + s + 1))
                                hi, lo = as_chunk("ffn_down", w_hi[:, s, :]), as_chunk("ffn_down", w_lo[:, s, :])
                                for k in range(FT // 2):
                                    kk = s * (FT // 2) + k
                                    ins = three(ps[:, 2 * b, 0:T], [(hi[:, k, :], gu_hi[:, kk, :]), (hi[:, k, :], gu_lo[:, kk, :]),
                                                                    (lo[:, k, :], gu_hi[:, kk, :])], kk == 0, kk == FT - 1)
                                ins.then_inc(mm_done, 1)

            pe.wait_ge(h_ready, 2 * DEPTH * KT)
            for g in range(8):
                if g >= 2:
                    pe.wait_ge(tok_copied, g - 1)
                part, t, half = (h_hi if g < 4 else h_lo), g // 2 % 2, g % 2
                for b in range(4):
                    ins = nc.tensor.transpose(ps[:, 6 + g % 2, b * P:(b + 1) * P], part[:, half * 4 + b, t * P:(t + 1) * P].bitcast(f32), ident[:])
                ins.then_inc(tok_turned, 1)
            pe.wait_ge(wr_ready, 1)
            for t in range(2):
                r = slice(t * P, (t + 1) * P)
                for k in range(KT):
                    ins = three(ps[:, 5, t * NE:(t + 1) * NE], [(h_hi[:, k, r], wr_hi[:, k, :]), (h_hi[:, k, r], wr_lo[:, k, :]),
                                                                (h_lo[:, k, r], wr_hi[:, k, :])], k == 0, k == KT - 1)
            ins.then_inc(logit_done, 1)
            pe.wait_ge(mask_ready, 1)
            pos = ps[:, 4, :]
            mm(pos[:, 0:NE], before[:], mask[:, 0, :], start=True, stop=True)
            mm(pos[:, NE:2 * NE], before[:], mask[:, 1, :], start=True, stop=False)
            mm(pos[:, NE:2 * NE], ones[:], mask[:, 0, :], start=False, stop=True)
            mm(pos[:, 2 * NE:3 * NE], ones[:], mask[:, 0, :], start=True, stop=False)
            mm(pos[:, 2 * NE:3 * NE], ones[:], mask[:, 1, :], start=False, stop=True).then_inc(pos_done, 1)
            pe.wait_ge(tok_copied, 8)
            pe.wait_ge(route_ready, 1)
            pe.wait_ge(moe_fills, 2)

            def send(v):
                pe.wait_ge(pick_ready, v + 1)
                for part, banks in ((t_hi, (3, 4)), (t_lo, (5, 0))):
                    for k in range(KT):
                        for t in range(2):
                            ins = mm(ps[:, banks[k // 4], k % 4 * P:(k % 4 + 1) * P], part[:, t, k * P:(k + 1) * P], pick[:, t, :],
                                     start=t == 0, stop=t == 1)
                ins.then_inc(sent, 1)

            def zero_y():
                for a in range(2):
                    ins = mm(ps[:, 6 + a, :], zero_r[:, 0:P], zero_r[:], start=True, stop=True)
                ins.then_inc(y_zeroed, 1)

            def up(n, j0):
                for a in range(4):
                    pe.wait_ge(lo_done, n + (a + 1))
                    hi, lo = (w.rearrange("p (t c) -> p t c", c=EC) for w in moe_parts(j0 + a))
                    for k in range(4):
                        kk = a % 2 * 4 + k
                        ins = three(ps[:, a // 2, :], [(xe_hi[:, kk, :], hi[:, k, :]), (xe_hi[:, kk, :], lo[:, k, :]),
                                                       (xe_lo[:, kk, :], hi[:, k, :])], kk == 0, kk == KT - 1)
                    ins.then_inc(mm_done, 1)

            def turn_hidden(h):
                pe.wait_ge(hid_done, h + 1 + 1)
                for b in range(4):
                    ins = nc.tensor.transpose(ps[:, 2, b * P:(b + 1) * P], e_hid[:, b * P:(b + 1) * P], ident[:])
                ins.then_inc(hid_turned, 1)

            def down(n, h, j0):
                pe.wait_ge(hu_hi_done, h + 1)
                pe.wait_ge(hu_lo_done, h + 1)
                for a in range(2):
                    pe.wait_ge(lo_done, n + (a + 1))
                    hi, lo = (w.rearrange("p (t c) -> p t c", c=D) for w in moe_parts(j0 + a))
                    for k in range(2):
                        for half in range(2):
                            c = slice(half * 512, (half + 1) * 512)
                            for lhs, rhs in ((hu_hi, hi), (hu_hi, lo), (hu_lo, hi)):
                                ins = mm(ps[:, 6 + half, :], lhs[:, 2 * a + k, :], rhs[:, k, c], start=False, stop=True, skip_group_check=True)
                    ins.then_inc(mm_done, 1)

            def give_back(v):
                pe.wait_ge(y_copied, v * 2 + 2)
                zero_y()
                for a in range(4):
                    for b in range(2):
                        k = 2 * a + b
                        ins = mm(ps[:, 2 + a, b * SEQ:(b + 1) * SEQ], y_rows[:, k * P:(k + 1) * P], put[:].rearrange("p t c -> p (t c)"),
                                 start=True, stop=True)
                    ins.then_inc(back_done, 1)

            def expert(q, v):
                n = q * MOE_N + DENSE_CHUNKS
                h = q * NC
                pe.wait_ge(xe_hi_done, v * 2 + 2)
                pe.wait_ge(xe_lo_done, v * 2 + 2)
                pe.wait_ge(put_copied, q + 1)
                up(n, 0)
                give_back(v)
                with pe.Fori(1, NC) as c:
                    nn = n + c * 6 - 2
                    hc = h + c
                    pe.wait_ge(back_added, v * 4 + 4 + 1)
                    turn_hidden(hc - 1)
                    pe.wait_ge(silu_done, hc)
                    up(nn, 4)
                    down(nn + 4, hc - 1, 2)
                pe.wait_ge(silu_done, h + NC)
                send(v + 1)
                turn_hidden(h + (NC - 1))
                pe.wait_ge(pick_g_ready, q + 1)
                for t in range(2):
                    ins = nc.tensor.transpose(ps[:, 1, t * P:(t + 1) * P], pick_g[:, t, :], ident[:])
                ins.then_inc(put_turned, 1)
                down(n + (MOE_N - 2), h + (NC - 1), 4)

            def last_rows(q, v):
                pe.wait_ge(put_copied, q + 1)
                pe.wait_ge(xe_hi_done, v * 2 + 2)
                pe.wait_ge(xe_lo_done, v * 2 + 2)
                give_back(v)
                pe.wait_ge(back_added, v * 4 + 4 + 1)

            zero_y()
            send(0)
            with pe.Fori(0, NE) as e:
                expert(e, e)
            last_rows(NE, NE)
            with pe.Fori(0, FULL) as f:
                used = pe.value_load(full_i[0:1, 1, ds(f, 1)], min_val=0, max_val=1)
                with pe.If(used > 0):
                    v = f * 2 + (NE + 1)
                    send(v)
                    expert(f + NE, v)
                    last_rows(f + (NE + 1), v + 1)
                with pe.Else():
                    pe.nop()
            mean(sum_done, 2 * DEPTH + 1, SEQ, 5, ms_done)
            spread(diag_done, 2 * DEPTH + 1, SEQ, 5, spread_done)


def kernel(**inputs):
    import concourse.bacc as bacc
    from concourse.bass_utils import run_bass_kernel_spmd as run

    a = {k: np.asarray(v) for k, v in inputs.items()}

    def c(v):
        return np.ascontiguousarray(v)

    def blocks(v):
        return c(np.moveaxis(v.reshape(*v.shape[:-1], -1, P), -1, 0))

    pos = np.arange(SEQ)
    freqs = np.float32(ROPE_THETA) ** (-np.arange(HD // 4, dtype=np.float32) / (HD // 4))
    ang = np.concatenate([(pos // GRID_W)[:, None].astype(np.float32) * freqs, (pos % GRID_W)[:, None].astype(np.float32) * freqs], -1)
    rope = np.stack([np.cos(ang), np.sin(ang)]).astype(np.float32).reshape(2, SEQ // P, P, HALF).transpose(2, 0, 1, 3)
    arrays = {
        "x_t": c(a["x"][0].T), "ctx_t": c(a["ctx"][0].T),
        "c_t": c(np.stack([a["c"][0], a["c_ctx"]], -1).reshape(KT, P, 2).transpose(1, 0, 2)),
        "ident": np.eye(P, dtype=np.float32), "rope": c(rope),
        "dw": c(a["conv_dw"].transpose(0, 2, 1).reshape(DEPTH, KT, P, TAPS).transpose(2, 0, 1, 3)),
        "vecs": blocks(np.stack([a[n] for n in ("g_mix", "g_ffn", "conv_b", "conv_ln_g", "conv_ln_b")])),
        "g_final": blocks(a["g_final"]),
        "qk_gain": c(np.broadcast_to(np.stack([a["q_norm"], a["k_norm"]])[None], (P, 2, DEPTH, HD))),
        "b_ada": c(blocks(a["b_ada"]).reshape(P, -1)),
        "w_router": c(a["w_router"][0].reshape(KT, P, NE).transpose(1, 0, 2)),
        "b_router": c(np.broadcast_to(a["b_router"], (P, NE))),
        "iota": c(np.broadcast_to(np.arange(2 * P, dtype=np.float32), (P, 2 * P))),
        "before": np.triu(np.ones((P, P), np.float32), 1),
        "rank8": c(np.broadcast_to(np.arange(NE, 0, -1, dtype=np.float32), (P, NE))),
    }
    for name in ("w_ada", "w_in", "w_attn_o", "w_conv_o", "w_out", "w_ff_gate", "w_ff_up", "w_ff_down", "w_moe_gate", "w_moe_up", "w_moe_down"):
        arrays[name] = c(a[name])
    nc = bacc.Bacc("TRN2", target_bir_lowering=False, num_devices=1)
    A = {k: nc.dram_tensor("in_" + k, v.shape, mybir.dt.from_np(v.dtype), kind="ExternalInput").ap() for k, v in arrays.items()}
    out = nc.dram_tensor("out_t", (D, SEQ), mybir.dt.float32, kind="ExternalOutput").ap()
    build(nc, A, out)
    r = run(nc, [{"in_" + k: v for k, v in arrays.items()}], core_ids=[0])
    return np.ascontiguousarray(r.results[0]["out_t"].T)[None]
```

```python
import concourse.bass as bass
from concourse import mybir
from contextlib import ExitStack, contextmanager
import numpy as np

P = 128
D = 1024
SEQ = 256
CTX = 256
TOK = SEQ + CTX
DEPTH = 2
NH, NKV, HD = 16, 4, 64
HALF = HD // 2
GRID_W = 64
ROPE_THETA = 10000.0
TAPS, PAD = 31, 15
DFF = 2816
NE = 8
DE = 3584
NMOD = 6
EPS = 1e-6
KT = D // P
QW, KVW = NH * HD, NKV * HD
OFF_K, OFF_V, OFF_CONV = QW, QW + KVW, QW + 2 * KVW
OFF_GATE = OFF_CONV + 2 * D
FT = DFF // P
CC = 256
CHUNK = KT * CC
HP = NH // 2
ZW = SEQ + 2 * PAD
EC = 512
NC = DE // EC
TAPS_Q, TAPS_KV, TAPS_ATT = 12, 20, 16
TAPS_AO = (TAPS_KV + TAPS) // 2
TAPS_AO2 = (TAPS_ATT + TAPS + 1) // 2
ADA = NMOD * D // CC
ADA_PHASES = {"ag_a": 0, "q": 2, "kv": 4, "ag_b": 5, "attn_o": 7, "ga": 9, "gc": 11}
ADA_FIRST = ADA - 13
ADA_SLOTS = 4
MOE_RAW = 6
MOE_N = 6 * NC
MOE_PARTS = 3
K_SQ = 4 * NH * HALF
FULL = 2 * SEQ // (P + 1)

PHASES = []
for _l in range(DEPTH):
    PHASES += [("ag_a", _l, D // CC), ("q", _l, QW // CC), ("kv", _l, 2), ("ag_b", _l, D // CC),
               ("attn_o", _l, D // CC), ("ga", _l, D // CC), ("gc", _l, D // CC), ("conv_o", _l, D // CC),
               ("w_out", _l, D // CC)]
    if _l % 2 == 0:
        PHASES += [("ffn_up", _l, 2 * DFF // CC), ("ffn_down", _l, 2 * KT)]
BASE, COUNT, _n = {}, {}, 0
for _name, _l, _c in PHASES:
    BASE[_name, _l], COUNT[_name, _l] = _n, _c
    _n += _c
DENSE_CHUNKS = _n
LAST_PHASE = PHASES[-1][:2]


class Chain:

    def __init__(self, eng, sem):
        self.eng, self.sem, self.base, self.k = eng, sem, 0, 0

    def step(self, ins):
        self.k += 1
        ins.then_inc(self.sem, 1)

    def wait(self, back=0):
        self.eng.wait_ge(self.sem, self.base + (self.k - back))

    def link(self, ins):
        self.step(ins)
        self.wait()

    @contextmanager
    def loop(self, start, stop, count):
        at = self.base + self.k
        with self.eng.Fori(start, stop) as i:
            self.base, self.k = i * count + (at - start * count), 0
            yield i
            assert self.k == count, (self.k, count)
        self.base, self.k = at + (stop - start) * count, 0


def build(nc, A, out_t):
    f32, f32r, i32 = mybir.dt.float32, mybir.dt.float32r, mybir.dt.int32
    ALU, ACT, AX = mybir.AluOpType, mybir.ActivationFunctionType, mybir.AxisListType
    ds = bass.ds
    with ExitStack() as ctx:
        def sb(name, shape, dt=f32):
            return ctx.enter_context(nc.sbuf_tensor(name, shape, dt))

        def sem(name):
            return ctx.enter_context(nc.semaphore(name))

        x = sb("x", [P, KT, TOK])
        raw = sb("raw", [P, 2, CHUNK])
        w_hi = sb("w_hi", [P, 2, CHUNK], f32r)
        w_lo = sb("w_lo", [P, 2, CHUNK], f32r)
        ident = sb("ident", [P, P])
        mean_w = sb("mean_w", [P, 1])
        ones = sb("ones", [P, P])
        rope = sb("rope", [P, 2, 2, HALF])
        dw = sb("dw", [P, DEPTH, KT, TAPS])
        vecs = sb("vecs", [P, 5, DEPTH, KT])
        g_final = sb("g_final", [P, KT])
        qk_gain = sb("qk_gain", [P, 2, DEPTH, HD])
        b_ada = sb("b_ada", [P, DEPTH * NMOD * KT])
        cvec = sb("cvec", [P, KT, 2])
        cs = sb("cs", [P, KT, 2])
        ada_row_0 = sb("ada_row_0", [2, CC])
        mods = sb("mods", [P, DEPTH * NMOD * KT, 2])
        scale1 = sb("scale1", [P, KT, 2])
        eps_t = sb("eps_t", [P, 1])
        scratch = sb("scratch", [P, 1])
        col = sb("col", [P, TOK // P])
        diag = sb("diag", [P, TOK // P, P])
        ss = sb("ss", [P, 4 * NH + 4 * NKV])
        nbias = sb("nbias", [P, 4])
        rowsum = sb("rowsum", [P, 4])
        rinv = sb("rinv", [P, 2])

        top = -(-nc.sbuf_base // 64) * 64
        end = nc.sbuf_usable_end

        def at(name, offset, shape, dt=f32):
            assert offset + 4 * int(np.prod(shape[1:])) <= end, (name, offset)
            return nc.alloc_sbuf_tensor_at(name, shape, dt, offset=offset)

        KB = 1024
        h_hi = at("h_hi", top, [P, KT, TOK], f32r)
        h_lo = at("h_lo", top + 16 * KB, [P, KT, TOK], f32r)
        r1 = top + 32 * KB
        r2 = r1 + 4 * KT * 2 * ZW
        r3, r4, r5, r6 = (r2 + n * 16 * KB for n in (1, 2, 3, 4))
        normed = at("normed", r1, [P, KT, TOK])
        zpad = at("zpad", r1, [P, KT, 2, ZW])
        conv_sq = at("conv_sq", r1, [P, KT, TOK])
        z_hi = at("z_hi", r1, [P, KT, TOK], f32r)
        conv = at("conv", r2, [P, KT, TOK])
        z_lo = at("z_lo", r2, [P, KT, TOK], f32r)
        q_tm = at("q_tm", r3, [P, 4, QW])
        o_lo = at("o_lo", r3, [P, KT, TOK], f32r)
        m_hi = at("m_hi", r3, [P, KT, TOK], f32r)
        qk_tmp = at("qk_tmp", r4, [P, 4 * QW])
        q_fm = at("q_fm", r4, [P, HP, TOK])
        o_hi = at("o_hi", r4, [P, KT, TOK], f32r)
        gate_c = at("gate_c", r4, [P, KT, TOK])
        kv_tm = at("kv_tm", r5, [P, 4, 2 * KVW])
        k_fm = at("k_fm", r5 + 8 * KB, [P, NKV, TOK])
        merged = at("merged", r5, [P, KT, TOK])
        m_lo = at("m_lo", r5, [P, KT, TOK], f32r)
        sig = at("sig", r6, [P, 2, TOK])
        prob = at("prob", r6, [P, 4, TOK])
        prob_t = at("prob_t", r6 + 8 * KB, [P, 2, 4, P])
        k_dup = at("k_dup", r6 + 4 * KB, [P, 4, NKV, 2, HD])
        ff_normed = at("ff_normed", r1, [P, KT, TOK])
        gu_hi = at("gu_hi", r1, [P, FT, TOK], f32r)
        gu_lo = at("gu_lo", r1 + FT * 2 * KB, [P, FT, TOK], f32r)
        ff_silu = at("ff_silu", r1 + FT * 4 * KB, [P, 2, TOK])
        ada_raw = at("ada_raw", r1 + 94 * KB, [P, CHUNK])
        ada_row_1 = at("ada_row_1", r5, [2, CC])
        ada_row = (ada_row_0, ada_row_1)
        ada_first = at("ada_first", r3, [P, ADA_SLOTS, CHUNK])
        w_hi_3 = at("w_hi_3", top, [P, CHUNK], f32r)
        w_lo_3 = at("w_lo_3", top + 16 * KB, [P, CHUNK], f32r)
        e0 = r1 + 16 * KB
        moe_raw = at("moe_raw", e0, [P, MOE_RAW - 2, CHUNK])
        e1 = e0 + 32 * KB
        t_hi = at("t_hi", e1, [P, 2, D], f32r)
        t_lo = at("t_lo", e1 + 8 * KB, [P, 2, D], f32r)
        xe_hi = at("xe_hi", e1 + 16 * KB, [P, KT, P], f32r)
        xe_lo = at("xe_lo", e1 + 20 * KB, [P, KT, P], f32r)
        hu_hi = at("hu_hi", e1 + 24 * KB, [P, 4, P], f32r)
        hu_lo = at("hu_lo", e1 + 26 * KB, [P, 4, P], f32r)
        e_silu = at("e_silu", e1 + 28 * KB, [P, EC])
        e_hid = at("e_hid", e1 + 30 * KB, [P, EC])
        y_rows = at("y_rows", e1 + 32 * KB, [P, D])
        e2 = e1 + 36 * KB
        pick = at("pick", e2, [P, 2, P], f32r)
        pick_g = at("pick_g", e2 + KB, [P, 2, P])
        put = at("put", e2 + 2 * KB, [P, 2, P])
        wr = at("wr", e2 + 3 * KB, [P, KT, NE])
        wr_hi = at("wr_hi", e2 + 3 * KB + 256, [P, KT, NE], f32r)
        wr_lo = at("wr_lo", e2 + 3 * KB + 512, [P, KT, NE], f32r)
        e3 = e2 + 4 * KB
        b_router = at("b_router", e3, [P, NE])
        iota = at("iota", e3 + 64, [P, P])
        before = at("before", e3 + 64 + KB, [P, P])
        e4 = e3 + 64 + 2 * KB
        logit = at("logit", e4, [P, 2, NE])
        rank8 = at("rank8", e4 + 64, [P, NE])
        top1 = at("top1", e4 + 128, [P, 2, NE])
        top2 = at("top2", e4 + 192, [P, 2, NE])
        rest = at("rest", e4 + 256, [P, 2, NE])
        tie = at("tie", e4 + 320, [P, 2, NE])
        two = at("two", e4 + 384, [P, 2, 8])
        mask = at("mask", e4 + 448, [P, 2, NE])
        slot = at("slot", e4 + 640, [P, 2, 16])
        gate_at = at("gate_at", e3 + 64 + KB + 512, [P, 2, 16])
        over = at("over", e4 + 768, [P, 2, NE])
        full_sel = at("full_sel", e4 + 832, [P, FULL, NE])
        full_e = at("full_e", e4 + 928, [P, 4])
        used_f = at("used_f", e4 + 512, [P, 4])
        most = at("most", e4 + 576, [P, 1])
        full_n = at("full_n", e4 + 544, [P, 1], i32)
        full_i = at("full_i", e4 + 960, [P, 2, 4], i32)
        zeros = at("zeros", e4 + 1024, [P, EC])
        zero_r = at("zero_r", e4 + 1024 + 2 * KB, [P, EC], f32r)

        ps = ctx.enter_context(nc.psum_tensor("ps", [P, 8, 512], f32))

        raw_loaded = [sem(f"raw_loaded{s}") for s in range(MOE_RAW)]
        hi_done = sem("hi_done")
        lo_done = sem("lo_done")
        mm_done = sem("mm_done")
        evac = [sem("evac0"), sem("evac1")]
        c_loaded, consts_loaded, x_loaded, fills = (sem(n) for n in ("c_loaded", "consts_loaded", "x_loaded", "fills"))
        cs_done = sem("cs_done")
        ada_first_loaded = [sem(f"ada_first_loaded{a}") for a in range(ADA_SLOTS)]
        ada_loaded, ada_done, ada_copied, ada_turned, mods_done = (sem(n) for n in ("ada_loaded", "ada_done", "ada_copied", "ada_turned", "mods_done"))
        sq_done, sum_done, ms_done, std_done = (sem(n) for n in ("sq_done", "sum_done", "ms_done", "std_done"))
        diag_done, spread_done = sem("diag_done"), sem("spread_done")
        unit_done, h_hi_done, h_ready = (sem(n) for n in ("unit_done", "h_hi_done", "h_ready"))
        qk_sq, qk_ss, qk_std, qk_ready = (sem(n) for n in ("qk_sq", "qk_ss", "qk_std", "qk_ready"))
        turn_done, turn_copied = sem("turn_done"), sem("turn_copied")
        score_done, nbias_done, exp_done, prob_done = (sem(n) for n in ("score_done", "nbias_done", "exp_done", "prob_done"))
        rinv_done = sem("rinv_done")
        pt_done, pt_copied, pv_done = (sem(n) for n in ("pt_done", "pt_copied", "pv_done"))
        o_hi_done, o_lo_done = sem("o_hi_done"), sem("o_lo_done")
        csum_done, csum_spread, cent_done, csq_done, csq_sum, var_done = (
            sem(n) for n in ("csum_done", "csum_spread", "cent_done", "csq_done", "csq_sum", "var_done"))
        cstd_done, var_diag, var_spread = (sem(n) for n in ("cstd_done", "var_diag", "var_spread"))
        cunit_done, z_hi_done, z_ready = (sem(n) for n in ("cunit_done", "z_hi_done", "z_ready"))
        sig_used, merged_done, m_hi_done, m_ready = (sem(n) for n in ("sig_used", "merged_done", "m_hi_done", "m_ready"))
        gu_hi_done, gu_ready = sem("gu_hi_done"), sem("gu_ready")
        moe_consts, moe_fills = sem("moe_consts"), sem("moe_fills")
        wr_hi_done, wr_ready, tok_turned, tok_copied, logit_done = (sem(n) for n in ("wr_hi_done", "wr_ready", "tok_turned", "tok_copied", "logit_done"))
        top_ready, top_exp, mask_ready, pos_done, route_ready = (sem(n) for n in ("top_ready", "top_exp", "mask_ready", "pos_done", "route_ready"))
        pick_ready, pick_g_ready, sent, xe_hi_done, xe_lo_done = (sem(n) for n in ("pick_ready", "pick_g_ready", "sent", "xe_hi_done", "xe_lo_done"))
        silu_done, hid_done, hid_turned, hu_hi_done, hu_lo_done = (sem(n) for n in ("silu_done", "hid_done", "hid_turned", "hu_hi_done", "hu_lo_done"))
        y_zeroed, y_copied, put_turned, put_copied, back_done, back_added = (sem(n) for n in ("y_zeroed", "y_copied", "put_turned", "put_copied", "back_done", "back_added"))
        x_final, out_ready, out_done = sem("x_final"), sem("out_ready"), sem("out_done")
        act_own, dve_own = sem("act_own"), sem("dve_own")

        def tokens(l):
            return SEQ if l == DEPTH - 1 else TOK

        def src(name, l, i, s):
            def cols(w, c):
                return w.rearrange("(t p) c -> p t c", p=P)[:, :, ds(c, CC)]
            if name in ("ag_a", "ag_b"):
                first = OFF_CONV + (D // 2 if name == "ag_b" else 0)
                return cols(A["w_in"][l], i * CC + (first + D if s == 0 else first))
            first = {"q": 0, "kv": OFF_K, "ga": OFF_GATE, "gc": OFF_GATE + D}
            if name in first:
                return cols(A["w_in"][l], i * (2 * CC) + (first[name] + s * CC))
            square = {"attn_o": "w_attn_o", "conv_o": "w_conv_o", "w_out": "w_out"}
            if name in square:
                return cols(A[square[name]][l], i * (2 * CC) + s * CC)
            if name == "ffn_up":
                return cols(A["w_ff_up" if s else "w_ff_gate"][l // 2], i * CC)
            half = FT // 2
            w = A["w_ff_down"][l // 2].rearrange("(t p) c -> p t c", p=P)
            return w[:, s * half:(s + 1) * half, ds(i * P, P)]

        def as_chunk(name, buf):
            if name == "ffn_down":
                return buf[:, 0:FT // 2 * P].rearrange("p (t c) -> p t c", c=P)
            return buf.rearrange("p (t c) -> p t c", c=CC)

        def ada_number(name, l, i):
            if name in ADA_PHASES:
                return i + (l * ADA + ADA_FIRST + ADA_PHASES[name])
            return i + (l + 1) * ADA if name == "ffn_up" else None

        def norm_bank(nrm):
            return 5 if nrm else 7

        def moe_slot(slot_):
            return raw[:, slot_, :] if slot_ < 2 else moe_raw[:, slot_ - 2, :]

        def moe_parts(slot_):
            a = slot_ % MOE_PARTS
            return (w_hi[:, a, :], w_lo[:, a, :]) if a < 2 else (w_hi_3[:], w_lo_3[:])

        def moe_loads(h, slot_, j):
            return (h + (j // MOE_RAW + 1 + (DENSE_CHUNKS // 2 if slot_ < 2 else 0))) * 16

        def turn_groups(l):
            return [("q", t, a) for t in range(tokens(l) // P) for a in range(2)] + [("k", t, 0) for t in range(TOK // P)]

        def turn_base(l):
            return sum(len(turn_groups(m)) for m in range(l))

        def steps(l):
            return 2 * (tokens(l) // P)

        def step_base(l):
            return sum(HP * steps(m) for m in range(l))

        def step(l, u):
            nt = tokens(l) // P
            t = u % nt
            return u // nt, t, (range(4) if t < SEQ // P else range(2, 4))

        block = ctx.enter_context(nc.Block())

        @block.sync
        def _(sp):
            sp.dma_start(cvec[:, :, :], A["c_t"]).then_inc(c_loaded, 16)

            def load(name, l, i, wait=True):
                n = BASE[name, l] + 2 * i
                for s in range(2):
                    if wait:
                        sp.wait_ge(lo_done, n + (s - 1))
                    sp.dma_start(as_chunk(name, raw[:, s, :]), src(name, l, i, s)).then_inc(raw_loaded[s], 16)

            def ada_load(l, jl, dst, loaded):
                w = A["w_ada"][l].rearrange("(t p) c -> p t c", p=P)
                sp.dma_start(dst.rearrange("p (t c) -> p t c", c=CC), w[:, :, ds(jl * CC, CC)]).then_inc(loaded, 16)

            def load_beside(name, l, i):
                j = ada_number(name, l, i)
                if j is not None:
                    sp.wait_ge(ada_done, j)
                    if name == "ffn_up":
                        ada_load(l + 1, i, ada_raw[:], ada_loaded)
                    else:
                        ada_load(l, i + (ADA_FIRST + ADA_PHASES[name]), ada_raw[:], ada_loaded)

            for name, l, chunks in PHASES:
                if BASE[name, l] == 0:
                    for j in range(ADA_FIRST):
                        if j >= ADA_SLOTS:
                            sp.wait_ge(ada_done, j - ADA_SLOTS + 1)
                        ada_load(0, j, ada_first[:, j % ADA_SLOTS, :], ada_first_loaded[j % ADA_SLOTS])
                        if j == ADA_FIRST - 3:
                            load(name, l, 0, wait=False)
                        if j == ADA_SLOTS - 1:
                            sp.dma_start(x[:, :, 0:SEQ], A["x_t"].rearrange("(k p) t -> p k t", p=P)).then_inc(x_loaded, 16)
                            sp.dma_start(x[:, :, SEQ:TOK], A["ctx_t"].rearrange("(k p) t -> p k t", p=P)).then_inc(x_loaded, 16)
                        if j != 1:
                            continue
                        for dst, nm in ((ident, "ident"), (rope, "rope"), (dw, "dw"), (vecs, "vecs"), (g_final, "g_final"),
                                        (qk_gain, "qk_gain"), (b_ada, "b_ada")):
                            sp.dma_start(dst[:], A[nm]).then_inc(consts_loaded, 16)
                    load_beside(name, l, 0)
                with sp.Fori(1 if BASE[name, l] == 0 else 0, chunks // 2) as i:
                    load(name, l, i)
                    load_beside(name, l, i)

            sp.wait_ge(mm_done, DENSE_CHUNKS)
            for dst, nm in ((wr, "w_router"), (b_router, "b_router"), (iota, "iota"), (before, "before"), (rank8, "rank8")):
                sp.dma_start(dst[:], A[nm]).then_inc(moe_consts, 16)
            w_g, w_u, w_d = (A[n].rearrange("l e (t p) c -> (l e) p t c", p=P) for n in ("w_moe_gate", "w_moe_up", "w_moe_down"))

            def moe_load(e, q, j, slot_, w, row, rows, col, cols):
                sp.wait_ge(lo_done, q * MOE_N + (j + (DENSE_CHUNKS - MOE_RAW + 1)))
                sp.dma_start(moe_slot(slot_).rearrange("p (t c) -> p t c", t=rows),
                             w[ds(e, 1), :, ds(row, rows), ds(col, cols)].rearrange("o p t c -> p (o t) c")).then_inc(raw_loaded[slot_], 16)

            def load_up(e, q, c, j, slot0):
                for a in range(4):
                    moe_load(e, q, j + a, (slot0 + a) % MOE_RAW, w_g if a < 2 else w_u, a % 2 * (KT // 2), KT // 2, c * EC, EC)

            def load_down(e, q, c, j, slot0):
                for a in range(2):
                    moe_load(e, q, j + a, (slot0 + a) % MOE_RAW, w_d, c * 4 + 2 * a, 2, 0, D)

            def expert(e, q):
                load_up(e, q, 0, 0, 0)
                with sp.Fori(1, NC) as c:
                    load_up(e, q, c, c * 6 - 2, 4)
                    load_down(e, q, c - 1, c * 6 + 2, 2)
                load_down(e, q, NC - 1, MOE_N - 2, 4)

            with sp.Fori(0, NE) as e:
                expert(e, e)
            sp.wait_ge(route_ready, 1)
            with sp.Fori(0, FULL) as f:
                e = sp.value_load(full_i[0:1, 0, ds(f, 1)], min_val=0, max_val=NE - 1)
                used = sp.value_load(full_i[0:1, 1, ds(f, 1)], min_val=0, max_val=1)
                with sp.If(used > 0):
                    expert(e, f + NE)
                with sp.Else():
                    sp.nop()
            for k in range(KT):
                sp.wait_ge(out_ready, k + 1)
                sp.dma_start(out_t[k * P:(k + 1) * P, :], x[:, k, 0:SEQ]).then_inc(out_done, 16)
            sp.wait_ge(out_done, 16 * KT)

        @block.gpsimd
        def _(pool):
            nc.gpsimd.memset(mean_w[:], 1.0 / D).then_inc(fills, 1)
            nc.gpsimd.memset(eps_t[:], EPS).then_inc(fills, 1)
            nc.gpsimd.memset(ones[:], 1.0).then_inc(fills, 1)

        @block.scalar
        def _(act):
            own = Chain(act, act_own)

            act.nop().then_inc(put_copied, 1)

            def split(n, s, pair, first=False):
                act.wait_ge(raw_loaded[s], pair * 16 + 16)
                if not first:
                    act.wait_ge(mm_done, n - 1)
                nc.scalar.activation(w_hi[:, s, :], raw[:, s, :], ACT.Copy).then_inc(hi_done, 1)

            def phase(name, l, evacuate, start=0, stop=None):
                n0, pairs = BASE[name, l], COUNT[name, l] // 2
                stop = pairs if stop is None else stop
                last = (name, l) == LAST_PHASE and stop == pairs

                def body(i, more=True):
                    n = n0 + 2 * i
                    split(n + 1, 1, n0 // 2 + i, first=isinstance(n, int) and n == 0)
                    evacuate(i, n, 0)
                    if more:
                        split(n + 2, 0, n0 // 2 + 1 + i)
                    j = ada_number(name, l, i)
                    if j is not None:
                        ada_copy(j)
                    evacuate(i, n + 1, 1)
                if n0 == 0:
                    body(start)
                    start += 1
                if stop - last > start:
                    with act.Fori(start, stop - last) as i:
                        body(i)
                if last:
                    body(stop - 1, more=False)

            def none(i, n, s):
                pass

            act.wait_ge(c_loaded, 16)
            nc.scalar.activation(cs[:], cvec[:], ACT.Silu).then_inc(cs_done, 1)

            def ada_copy(j, b=0):
                act.wait_ge(ada_done, j + 1)
                nc.scalar.activation(ada_row[b][:], ps[0:2, 4 + b, 0:CC], ACT.Copy).then_inc(ada_copied, 1)

            def squares(dst, src_, T, done):
                for k in range(KT):
                    nc.scalar.activation(dst[:, k, 0:T], src_[:, k, 0:T], ACT.Square).then_inc(done, 1)

            def load_sqrt():
                own.link(nc.scalar.activation(scratch[:], eps_t[:], ACT.Sqrt))

            def root(nrm, T):
                load_sqrt()
                act.wait_ge(ms_done, nrm + 1)
                nc.scalar.activation(col[:, 0:T // P], ps[:, norm_bank(nrm), 0:T // P], ACT.Sqrt, bias=eps_t[:, 0:1]).then_inc(std_done, 1)

            def norm(nrm, l, T, shift, buf):
                if nrm:
                    root(nrm, T)
                for k in range(KT):
                    act.wait_ge(unit_done, nrm * KT + k + 1)
                    for g in range(T // SEQ):
                        seg_ = slice(g * SEQ, (g + 1) * SEQ)
                        own.step(nc.scalar.activation(buf[:, k, seg_], buf[:, k, seg_], ACT.Identity,
                                                      bias=mods[:, (l * NMOD + shift) * KT + k, g:g + 1], scale=scale1[:, k, g:g + 1]))
                    own.wait()
                    nc.scalar.activation(h_hi[:, k, 0:T], buf[:, k, 0:T], ACT.Copy).then_inc(h_hi_done, 1)

            def whole(name, l):
                for s in range(2):
                    act.wait_ge(evac[s], (BASE[name, l] + COUNT[name, l]) // 2)

            for l in range(DEPTH):
                T = tokens(l)
                nt = T // P

                if l == 0:
                    for j in range(ADA_FIRST // 2):
                        ada_copy(j, j % 2)
                    act.wait_ge(x_loaded, 32)
                    act.wait_ge(fills, 3)
                else:
                    whole(*PHASES[[p[:2] for p in PHASES].index(("ag_a", l)) - 1][:2])
                squares(normed, x, TOK, sq_done)
                if l == 0:
                    for j in range(ADA_FIRST // 2, ADA_FIRST):
                        ada_copy(j, j % 2)
                        if j == ADA_FIRST - 2:
                            root(0, TOK)
                    split(0, 0, 0, first=True)
                norm(2 * l, l, TOK, 0, normed)

                def e_q(i, n, s):
                    act.wait_ge(mm_done, n + 1)
                    for b in range(nt // 2):
                        ins = nc.scalar.activation(q_tm[:, 2 * b:2 * b + 2, ds(i * (2 * CC) + s * CC, CC)],
                                                   ps[:, 2 * s + b, :].rearrange("p (t c) -> p t c", t=2), ACT.Copy)
                    ins.then_inc(evac[s], 1)

                def e_kv(i, n, s):
                    act.wait_ge(mm_done, n + 1)
                    for b in range(2):
                        ins = nc.scalar.activation(kv_tm[:, 2 * b:2 * b + 2, s * CC:(s + 1) * CC],
                                                   ps[:, 2 * s + b, :].rearrange("p (t c) -> p t c", t=2), ACT.Copy)
                    ins.then_inc(evac[s], 1)

                def e_ag(name):
                    def run(i, n, s):
                        if s == 0:
                            act.wait_ge(mm_done, n + 1)
                            act.wait_ge(evac[1], i + BASE[name, l] // 2)
                            nc.scalar.activation(sig[:, :, 0:T], ps[:, 0:2, 0:T], ACT.Sigmoid).then_inc(evac[0], 1)
                    return run

                phase("ag_a", l, e_ag("ag_a"))
                phase("q", l, e_q)
                for s in range(2):
                    act.wait_ge(evac[s], BASE["kv", l] // 2)
                nc.scalar.activation(qk_tmp[:, 0:nt * QW], q_tm[:, 0:nt, :].rearrange("p t c -> p (t c)"), ACT.Square).then_inc(qk_sq, 1)
                phase("kv", l, e_kv)
                for s in range(2):
                    act.wait_ge(evac[s], BASE["ag_b", l] // 2)
                act.wait_ge(qk_ss, 2 * l + 1)
                nc.scalar.activation(qk_tmp[:, K_SQ:K_SQ + 4 * KVW].rearrange("p (t c) -> p t c", t=4), kv_tm[:, :, 0:KVW], ACT.Square).then_inc(qk_sq, 1)
                act.wait_ge(qk_ss, 2 * l + 2)
                used = [(0, nt * NH), (4 * NH, 4 * NKV)] if nt < 4 else [(0, 4 * NH + 4 * NKV)]
                for first, width in used:
                    ins = nc.scalar.activation(ss[:, first:first + width], ss[:, first:first + width], ACT.Sqrt, scale=1.0 / HD, bias=eps_t[:, 0:1])
                ins.then_inc(qk_std, 1)
                phase("ag_b", l, e_ag("ag_b"))

                for g, (kind, t, a) in enumerate(turn_groups(l)):
                    act.wait_ge(turn_done, turn_base(l) + g + 1)
                    dst = q_fm[:, 4 * a:4 * a + 4, t * P:(t + 1) * P] if kind == "q" else k_fm[:, :, t * P:(t + 1) * P]
                    nc.scalar.activation(dst, ps[:, 6 + g % 2, :].rearrange("p (b c) -> p b c", b=4), ACT.Copy).then_inc(turn_copied, 1)

                U = steps(l)
                with act.Fori(0, HP // 2) as r:
                    g0 = r * (2 * U) + step_base(l)
                    for w in range(-1, 2 * U + 1):
                        if w + 1 < 2 * U:
                            e = w + 1
                            K = len(step(l, e % U)[2]) * P
                            act.wait_ge(nbias_done, g0 + (e + 1))
                            act.wait_ge(pt_done, g0 + max(e - 3, 0) + 1)
                            nc.scalar.activation(prob[:, e % 4, 0:K], ps[:, 2 + e % 4, 0:K], ACT.Exp, bias=nbias[:, e % 4:e % 4 + 1],
                                                 accum_out=rowsum[:, e % 4:e % 4 + 1]).then_inc(exp_done, 1)
                        if 0 <= w < 2 * U:
                            K = len(step(l, w % U)[2]) * P
                            act.wait_ge(rinv_done, g0 + (w + 1))
                            nc.scalar.activation(prob[:, w % 4, 0:K], prob[:, w % 4, 0:K], ACT.Copy, scale=rinv[:, w % 2:w % 2 + 1]).then_inc(prob_done, 1)
                        if w >= 1:
                            v = w - 1
                            nb = len(step(l, v % U)[2])
                            act.wait_ge(pt_done, g0 + (v + 1) + 1)
                            act.wait_ge(pv_done, g0 + max(v - 1, 0) + 1)
                            nc.scalar.activation(prob_t[:, v % 2, 0:nb, :], ps[:, 6 + v % 2, 0:nb * P].rearrange("p (b c) -> p b c", b=nb),
                                                 ACT.Copy).then_inc(pt_copied, 1)
                        if w == U + 3:
                            act.wait_ge(pv_done, g0 + U + 1)
                            nc.scalar.activation(o_hi[:, ds(r * 2, 1), 0:T], ps[:, 0:1, 0:T], ACT.Copy).then_inc(o_hi_done, 1)
                    act.wait_ge(pv_done, g0 + 2 * U + 1)
                    nc.scalar.activation(o_hi[:, ds(r * 2 + 1, 1), 0:T], ps[:, 1:2, 0:T], ACT.Copy).then_inc(o_hi_done, 1)

                def e_ga(i, n, s):
                    act.wait_ge(mm_done, n + 1)
                    act.wait_ge(sig_used, i * 2 + (4 * l + s) + 1)
                    nc.scalar.activation(sig[:, :, 0:T], ps[:, 2 * s:2 * s + 2, 0:T], ACT.Sigmoid).then_inc(evac[s], 1)

                def e_gc(i, n, s):
                    act.wait_ge(mm_done, n + 1)
                    nc.scalar.activation(gate_c[:, ds(i * 4 + 2 * s, 2), 0:T], ps[:, 2 * s:2 * s + 2, 0:T], ACT.Sigmoid).then_inc(evac[s], 1)

                phase("attn_o", l, none)
                phase("ga", l, e_ga)
                phase("gc", l, e_gc, 0, 1)
                for k in range(KT):
                    act.wait_ge(cent_done, l * KT + k + 1)
                    nc.scalar.activation(conv_sq[:, k, 0:T], conv[:, k, 0:T], ACT.Square).then_inc(csq_done, 1)
                phase("gc", l, e_gc, 1, 2)
                load_sqrt()
                act.wait_ge(var_done, l + 1)
                nc.scalar.activation(col[:, 0:nt], ps[:, 7, 0:nt], ACT.Sqrt, bias=eps_t[:, 0:1]).then_inc(cstd_done, 1)
                for k in range(KT):
                    act.wait_ge(cunit_done, l * KT + k + 1)
                    own.link(nc.scalar.activation(conv[:, k, 0:T], conv[:, k, 0:T], ACT.Silu,
                                                  bias=vecs[:, 4, l, k:k + 1], scale=vecs[:, 3, l, k:k + 1]))
                    nc.scalar.activation(z_hi[:, k, 0:T], conv[:, k, 0:T], ACT.Copy).then_inc(z_hi_done, 1)
                def e_co(i, n, s):
                    act.wait_ge(merged_done, i * 2 + (4 * l + s + 1) + 1)
                    nc.scalar.activation(m_hi[:, ds(i * 4 + 2 * s, 2), 0:T], merged[:, ds(i * 4 + 2 * s, 2), 0:T], ACT.Copy).then_inc(m_hi_done, 1)

                phase("conv_o", l, e_co)

                def e_sq(i, n, s):
                    act.wait_ge(evac[s], i + (BASE["w_out", l] // 2 + 1))
                    k = ds(i * 4 + 2 * s, 2)
                    nc.scalar.activation(ff_normed[:, k, 0:T], x[:, k, 0:T], ACT.Square).then_inc(sq_done, 2)

                phase("w_out", l, e_sq)
                norm(2 * l + 1, l, T, 3, ff_normed)

                if l % 2 == 0:
                    def e_up(i, n, s):
                        act.wait_ge(mm_done, n + 1)
                        if s == 0:
                            act.wait_ge(gu_ready, i + 1)
                            nc.scalar.activation(ff_silu[:], ps[:, 0:2, :], ACT.Silu).then_inc(evac[0], 1)
                        else:
                            act.wait_ge(evac[1], i + (BASE["ffn_up", l] // 2 + 1))
                            nc.scalar.activation(gu_hi[:, ds(i * 2, 2), :], ff_silu[:], ACT.Copy).then_inc(gu_hi_done, 1)
                    phase("ffn_up", l, e_up)
                    phase("ffn_down", l, none)

            act.wait_ge(moe_consts, 16 * 5)
            nc.scalar.activation(wr_hi[:], wr[:], ACT.Copy).then_inc(wr_hi_done, 1)
            for g in range(8):
                act.wait_ge(tok_turned, g + 1)
                nc.scalar.activation((t_hi if g < 4 else t_lo)[:, g // 2 % 2, g % 2 * 512:(g % 2 + 1) * 512], ps[:, 6 + g % 2, :],
                                     ACT.Copy).then_inc(tok_copied, 1)
            act.wait_ge(top_ready, 1)
            nc.scalar.activation(two[:, :, 2:3], two[:, :, 4:5], ACT.Exp).then_inc(top_exp, 1)

            def moe_split(n, h, j, slot_):
                act.wait_ge(raw_loaded[slot_], moe_loads(h, slot_, j if isinstance(j, int) else slot_))
                act.wait_ge(mm_done, n + (j - (MOE_PARTS - 1)))
                nc.scalar.activation(moe_parts(slot_)[0], moe_slot(slot_), ACT.Copy).then_inc(hi_done, 1)

            def copy_sent(v):
                act.wait_ge(sent, v + 1)
                for a in range(2):
                    nc.scalar.activation(xe_hi[:, 4 * a:4 * a + 4, :], ps[:, 3 + a, :].rearrange("p (b c) -> p b c", b=4), ACT.Copy).then_inc(xe_hi_done, 1)

            def later_split(nn, hc, j):
                slot_ = (j + 4) % MOE_RAW
                act.wait_ge(raw_loaded[slot_], hc * 16 if j < 2 else moe_loads(hc, slot_, 0))
                act.wait_ge(mm_done, nn + (j - (MOE_PARTS - 1)))
                nc.scalar.activation(moe_parts(slot_)[0], moe_slot(slot_), ACT.Copy).then_inc(hi_done, 1)

            def copy_rows(v):
                act.wait_ge(mm_done, v * MOE_N + DENSE_CHUNKS)
                act.wait_ge(y_zeroed, v + 1)
                act.wait_ge(back_done, v * 4 + 1)
                for a in range(2):
                    nc.scalar.activation(y_rows[:, a * 512:(a + 1) * 512], ps[:, 6 + a, :], ACT.Copy).then_inc(y_copied, 1)

            def silu(h, n):
                act.wait_ge(mm_done, n)
                act.wait_ge(hid_done, h + 1)
                nc.scalar.activation(e_silu[:], ps[:, 0, :], ACT.Silu).then_inc(silu_done, 1)

            def turned(h):
                act.wait_ge(hid_turned, h + 1 + 1)
                nc.scalar.activation(hu_hi[:], ps[:, 2, :].rearrange("p (b c) -> p b c", b=4), ACT.Copy).then_inc(hu_hi_done, 1)

            def expert(q):
                n = q * MOE_N + DENSE_CHUNKS
                h = q * NC
                moe_split(n, h, 0, 0)
                copy_sent(q)
                moe_split(n, h, 1, 1)
                moe_split(n, h, 2, 2)
                copy_rows(q)
                moe_split(n, h, 3, 3)
                silu(h, n + 2)
                with act.Fori(1, NC) as c:
                    nn = n + c * 6 - 2
                    hc = h + c
                    later_split(nn, hc, 0)
                    later_split(nn, hc, 1)
                    turned(hc - 1)
                    later_split(nn, hc, 2)
                    later_split(nn, hc, 3)
                    later_split(nn, hc, 4)
                    silu(hc, nn + 2)
                    later_split(nn, hc, 5)
                moe_split(n, h, MOE_N - 2, 4)
                moe_split(n, h, MOE_N - 1, 5)
                turned(h + (NC - 1))
                act.wait_ge(put_turned, q + 1 + 1)
                nc.scalar.activation(put[:], ps[:, 1, 0:2 * P].rearrange("p (t c) -> p t c", t=2), ACT.Copy).then_inc(put_copied, 1)

            with act.Fori(0, NE) as q:
                expert(q)
            act.wait_ge(route_ready, 1)
            with act.Fori(0, FULL) as f:
                used = act.value_load(full_i[0:1, 1, ds(f, 1)], min_val=0, max_val=1)
                with act.If(used > 0):
                    expert(f + NE)
                with act.Else():
                    act.nop()
            copy_rows(act.value_load(full_n[0:1, 0:1], min_val=0, max_val=FULL) + NE)

            act.wait_ge(x_final, 1)
            squares(ff_normed, x, SEQ, sq_done)
            root(2 * DEPTH, SEQ)

        @block.vector
        def _(dve):
            own = Chain(dve, dve_own)
            V = nc.vector
            for s_ in (sig_used, merged_done, gu_ready, hid_done, back_added):
                dve.nop().then_inc(s_, 1)

            def split(n, s):
                dve.wait_ge(hi_done, n + 1)
                V.tensor_tensor(w_lo[:, s, :], raw[:, s, :], w_hi[:, s, :].bitcast(f32), ALU.subtract).then_inc(lo_done, 1)

            def phase(name, l, evacuate, start=0, stop=None, between=None, count=0):
                n0, pairs = BASE[name, l], COUNT[name, l] // 2
                stop = pairs if stop is None else stop
                last = (name, l) == LAST_PHASE and stop == pairs
                by = 2 if name == "ffn_down" else 1

                def body(i, more=True):
                    for b in range(by):
                        n = n0 + 2 * by * i + 2 * b
                        split(n + 1, 1)
                        evacuate(i * by + b, n, 0, b)
                        if between:
                            between(i, 0)
                        if more:
                            split(n + 2, 0)
                        evacuate(i * by + b, n + 1, 1, b)
                        j = ada_number(name, l, i)
                        if j is not None:
                            ada_add(j)
                        if between:
                            between(i, 1)
                if by == 1 and stop - start == 1 and not last:
                    body(start)
                elif stop // by - last > start:
                    with own.loop(start, stop // by - last, count) as i:
                        body(i)
                if last:
                    body(stop - 1, more=False)

            def none(i, n, s, b):
                pass

            dve.wait_ge(consts_loaded, 7 * 16)

            def ada_add(j):
                dve.wait_ge(ada_turned, j + 1)
                V.tensor_tensor(mods[:, ds(j * 2, 2), :], ps[:, 6, 0:4].rearrange("p (t c) -> p t c", c=2),
                                b_ada[:, ds(j * 2, 2)].unsqueeze(2).to_broadcast([P, 2, 2]), ALU.add).then_inc(mods_done, 1)

            acc = diag.rearrange("p t c -> p (t c)")

            def add_squares(buf, T, a, b, nrm):
                for k in range(max(a, 1), b):
                    dve.wait_ge(sq_done, nrm * KT + k + 1)
                    own.wait()
                    ins = V.tensor_tensor(acc[:, 0:T], buf[:, 0, 0:T] if k == 1 else acc[:, 0:T], buf[:, k, 0:T], ALU.add)
                    ins.then_inc(sum_done, 1) if k == KT - 1 else own.step(ins)

            def make_diag(done, value, T):
                dve.wait_ge(done, value)
                own.link(V.reciprocal(col[:, 0:T // P], col[:, 0:T // P]))
                return V.tensor_tensor(diag[:, 0:T // P, :], ident[:].unsqueeze(1).to_broadcast([P, T // P, P]),
                                       col[:, 0:T // P].unsqueeze(2).to_broadcast([P, T // P, P]), ALU.mult)

            def norm(nrm, l, T, which, scale, buf):
                if scale == 1:
                    add_squares(buf, T, 0, KT, nrm)
                if nrm == 0:
                    for j in range(ADA_FIRST // 2, ADA_FIRST - 2):
                        ada_add(j)
                make_diag(std_done, nrm + 1, T).then_inc(diag_done, 1)
                if nrm == 0:
                    for j in range(ADA_FIRST - 2, ADA_FIRST):
                        ada_add(j)
                    split(0, 0)
                row = (l * NMOD + scale) * KT
                dve.wait_ge(mods_done, l * ADA + (ADA_FIRST if scale == 1 else ADA))
                own.step(V.scalar_tensor_tensor(out=scale1[:], in0=mods[:, row:row + KT, :], scalar=1.0,
                                                in1=vecs[:, which, l, :].unsqueeze(2).to_broadcast([P, KT, 2]), op0=ALU.add, op1=ALU.mult))
                dve.wait_ge(spread_done, nrm + 1)
                for k in range(KT + 2):
                    if k < KT:
                        V.tensor_tensor(buf[:, k, 0:T], x[:, k, 0:T], ps[:, norm_bank(nrm), 0:T], ALU.mult).then_inc(unit_done, 1)
                    if k >= 2:
                        b = k - 2
                        dve.wait_ge(h_hi_done, nrm * KT + b + 1)
                        V.tensor_tensor(h_lo[:, b, 0:T], buf[:, b, 0:T], h_hi[:, b, 0:T].bitcast(f32), ALU.subtract).then_inc(h_ready, 1)

            for l in range(DEPTH):
                T = tokens(l)
                nt = T // P
                S = T // SEQ

                if l == 0:
                    for j in range(ADA_FIRST // 2):
                        ada_add(j)
                norm(2 * l, l, TOK, 0, 1, normed)
                dve.wait_ge(h_ready, (2 * l + 1) * KT)
                for g in range(S):
                    V.memset(zpad[:, :, g, 0:PAD], 0.0)
                    own.step(V.memset(zpad[:, :, g, PAD + SEQ:ZW], 0.0))
                def e_ag(name):
                    def run(i, n, s, b):
                        if s == 1:
                            dve.wait_ge(mm_done, n + 1)
                            dve.wait_ge(evac[0], i + (BASE[name, l] // 2 + 1))
                            for a in range(2):
                                k = i * 2 + (a + (KT // 2 if name == "ag_b" else 0))
                                ins = V.tensor_tensor(zpad[:, ds(k, 1), 0:S, PAD:PAD + SEQ].rearrange("p o g t -> p (o g) t"),
                                                      ps[:, 2 + a, 0:T].rearrange("p (g t) -> p g t", g=S),
                                                      sig[:, a, 0:T].rearrange("p (g t) -> p g t", g=S), ALU.mult)
                            ins.then_inc(evac[1], 1)
                    return run

                def sum_squares(value, at_tmp, at_ss, n):
                    dve.wait_ge(qk_sq, value)
                    V.tensor_reduce(ss[:, at_ss:at_ss + n], qk_tmp[:, at_tmp:at_tmp + n * HD].rearrange("p (h d) -> p h d", d=HD), AX.X, ALU.add).then_inc(qk_ss, 1)

                def head_norm(tiles, nh, at_ss, v, gain, factor):
                    for t in tiles:
                        own.step(V.tensor_tensor(v(t), v(t), ss[:, at_ss + t * nh:at_ss + (t + 1) * nh].unsqueeze(2).to_broadcast([P, nh, HD]), ALU.mult))
                    for t in tiles:
                        own.wait(back=len(tiles) - 1)
                        own.step(V.scalar_tensor_tensor(out=v(t), in0=v(t), scalar=factor, in1=gain.unsqueeze(1).to_broadcast([P, nh, HD]),
                                                        op0=ALU.mult, op1=ALU.mult))
                    size = nh * HALF
                    for t in tiles:
                        if t >= SEQ // P:
                            continue
                        tmp = [qk_tmp[:, a * size:(a + 1) * size].rearrange("p (h d) -> p h d", h=nh) for a in range(4)]
                        x1, x2 = v(t)[:, :, 0:HALF], v(t)[:, :, HALF:HD]
                        cos_, sin_ = (rope[:, a, t, :].unsqueeze(1).to_broadcast([P, nh, HALF]) for a in range(2))
                        own.wait()
                        own.step(V.tensor_tensor(tmp[0], x1, cos_, ALU.mult))
                        own.step(V.tensor_tensor(tmp[1], x2, sin_, ALU.mult))
                        own.step(V.tensor_tensor(tmp[2], x1, sin_, ALU.mult))
                        own.step(V.tensor_tensor(tmp[3], x2, cos_, ALU.mult))
                        own.wait()
                        own.step(V.tensor_tensor(x1, tmp[0], tmp[1], ALU.subtract))
                        own.step(V.tensor_tensor(x2, tmp[2], tmp[3], ALU.add))

                def q_view(t):
                    return q_tm[:, t, :].rearrange("p (h d) -> p h d", d=HD)

                def k_view(t):
                    return kv_tm[:, t, 0:KVW].rearrange("p (h d) -> p h d", d=HD)

                def taps(*runs):
                    k0, last = own.k, {}
                    for tap in range(max(b - a for _, a, b in runs)):
                        for m, (k, a, b) in enumerate(runs):
                            if a + tap < b:
                                out = conv[:, ds(k, 1), 0:T].rearrange("p o (g t) -> p (o g) t", g=S)
                                z = zpad[:, ds(k, 1), 0:S, a + tap:a + tap + SEQ].rearrange("p o g t -> p (o g) t")
                                wt = dw[:, l, ds(k, 1), a + tap]
                                if a + tap == 0:
                                    own.step(V.tensor_scalar(out, z, wt, vecs[:, 2, l, ds(k, 1)], ALU.mult, ALU.add))
                                else:
                                    own.wait(back=own.k - last.get(m, k0))
                                    own.step(V.scalar_tensor_tensor(out=out, in0=z, scalar=wt, in1=out, op0=ALU.mult, op1=ALU.add))
                                last[m] = own.k

                def pair_taps(k, s, a, mid, b):
                    return [(k, a, mid) if s == 0 else (k, mid, b), (k + 1, a, mid) if s == 0 else (k + 1, mid, b)]

                phase("ag_a", l, e_ag("ag_a"))
                dve.wait_ge(evac[1], BASE["q", l] // 2)
                phase("q", l, none, between=lambda i, s: taps(*pair_taps(i * 2, s, 0, TAPS_Q // 2, TAPS_Q)), count=2 * TAPS_Q)
                sum_squares(2 * l + 1, 0, 0, nt * NH)
                phase("kv", l, none, between=lambda i, s: taps(*((k, TAPS_Q, TAPS_KV) for k in (2 * s, 2 * s + 1))), count=4 * (TAPS_KV - TAPS_Q))
                sum_squares(2 * l + 2, K_SQ, 4 * NH, 4 * NKV)
                dve.wait_ge(qk_std, l + 1)
                own.link(V.reciprocal(ss[:, 0:nt * NH], ss[:, 0:nt * NH]))
                own.link(V.reciprocal(ss[:, 4 * NH:4 * NH + 4 * NKV], ss[:, 4 * NH:4 * NH + 4 * NKV]))

                def norm_heads(i, s):
                    if (i, s) in ((0, 0), (0, 1)):
                        head_norm([s], NH, 0, q_view, qk_gain[:, 0, l, :], HD ** -0.5)
                    elif s == 0:
                        head_norm(range(TOK // P), NKV, 4 * NH, k_view, qk_gain[:, 1, l, :], 1.0)
                        own.wait()
                        for t in range(TOK // P):
                            for a in range(2):
                                ins = V.tensor_copy(k_dup[:, t, :, a, :], k_view(t))
                        own.step(ins)
                        head_norm(range(SEQ // P, nt), NH, 0, q_view, qk_gain[:, 0, l, :], HD ** -0.5)

                for i in range(COUNT["ag_b", l] // 2):
                    phase("ag_b", l, e_ag("ag_b"), i, i + 1, between=norm_heads)
                own.wait()
                V.memset(rinv[:], 0.0).then_inc(qk_ready, 1)

                U = steps(l)
                dve.wait_ge(evac[1], (BASE["ag_b", l] + COUNT["ag_b", l]) // 2)
                with own.loop(0, HP // 2, TAPS_ATT) as r:
                    g0 = r * (2 * U) + step_base(l)

                    def top(w):
                        K = len(step(l, w % U)[2]) * P
                        dve.wait_ge(score_done, g0 + (w + 1))
                        V.tensor_reduce(nbias[:, w % 4:w % 4 + 1], ps[:, 2 + w % 4, 0:K], AX.X, ALU.max, negate=True).then_inc(nbias_done, 1)

                    def lower(a):
                        dve.wait_ge(o_hi_done, r * 2 + (HP * l + a + 1))
                        V.tensor_tensor(o_lo[:, ds(r * 2 + a, 1), 0:T], ps[:, a:a + 1, 0:T], o_hi[:, ds(r * 2 + a, 1), 0:T].bitcast(f32),
                                        ALU.subtract).then_inc(o_lo_done, 1)

                    def att_taps(w, spot):
                        a, b = (TAPS_ATT * (2 * w + spot + c) // (4 * U) for c in (0, 1))
                        if b > a:
                            taps((r + KT // 2, a, b))

                    top(0)
                    top(1)
                    for w in range(2 * U):
                        if w + 2 < 2 * U:
                            top(w + 2)
                        att_taps(w, 0)
                        dve.wait_ge(exp_done, g0 + (w + 1))
                        V.reciprocal(rinv[:, w % 2:w % 2 + 1], rowsum[:, w % 4:w % 4 + 1]).then_inc(rinv_done, 1)
                        att_taps(w, 1)
                        if w == min(U + 4, 2 * U - 1):
                            lower(0)
                    lower(1)

                def e_ao(i, n, s, b):
                    dve.wait_ge(mm_done, n + 1)
                    V.tensor_copy(merged[:, ds(i * 4 + 2 * s, 2), 0:T], ps[:, 2 * s:2 * s + 2, 0:T]).then_inc(evac[s], 1)

                def e_ga(i, n, s, b):
                    dve.wait_ge(evac[s], i + (BASE["ga", l] // 2 + 1))
                    m = merged[:, ds(i * 4 + 2 * s, 2), 0:T]
                    V.tensor_tensor(m, m, sig[:, :, 0:T], ALU.mult).then_inc(sig_used, 1)

                def e_co(i, n, s, b):
                    dve.wait_ge(mm_done, n + 1)
                    m = merged[:, ds(i * 4 + 2 * s, 2), 0:T]
                    dve.wait_ge(merged_done, i * 2 + (4 * l + s) + 1)
                    V.tensor_tensor(sig[:, :, 0:T], ps[:, 2 * s:2 * s + 2, 0:T], gate_c[:, ds(i * 4 + 2 * s, 2), 0:T], ALU.mult).then_inc(evac[s], 1)
                    dve.wait_ge(evac[s], i + (BASE["conv_o", l] // 2 + 1))
                    V.tensor_tensor(m, m, sig[:, :, 0:T], ALU.add).then_inc(merged_done, 1)
                    dve.wait_ge(m_hi_done, i * 2 + (4 * l + s + 1))
                    V.tensor_tensor(m_lo[:, ds(i * 4 + 2 * s, 2), 0:T], m, m_hi[:, ds(i * 4 + 2 * s, 2), 0:T].bitcast(f32), ALU.subtract).then_inc(m_ready, 1)

                def add_to_x(which, k, bank):
                    for g in range(S):
                        xs = x[:, ds(k, 1), g * SEQ:(g + 1) * SEQ]
                        ins = V.scalar_tensor_tensor(out=xs, in0=ps[:, bank:bank + 1, g * SEQ:(g + 1) * SEQ],
                                                     scalar=mods[:, ds(k + (l * NMOD + which) * KT, 1), g], in1=xs, op0=ALU.mult, op1=ALU.add)
                    return ins

                def e_out(i, n, s, b):
                    dve.wait_ge(mm_done, n + 1)
                    for a in range(2):
                        ins = add_to_x(2, i * 4 + (2 * s + a), 2 * s + a)
                    ins.then_inc(evac[s], 1)
                    if i or s:
                        add_squares(ff_normed, T, 4 * i + 2 * s - 2, 4 * i + 2 * s, 2 * l + 1)

                def taps_ao(i, s):
                    taps(*pair_taps(i * 2, s, TAPS_KV, TAPS_AO - 2, TAPS_AO), *pair_taps(i * 2 + KT // 2, s, TAPS_ATT, TAPS_ATT + 4, TAPS_AO2))

                def taps_ga(i, s):
                    taps(*pair_taps(i * 2, s, TAPS_AO, TAPS - 3, TAPS), *pair_taps(i * 2 + KT // 2, s, TAPS_AO2, TAPS - 4, TAPS))

                phase("attn_o", l, e_ao, between=taps_ao, count=2 * (TAPS_AO - TAPS_KV + TAPS_AO2 - TAPS_ATT))
                phase("ga", l, e_ga, between=taps_ga, count=2 * (TAPS - TAPS_AO + TAPS - TAPS_AO2))
                own.wait()
                V.tensor_reduce(acc[:, 0:T], conv[:, :, 0:T].rearrange("p k t -> p t k"), AX.X, ALU.add).then_inc(csum_done, 1)
                phase("gc", l, none, 0, 1)
                dve.wait_ge(csum_spread, l + 1)
                for k in range(KT):
                    V.scalar_tensor_tensor(out=conv[:, k, 0:T], in0=ps[:, 5, 0:T], scalar=-1.0 / D, in1=conv[:, k, 0:T],
                                           op0=ALU.mult, op1=ALU.add).then_inc(cent_done, 1)
                for k in range(1, KT):
                    dve.wait_ge(csq_done, l * KT + k + 1)
                    own.wait()
                    ins = V.tensor_tensor(acc[:, 0:T], conv_sq[:, 0, 0:T] if k == 1 else acc[:, 0:T], conv_sq[:, k, 0:T], ALU.add)
                    ins.then_inc(csq_sum, 1) if k == KT - 1 else own.step(ins)
                phase("gc", l, none, 1, 2)
                make_diag(cstd_done, l + 1, T).then_inc(var_diag, 1)
                dve.wait_ge(var_spread, l + 1)
                for k in range(KT + 2):
                    if k < KT:
                        V.tensor_tensor(conv[:, k, 0:T], conv[:, k, 0:T], ps[:, 7, 0:T], ALU.mult).then_inc(cunit_done, 1)
                    if k >= 2:
                        b = k - 2
                        dve.wait_ge(z_hi_done, l * KT + b + 1)
                        V.tensor_tensor(z_lo[:, b, 0:T], conv[:, b, 0:T], z_hi[:, b, 0:T].bitcast(f32), ALU.subtract).then_inc(z_ready, 1)
                phase("conv_o", l, e_co)
                phase("w_out", l, e_out, 0, 1)
                phase("w_out", l, e_out, 1, 2)
                add_squares(ff_normed, T, KT - 2, KT, 2 * l + 1)
                norm(2 * l + 1, l, T, 1, 4, ff_normed)

                if l % 2 == 0:
                    def e_up(i, n, s, b):
                        if s == 1:
                            dve.wait_ge(mm_done, n + 1)
                            dve.wait_ge(evac[0], i + (BASE["ffn_up", l] // 2 + 1))
                            V.tensor_tensor(ff_silu[:], ps[:, 2:4, :], ff_silu[:], ALU.mult).then_inc(evac[1], 1)
                            dve.wait_ge(gu_hi_done, i + 1)
                            V.tensor_tensor(gu_lo[:, ds(i * 2, 2), :], ff_silu[:], gu_hi[:, ds(i * 2, 2), :].bitcast(f32), ALU.subtract).then_inc(gu_ready, 1)

                    def e_down(i, n, s, b):
                        if s == 1:
                            dve.wait_ge(mm_done, n + 1)
                            add_to_x(5, i, 2 * b).then_inc(evac[b], 2)

                    phase("ffn_up", l, e_up)
                    phase("ffn_down", l, e_down)

            dve.wait_ge(wr_hi_done, 1)
            V.tensor_tensor(wr_lo[:], wr[:], wr_hi[:].bitcast(f32), ALU.subtract).then_inc(wr_ready, 1)
            V.memset(zeros[:], 0.0)
            V.memset(slot[:], -1.0)
            V.memset(put[:], 0.0).then_inc(moe_fills, 1)
            dve.wait_ge(moe_fills, 1)
            V.tensor_copy(zero_r[:], zeros[:]).then_inc(moe_fills, 1)
            dve.wait_ge(logit_done, 1)
            own.link(V.tensor_tensor(logit[:], ps[:, 5, 0:2 * NE].rearrange("p (t e) -> p t e", t=2),
                                     b_router[:].unsqueeze(1).to_broadcast([P, 2, NE]), ALU.add))

            def field(a):
                return two[:, :, a:a + 1]

            def wide(a):
                return two[:, :, a:a + 1].to_broadcast([P, 2, NE])

            def best(of, value, index, hot):
                own.link(V.tensor_reduce(field(value), of, AX.X, ALU.max))
                own.link(V.tensor_tensor(tie[:], of, wide(value), ALU.is_equal))
                own.link(V.tensor_tensor(tie[:], tie[:], rank8[:].unsqueeze(1).to_broadcast([P, 2, NE]), ALU.mult))
                own.link(V.tensor_reduce(field(index), tie[:], AX.X, ALU.max))
                own.link(V.tensor_tensor(hot, tie[:], wide(index), ALU.is_equal))

            best(logit[:], 0, 1, top1[:])
            own.link(V.scalar_tensor_tensor(out=rest[:], in0=top1[:], scalar=-3.0e38, in1=logit[:], op0=ALU.mult, op1=ALU.add))
            best(rest[:], 3, 1, top2[:])
            V.tensor_tensor(field(4), field(3), field(0), ALU.subtract).then_inc(top_ready, 1)
            V.tensor_tensor(mask[:], top1[:], top2[:], ALU.add).then_inc(mask_ready, 1)
            dve.wait_ge(top_exp, 1)
            own.link(V.tensor_scalar(field(5), field(2), 1.0, None, ALU.add))
            own.link(V.reciprocal(field(5), field(5)))
            own.link(V.tensor_tensor(field(6), field(5), field(2), ALU.mult))
            own.link(V.tensor_tensor(tie[:], top1[:], wide(5), ALU.mult))
            own.link(V.tensor_tensor(rest[:], top2[:], wide(6), ALU.mult))
            own.link(V.tensor_tensor(gate_at[:, :, 0:NE], tie[:], rest[:], ALU.add))
            def build_pick(v):
                dve.wait_ge(sent, v)
                for t in range(2):
                    ins = V.tensor_scalar(pick[:, t, :], iota[:], slot[:, t, ds(v, 1)], None, ALU.is_equal)
                ins.then_inc(pick_ready, 1)

            dve.wait_ge(pos_done, 1)
            own.link(V.scalar_tensor_tensor(out=tie[:], in0=ps[:, 4, 0:2 * NE].rearrange("p (t e) -> p t e", t=2), scalar=1.0,
                                            in1=mask[:], op0=ALU.add, op1=ALU.mult))
            own.link(V.tensor_scalar(slot[:, :, 0:NE], tie[:], -1.0, None, ALU.add))
            own.step(V.tensor_scalar(over[:, 0, :], ps[:, 4, 2 * NE:3 * NE], float(P), None, ALU.is_gt))
            build_pick(0)
            own.link(V.memset(over[:, 1, 0:1], 0.0))
            for e in range(1, NE):
                own.link(V.tensor_tensor(over[:, 1, e:e + 1], over[:, 1, e - 1:e], over[:, 0, e - 1:e], ALU.add))
            own.link(V.tensor_tensor(full_sel[:], over[:, 1:2, :].to_broadcast([P, FULL, NE]), iota[:, 0:FULL].unsqueeze(2).to_broadcast([P, FULL, NE]), ALU.is_equal))
            own.link(V.tensor_tensor(full_sel[:], full_sel[:], over[:, 0:1, :].to_broadcast([P, FULL, NE]), ALU.mult))
            own.link(V.tensor_tensor(full_sel[:], full_sel[:], rank8[:].unsqueeze(1).to_broadcast([P, FULL, NE]), ALU.mult))
            own.link(V.tensor_reduce(full_e[:, 0:FULL], full_sel[:], AX.X, ALU.max))
            own.link(V.tensor_scalar(used_f[:, 0:FULL], full_e[:, 0:FULL], 1.0, None, ALU.min))
            own.link(V.tensor_copy(full_i[:, 1, 0:FULL], used_f[:, 0:FULL]))
            own.link(V.tensor_scalar(full_e[:, 0:FULL], full_e[:, 0:FULL], -1.0, float(NE), ALU.mult, ALU.add))
            own.link(V.tensor_scalar(full_i[:, 0, 0:FULL], full_e[:, 0:FULL], float(NE - 1), None, ALU.min))
            for f in range(FULL):
                e = dve.value_load(full_i[0:1, 0, f:f + 1], min_val=0, max_val=NE - 1)
                own.link(V.tensor_scalar(slot[:, :, NE + f:NE + f + 1], slot[:, :, ds(e, 1)], float(1 - P), used_f[:, f:f + 1], ALU.add, ALU.mult))
                own.step(V.tensor_scalar(slot[:, :, NE + f:NE + f + 1], slot[:, :, NE + f:NE + f + 1], -1.0, None, ALU.add))
                own.step(V.tensor_copy(gate_at[:, :, NE + f:NE + f + 1], gate_at[:, :, ds(e, 1)]))
            own.link(V.tensor_reduce(most[:], used_f[:, 0:FULL], AX.X, ALU.add))
            V.tensor_copy(full_n[:], most[:]).then_inc(route_ready, 1)

            def moe_split(n, jn, slot_):
                dve.wait_ge(hi_done, n + (jn + 1))
                hi, lo = moe_parts(slot_)
                V.tensor_tensor(lo, moe_slot(slot_), hi.bitcast(f32), ALU.subtract).then_inc(lo_done, 1)

            def copy_sent(v):
                dve.wait_ge(sent, v + 1)
                for a, bank in ((0, 5), (1, 0)):
                    V.tensor_copy(xe_lo[:, 4 * a:4 * a + 4, :], ps[:, bank, :].rearrange("p (b c) -> p b c", b=4)).then_inc(xe_lo_done, 1)

            def hidden(h, n):
                dve.wait_ge(mm_done, n)
                dve.wait_ge(silu_done, h + 1)
                dve.wait_ge(hid_turned, h + 1)
                V.tensor_tensor(e_hid[:], ps[:, 1, :], e_silu[:], ALU.mult).then_inc(hid_done, 1)

            def turned(h):
                dve.wait_ge(hu_hi_done, h + 1)
                V.tensor_tensor(hu_lo[:], ps[:, 2, :].rearrange("p (b c) -> p b c", b=4), hu_hi[:].bitcast(f32), ALU.subtract).then_inc(hu_lo_done, 1)

            def add_back(v):
                dve.wait_ge(back_added, v * 4 + 1)
                for a in range(4):
                    dve.wait_ge(back_done, v * 4 + (a + 1) + 1)
                    for b in range(2):
                        k = 2 * a + b
                        ins = V.scalar_tensor_tensor(out=x[:, k, 0:SEQ], in0=ps[:, 2 + a, b * SEQ:(b + 1) * SEQ],
                                                     scalar=mods[:, ((DEPTH - 1) * NMOD + 5) * KT + k, 0:1], in1=x[:, k, 0:SEQ], op0=ALU.mult, op1=ALU.add)
                    ins.then_inc(back_added, 1)

            def expert(q):
                n = q * MOE_N + DENSE_CHUNKS
                h = q * NC
                moe_split(n, 0, 0)
                copy_sent(q)
                moe_split(n, 1, 1)
                dve.wait_ge(put_turned, q + 1)
                for t in range(2):
                    ins = V.tensor_scalar(pick_g[:, t, :], iota[:], slot[:, t, ds(q, 1)], gate_at[:, t, ds(q, 1)],
                                          ALU.is_equal, ALU.mult)
                ins.then_inc(pick_g_ready, 1)
                build_pick(q + 1)
                moe_split(n, 2, 2)
                moe_split(n, 3, 3)
                hidden(h, n + 4)

                def round_(c):
                    nn = n + c * 6 - 2
                    hc = h + c
                    moe_split(nn, 0, 4)
                    moe_split(nn, 1, 5)
                    turned(hc - 1)
                    for j in range(2, 6):
                        moe_split(nn, j, j - 2)
                        if j == 4:
                            hidden(hc, nn + 4)

                round_(1)
                add_back(q)
                with dve.Fori(2, NC) as c:
                    round_(c)
                moe_split(n, MOE_N - 2, 4)
                moe_split(n, MOE_N - 1, 5)
                turned(h + (NC - 1))

            with dve.Fori(0, NE) as q:
                expert(q)
            with dve.Fori(0, FULL) as f:
                used = dve.value_load(full_i[0:1, 1, ds(f, 1)], min_val=0, max_val=1)
                with dve.If(used > 0):
                    expert(f + NE)
                with dve.Else():
                    dve.nop()
            add_back(dve.value_load(full_n[0:1, 0:1], min_val=0, max_val=FULL) + NE)
            V.memset(full_e[:], 0.0).then_inc(x_final, 1)

            add_squares(ff_normed, SEQ, 0, KT, 2 * DEPTH)
            make_diag(std_done, 2 * DEPTH + 1, SEQ).then_inc(diag_done, 1)
            dve.wait_ge(spread_done, 2 * DEPTH + 1)
            for k in range(KT):
                V.scalar_tensor_tensor(out=x[:, k, 0:SEQ], in0=x[:, k, 0:SEQ], scalar=g_final[:, k:k + 1], in1=ps[:, 5, 0:SEQ],
                                       op0=ALU.mult, op1=ALU.mult).then_inc(out_ready, 1)

        @block.tensor
        def _(pe):
            mm = nc.tensor.matmul
            for s_ in (pt_done, pv_done, back_done, put_turned, hid_turned):
                pe.nop().then_inc(s_, 1)

            def three(out, parts, first, last):
                for a, (lhs, rhs) in enumerate(parts):
                    ins = mm(out, lhs, rhs, start=first and a == 0, stop=last and a == len(parts) - 1)
                return ins

            def start(n, s, pair):
                pe.wait_ge(lo_done, n + 1)
                pe.wait_ge(evac[s], pair)

            def by_feature(xh, xl, T):
                def run(i, n, s, hi, lo, block_ready=None):
                    for a in range(2):
                        c = slice(a * P, (a + 1) * P)
                        for k in range(KT):
                            if block_ready and s == 0 and a == 0:
                                block_ready(k)
                            ins = three(ps[:, 2 * s + a, 0:T], [(hi[:, k, c], xh[:, k, 0:T]), (hi[:, k, c], xl[:, k, 0:T]),
                                                                (lo[:, k, c], xh[:, k, 0:T])], k == 0, k == KT - 1)
                    return ins
                return run

            def by_token(tiles):
                def run(i, n, s, hi, lo, block_ready=None):
                    for t in range(tiles):
                        r = slice(t * P, (t + 1) * P)
                        out = ps[:, 2 * s + t // 2, t % 2 * CC:(t % 2 + 1) * CC]
                        for k in range(KT):
                            ins = three(out, [(h_hi[:, k, r], hi[:, k, :]), (h_hi[:, k, r], lo[:, k, :]), (h_lo[:, k, r], hi[:, k, :])],
                                        k == 0, k == KT - 1)
                    return ins
                return run

            def phase(name, l, run, start_=0, stop=None, block_ready=None):
                n0, pairs = BASE[name, l], COUNT[name, l] // 2
                stop = pairs if stop is None else stop

                def body(i, **first):
                    n = n0 + 2 * i
                    for s in range(2):
                        start(n + s, s, i + n0 // 2)
                        run(i, n + s, s, as_chunk(name, w_hi[:, s, :]), as_chunk(name, w_lo[:, s, :]), **first).then_inc(mm_done, 1)
                        j = ada_number(name, l, i)
                        if j is not None:
                            (ada_turn if s else ada)(j)
                if block_ready:
                    body(start_, block_ready=block_ready)
                    start_ += 1
                if stop > start_:
                    with pe.Fori(start_, stop) as i:
                        body(i)

            def mean(summed, value, T, bank, done):
                pe.wait_ge(summed, value)
                for t in range(T // P):
                    ins = mm(ps[:, bank, t:t + 1], diag[:, t, :], mean_w[:], start=True, stop=True)
                ins.then_inc(done, 1)

            def spread(made, value, T, bank, done):
                pe.wait_ge(made, value)
                mm(ps[:, bank, 0:T], ones[:], diag[:, 0:T // P, :].rearrange("p t c -> p (t c)"), start=True, stop=True).then_inc(done, 1)

            def waits(sem_, base, blocks=1):
                def block_ready(k):
                    pe.wait_ge(sem_, base + k // blocks + 1)
                return block_ready

            def ada(j, first=False):
                raw_ = (ada_first[:, j % ADA_SLOTS, :] if first else ada_raw[:]).rearrange("p (t c) -> p t c", c=CC)
                if first:
                    pe.wait_ge(ada_first_loaded[j % ADA_SLOTS], (j // ADA_SLOTS + 1) * 16)
                else:
                    pe.wait_ge(ada_loaded, (j - ADA_FIRST) * 16 + 16)
                for k in range(KT):
                    ins = mm(ps[0:2, 4 + (j % 2 if first else 0), 0:CC], cs[:, k, :], raw_[:, k, :], start=k == 0, stop=k == KT - 1)
                ins.then_inc(ada_done, 1)

            def ada_turn(j, b=0):
                pe.wait_ge(ada_copied, j + 1)
                pe.wait_ge(mods_done, j)
                for a in range(2):
                    ins = mm(ps[:, 6, 2 * a:2 * a + 2], ada_row[b][:, a * P:(a + 1) * P], ident[0:2, 0:2], start=True, stop=True)
                ins.then_inc(ada_turned, 1)

            pe.wait_ge(cs_done, 1)
            for j in range(ADA_FIRST):
                ada(j, first=True)
                if j == 1:
                    pe.wait_ge(consts_loaded, 7 * 16)
                if j:
                    ada_turn(j - 1, (j - 1) % 2)
                if j == ADA_FIRST - 2:
                    pe.wait_ge(fills, 3)
                    mean(sum_done, 1, TOK, norm_bank(0), ms_done)
            spread(diag_done, 1, TOK, norm_bank(0), spread_done)
            ada_turn(ADA_FIRST - 1, (ADA_FIRST - 1) % 2)
            for l in range(DEPTH):
                T = tokens(l)
                nt = T // P
                if l:
                    mean(sum_done, 2 * l + 1, TOK, 5, ms_done)

                    spread(diag_done, 2 * l + 1, TOK, 5, spread_done)
                phase("ag_a", l, by_feature(h_hi, h_lo, T), block_ready=waits(h_ready, 2 * l * KT))
                phase("q", l, by_token(nt))
                phase("kv", l, by_token(TOK // P))
                phase("ag_b", l, by_feature(h_hi, h_lo, T))

                pe.wait_ge(qk_ready, l + 1)
                pe.wait_ge(mods_done, ada_number("ag_b", l, 1) + 1)
                for g, (kind, t, a) in enumerate(turn_groups(l)):
                    tg = turn_base(l) + g
                    if tg >= 2:
                        pe.wait_ge(turn_copied, tg - 1)
                    for b in range(4):
                        if kind == "q":
                            block_ = q_tm[:, t, (4 * a + b) * P:(4 * a + b + 1) * P]
                        else:
                            block_ = k_dup[:, t, b, :, :].rearrange("p a d -> p (a d)")
                        ins = nc.tensor.transpose(ps[:, 6 + g % 2, b * P:(b + 1) * P], block_, ident[:])
                    ins.then_inc(turn_done, 1)
                pe.wait_ge(turn_copied, turn_base(l + 1))
                for s in range(2):
                    pe.wait_ge(evac[s], BASE["attn_o", l] // 2)

                U, G0 = steps(l), step_base(l)
                N = HP * U

                def score(g):
                    hp, u = divmod(g, U)
                    h2, t, keys = step(l, u)
                    if G0 + g >= 4:
                        pe.wait_ge(exp_done, G0 + g - 3)
                    r = slice(h2 * HD, (h2 + 1) * HD)
                    mm(ps[:, 2 + g % 4, 0:len(keys) * P], q_fm[r, hp, t * P:(t + 1) * P],
                       k_fm[r, (2 * hp + h2) * NKV // NH, keys[0] * P:TOK], start=True, stop=True).then_inc(score_done, 1)

                def turn(g):
                    _, _, keys = step(l, g % U)
                    pe.wait_ge(prob_done, G0 + g + 1)
                    if G0 + g >= 2:
                        pe.wait_ge(pt_copied, G0 + g - 1)
                    for b in range(len(keys)):
                        ins = nc.tensor.transpose(ps[:, 6 + g % 2, b * P:(b + 1) * P], prob[:, g % 4, b * P:(b + 1) * P], ident[:])
                    ins.then_inc(pt_done, 1)

                def weigh(g):
                    hp, u = divmod(g, U)
                    h2, t, keys = step(l, u)
                    kv = (2 * hp + h2) * NKV // NH
                    pe.wait_ge(pt_copied, G0 + g + 1)
                    if u == 0 and hp >= 2:
                        pe.wait_ge(o_lo_done, l * HP + hp - 1)
                    for b, kb in enumerate(keys):
                        ins = mm(ps[h2 * HD:(h2 + 1) * HD, hp % 2, t * P:(t + 1) * P], kv_tm[:, kb, KVW + kv * HD:KVW + (kv + 1) * HD],
                                 prob_t[:, g % 2, b, :], start=b == 0, stop=b == len(keys) - 1)
                    ins.then_inc(pv_done, 1)

                for g in range(3):
                    score(g)
                for g in range(N):
                    if g + 3 < N:
                        score(g + 3)
                    turn(g)
                    if g % (2 * U):
                        weigh(g - 1)
                    if g % (2 * U) == 2 * U - 1:
                        weigh(g)

                pe.wait_ge(o_lo_done, (l + 1) * HP)
                phase("attn_o", l, by_feature(o_hi, o_lo, T))
                phase("ga", l, by_feature(h_hi, h_lo, T))
                phase("gc", l, by_feature(h_hi, h_lo, T), 0, 1)
                spread(csum_done, l + 1, T, 5, csum_spread)
                phase("gc", l, by_feature(h_hi, h_lo, T), 1, 2)
                mean(csq_sum, l + 1, T, 7, var_done)
                spread(var_diag, l + 1, T, 7, var_spread)
                phase("conv_o", l, by_feature(z_hi, z_lo, T), block_ready=waits(z_ready, l * KT))
                phase("w_out", l, by_feature(m_hi, m_lo, T), block_ready=waits(m_ready, l * KT // 2, 2))

                mean(sum_done, 2 * l + 2, T, 5, ms_done)
                spread(diag_done, 2 * l + 2, T, 5, spread_done)
                if l % 2 == 0:
                    phase("ffn_up", l, by_feature(h_hi, h_lo, T), block_ready=waits(h_ready, (2 * l + 1) * KT))
                    pe.wait_ge(gu_ready, COUNT["ffn_up", l] // 2 + 1)
                    n0 = BASE["ffn_down", l]
                    with pe.Fori(0, KT // 2) as ii:
                        for b in range(2):
                            pe.wait_ge(evac[b], ii * 2 + n0 // 2)
                            for s in range(2):
                                pe.wait_ge(lo_done, ii * 4 + (n0 + 2 * b + s + 1))
                                hi, lo = as_chunk("ffn_down", w_hi[:, s, :]), as_chunk("ffn_down", w_lo[:, s, :])
                                for k in range(FT // 2):
                                    kk = s * (FT // 2) + k
                                    ins = three(ps[:, 2 * b, 0:T], [(hi[:, k, :], gu_hi[:, kk, :]), (hi[:, k, :], gu_lo[:, kk, :]),
                                                                    (lo[:, k, :], gu_hi[:, kk, :])], kk == 0, kk == FT - 1)
                                ins.then_inc(mm_done, 1)

            pe.wait_ge(h_ready, 2 * DEPTH * KT)
            pe.wait_ge(wr_ready, 1)
            for t in range(2):
                r = slice(t * P, (t + 1) * P)
                for k in range(KT):
                    ins = three(ps[:, 5, t * NE:(t + 1) * NE], [(h_hi[:, k, r], wr_hi[:, k, :]), (h_hi[:, k, r], wr_lo[:, k, :]),
                                                                (h_lo[:, k, r], wr_hi[:, k, :])], k == 0, k == KT - 1)
            ins.then_inc(logit_done, 1)
            for g in range(8):
                if g >= 2:
                    pe.wait_ge(tok_copied, g - 1)
                part, t, half = (h_hi if g < 4 else h_lo), g // 2 % 2, g % 2
                for b in range(4):
                    ins = nc.tensor.transpose(ps[:, 6 + g % 2, b * P:(b + 1) * P], part[:, half * 4 + b, t * P:(t + 1) * P].bitcast(f32), ident[:])
                ins.then_inc(tok_turned, 1)
            pe.wait_ge(mask_ready, 1)
            pos = ps[:, 4, :]
            mm(pos[:, 0:NE], before[:], mask[:, 0, :], start=True, stop=True)
            mm(pos[:, NE:2 * NE], before[:], mask[:, 1, :], start=True, stop=False)
            mm(pos[:, NE:2 * NE], ones[:], mask[:, 0, :], start=False, stop=True)
            mm(pos[:, 2 * NE:3 * NE], ones[:], mask[:, 0, :], start=True, stop=False)
            mm(pos[:, 2 * NE:3 * NE], ones[:], mask[:, 1, :], start=False, stop=True).then_inc(pos_done, 1)
            pe.wait_ge(tok_copied, 8)
            pe.wait_ge(moe_fills, 2)

            def send(v):
                pe.wait_ge(pick_ready, v + 1)
                for part, banks in ((t_hi, (3, 4)), (t_lo, (5, 0))):
                    for k in range(KT):
                        for t in range(2):
                            ins = mm(ps[:, banks[k // 4], k % 4 * P:(k % 4 + 1) * P], part[:, t, k * P:(k + 1) * P], pick[:, t, :],
                                     start=t == 0, stop=t == 1)
                ins.then_inc(sent, 1)

            def zero_y():
                for a in range(2):
                    ins = mm(ps[:, 6 + a, :], zero_r[:, 0:P], zero_r[:], start=True, stop=True)
                ins.then_inc(y_zeroed, 1)

            def up(n, j0):
                for a in range(4):
                    pe.wait_ge(lo_done, n + (a + 1))
                    hi, lo = (w.rearrange("p (t c) -> p t c", c=EC) for w in moe_parts(j0 + a))
                    for k in range(4):
                        kk = a % 2 * 4 + k
                        ins = three(ps[:, a // 2, :], [(xe_hi[:, kk, :], hi[:, k, :]), (xe_hi[:, kk, :], lo[:, k, :]),
                                                       (xe_lo[:, kk, :], hi[:, k, :])], kk == 0, kk == KT - 1)
                    ins.then_inc(mm_done, 1)

            def turn_hidden(h):
                pe.wait_ge(hid_done, h + 1 + 1)
                for b in range(4):
                    ins = nc.tensor.transpose(ps[:, 2, b * P:(b + 1) * P], e_hid[:, b * P:(b + 1) * P], ident[:])
                ins.then_inc(hid_turned, 1)

            def down(n, h, j0):
                pe.wait_ge(hu_hi_done, h + 1)
                pe.wait_ge(hu_lo_done, h + 1)
                for a in range(2):
                    pe.wait_ge(lo_done, n + (a + 1))
                    hi, lo = (w.rearrange("p (t c) -> p t c", c=D) for w in moe_parts(j0 + a))
                    for k in range(2):
                        for half in range(2):
                            c = slice(half * 512, (half + 1) * 512)
                            for lhs, rhs in ((hu_hi, hi), (hu_hi, lo), (hu_lo, hi)):
                                ins = mm(ps[:, 6 + half, :], lhs[:, 2 * a + k, :], rhs[:, k, c], start=False, stop=True, skip_group_check=True)
                    ins.then_inc(mm_done, 1)

            def give_back(v):
                pe.wait_ge(y_copied, v * 2 + 2)
                zero_y()
                for a in range(4):
                    for b in range(2):
                        k = 2 * a + b
                        ins = mm(ps[:, 2 + a, b * SEQ:(b + 1) * SEQ], y_rows[:, k * P:(k + 1) * P], put[:].rearrange("p t c -> p (t c)"),
                                 start=True, stop=True)
                    ins.then_inc(back_done, 1)

            def expert(q):
                n = q * MOE_N + DENSE_CHUNKS
                h = q * NC
                pe.wait_ge(xe_hi_done, q * 2 + 2)
                pe.wait_ge(xe_lo_done, q * 2 + 2)
                pe.wait_ge(put_copied, q + 1)
                up(n, 0)

                def round_(c):
                    nn = n + c * 6 - 2
                    hc = h + c
                    first = isinstance(c, int)
                    if not first:
                        pe.wait_ge(back_added, q * 4 + 4 + 1)
                    turn_hidden(hc - 1)
                    pe.wait_ge(silu_done, hc)
                    up(nn, 4)
                    if first:
                        pe.wait_ge(hu_hi_done, hc)
                        pe.wait_ge(hu_lo_done, hc)
                        give_back(q)
                    down(nn + 4, hc - 1, 2)

                round_(1)
                with pe.Fori(2, NC) as c:
                    round_(c)
                pe.wait_ge(silu_done, h + NC)
                send(q + 1)
                turn_hidden(h + (NC - 1))
                pe.wait_ge(pick_g_ready, q + 1)
                for t in range(2):
                    ins = nc.tensor.transpose(ps[:, 1, t * P:(t + 1) * P], pick_g[:, t, :], ident[:])
                ins.then_inc(put_turned, 1)
                down(n + (MOE_N - 2), h + (NC - 1), 4)

            zero_y()
            send(0)
            with pe.Fori(0, NE) as q:
                expert(q)
            pe.wait_ge(route_ready, 1)
            with pe.Fori(0, FULL) as f:
                used = pe.value_load(full_i[0:1, 1, ds(f, 1)], min_val=0, max_val=1)
                with pe.If(used > 0):
                    expert(f + NE)
                with pe.Else():
                    pe.nop()
            v = pe.value_load(full_n[0:1, 0:1], min_val=0, max_val=FULL) + NE
            pe.wait_ge(put_copied, v + 1)
            give_back(v)
            pe.wait_ge(back_added, v * 4 + 4 + 1)
            mean(sum_done, 2 * DEPTH + 1, SEQ, 5, ms_done)
            spread(diag_done, 2 * DEPTH + 1, SEQ, 5, spread_done)


def kernel(**inputs):
    import concourse.bacc as bacc
    from concourse.bass_utils import run_bass_kernel_spmd as run

    a = {k: np.asarray(v) for k, v in inputs.items()}

    def c(v):
        return np.ascontiguousarray(v)

    def blocks(v):
        return c(np.moveaxis(v.reshape(*v.shape[:-1], -1, P), -1, 0))

    pos = np.arange(SEQ)
    freqs = np.float32(ROPE_THETA) ** (-np.arange(HD // 4, dtype=np.float32) / (HD // 4))
    ang = np.concatenate([(pos // GRID_W)[:, None].astype(np.float32) * freqs, (pos % GRID_W)[:, None].astype(np.float32) * freqs], -1)
    rope = np.stack([np.cos(ang), np.sin(ang)]).astype(np.float32).reshape(2, SEQ // P, P, HALF).transpose(2, 0, 1, 3)
    arrays = {
        "x_t": c(a["x"][0].T), "ctx_t": c(a["ctx"][0].T),
        "c_t": c(np.stack([a["c"][0], a["c_ctx"]], -1).reshape(KT, P, 2).transpose(1, 0, 2)),
        "ident": np.eye(P, dtype=np.float32), "rope": c(rope),
        "dw": c(a["conv_dw"].transpose(0, 2, 1).reshape(DEPTH, KT, P, TAPS).transpose(2, 0, 1, 3)),
        "vecs": blocks(np.stack([a[n] for n in ("g_mix", "g_ffn", "conv_b", "conv_ln_g", "conv_ln_b")])),
        "g_final": blocks(a["g_final"]),
        "qk_gain": c(np.broadcast_to(np.stack([a["q_norm"], a["k_norm"]])[None], (P, 2, DEPTH, HD))),
        "b_ada": c(blocks(a["b_ada"]).reshape(P, -1)),
        "w_router": c(a["w_router"][0].reshape(KT, P, NE).transpose(1, 0, 2)),
        "b_router": c(np.broadcast_to(a["b_router"], (P, NE))),
        "iota": c(np.broadcast_to(np.arange(P, dtype=np.float32), (P, P))),
        "before": np.triu(np.ones((P, P), np.float32), 1),
        "rank8": c(np.broadcast_to(np.arange(NE, 0, -1, dtype=np.float32), (P, NE))),
    }
    for name in ("w_ada", "w_in", "w_attn_o", "w_conv_o", "w_out", "w_ff_gate", "w_ff_up", "w_ff_down", "w_moe_gate", "w_moe_up", "w_moe_down"):
        arrays[name] = c(a[name])
    nc = bacc.Bacc("TRN2", target_bir_lowering=False, num_devices=1)
    A = {k: nc.dram_tensor("in_" + k, v.shape, mybir.dt.from_np(v.dtype), kind="ExternalInput").ap() for k, v in arrays.items()}
    out = nc.dram_tensor("out_t", (D, SEQ), mybir.dt.float32, kind="ExternalOutput").ap()
    build(nc, A, out)
    r = run(nc, [{"in_" + k: v for k, v in arrays.items()}], core_ids=[0])
    return np.ascontiguousarray(r.results[0]["out_t"].T)[None]
```
